# Optimizing a Trainium2 kernel written in Bass

```python
import jax, jax.numpy as jnp
from jax import lax
import numpy as np
import math

D_MODEL = 1024
BATCH = 1
SEQ = 256
DEPTH = 1

CONV_CH = D_MODEL
CONV_WIDTH = 31
N_HEADS = 16
HEAD_DIM = 64
ATTN_DIM = N_HEADS * HEAD_DIM
DILATION_GROUPS = ((128, 1), (512, 4), (2048, 16))
ATTN_BLOCK = 128
D_FF = 2816
FFN_CONV_WIDTH = 3
EPS = 1e-6
SPLITS = (2 * CONV_CH, 2 * CONV_CH + ATTN_DIM, 2 * CONV_CH + 2 * ATTN_DIM, 2 * CONV_CH + 3 * ATTN_DIM)
IN_COLS = 2 * CONV_CH + 3 * ATTN_DIM + 2 * D_MODEL


def rms_norm(x, g):
    xf = x.astype(jnp.float32)
    xf = xf * lax.rsqrt(jnp.mean(xf * xf, axis=-1, keepdims=True) + EPS)
    return (xf * g.astype(jnp.float32)).astype(x.dtype)

def causal_depthwise_conv(u, w, b):
    width, ch = w.shape
    out = lax.conv_general_dilated(
        u, w[:, None, :].astype(u.dtype), window_strides=(1,), padding=[(width - 1, 0)],
        dimension_numbers=('NWC', 'WIO', 'NWC'), feature_group_count=ch)
    return out + b.astype(u.dtype)

def alibi_slopes(n_heads):
    return 2.0 ** (-8.0 * jnp.arange(1, n_heads + 1, dtype=jnp.float32) / n_heads)

def dilated_window_attention(q, k, v, slopes, window, dilation):
    B, S, H, Dh = q.shape
    n_back = window // dilation
    L = S // dilation
    nb = -(-L // ATTN_BLOCK)
    Lp = nb * ATTN_BLOCK

    def to_sub(t):
        t = t.reshape(B, L, dilation, H, Dh).transpose(0, 2, 1, 3, 4).reshape(B * dilation, L, H, Dh)
        t = jnp.pad(t, ((0, 0), (0, Lp - L), (0, 0), (0, 0)))
        return t.reshape(B * dilation, nb, ATTN_BLOCK, H, Dh)

    def with_prev(t):
        prev = jnp.pad(t, ((0, 0), (1, 0), (0, 0), (0, 0), (0, 0)))[:, :-1]
        return jnp.concatenate([prev, t], axis=2)

    qb = to_sub(q)
    kc = with_prev(to_sub(k))
    vc = with_prev(to_sub(v))

    scores = jnp.einsum('nbqhd,nbkhd->nbhqk', qb, kc)
    steps = (jnp.arange(ATTN_BLOCK)[:, None] + ATTN_BLOCK) - jnp.arange(2 * ATTN_BLOCK)[None, :]
    valid = (steps >= 0) & (steps <= n_back)
    first_block = (jnp.arange(nb) == 0)[:, None, None]
    prev_cols = (jnp.arange(2 * ATTN_BLOCK) < ATTN_BLOCK)[None, None, :]
    valid = valid[None] & ~(first_block & prev_cols)
    dist = (steps * dilation).astype(jnp.float32)
    scores = scores - slopes[:, None, None] * dist
    scores = jnp.where(valid[None, :, None], scores, -jnp.inf)
    m = jnp.max(scores, axis=-1, keepdims=True)
    p = jnp.exp(scores - m)
    den = jnp.sum(p, axis=-1)
    o = jnp.einsum('nbhqk,nbkhd->nbqhd', p, vc) / jnp.swapaxes(den, 2, 3)[..., None]
    lse = jnp.swapaxes(m[..., 0] + jnp.log(den), 2, 3)

    def from_sub(t):
        rest = t.shape[3:]
        t = t.reshape(B, dilation, Lp, *rest)[:, :, :L]
        return jnp.swapaxes(t, 1, 2).reshape(B, S, *rest)

    return from_sub(o), from_sub(lse)

def first_inputs(seed: int = 0) -> dict:
    key = jax.random.key(seed)
    ks = jax.random.split(key, 18)
    f32 = jnp.float32

    def nrm(k, shape, scale):
        return jax.random.normal(k, shape, f32) * scale

    return {
        'x': nrm(ks[0], (BATCH, SEQ, D_MODEL), 1.0),
        'norm1_g': 1.0 + nrm(ks[1], (DEPTH, D_MODEL), 0.1),
        'w_in': nrm(ks[2], (DEPTH, D_MODEL, IN_COLS), D_MODEL ** -0.5),
        'gate_b': nrm(ks[3], (DEPTH, 2 * D_MODEL), 0.02),
        'conv_w': nrm(ks[4], (DEPTH, CONV_WIDTH, CONV_CH), CONV_WIDTH ** -0.5),
        'conv_b': nrm(ks[5], (DEPTH, CONV_CH), 0.02),
        'conv_norm_g': 1.0 + nrm(ks[6], (DEPTH, CONV_CH), 0.1),
        'w_conv_out': nrm(ks[7], (DEPTH, CONV_CH, D_MODEL), CONV_CH ** -0.5),
        'q_norm_g': 1.0 + nrm(ks[8], (DEPTH, HEAD_DIM), 0.1),
        'k_norm_g': 1.0 + nrm(ks[9], (DEPTH, HEAD_DIM), 0.1),
        'w_attn_out': nrm(ks[10], (DEPTH, ATTN_DIM, D_MODEL), ATTN_DIM ** -0.5),
        'w_out': nrm(ks[11], (DEPTH, D_MODEL, D_MODEL), D_MODEL ** -0.5),
        'norm2_g': 1.0 + nrm(ks[12], (DEPTH, D_MODEL), 0.1),
        'w_up': nrm(ks[13], (DEPTH, D_MODEL, 2 * D_FF), D_MODEL ** -0.5),
        'ffn_conv_w': nrm(ks[14], (DEPTH, FFN_CONV_WIDTH, 2 * D_FF), FFN_CONV_WIDTH ** -0.5),
        'ffn_conv_b': nrm(ks[15], (DEPTH, 2 * D_FF), 0.02),
        'w_down': nrm(ks[16], (DEPTH, D_FF, D_MODEL), D_FF ** -0.5),
    }

def first_block(x, norm1_g, w_in, gate_b, conv_w, conv_b, conv_norm_g, w_conv_out,
              q_norm_g, k_norm_g, w_attn_out, w_out, norm2_g, w_up, ffn_conv_w,
              ffn_conv_b, w_down):
    B, S, _ = x.shape
    slopes = alibi_slopes(N_HEADS)
    for l in range(DEPTH):
        h = rms_norm(x, norm1_g[l])
        z = h @ w_in[l].astype(h.dtype)
        glu_in, q, k, v, gate_logits = jnp.split(z, SPLITS, axis=-1)

        a_val, a_gate = jnp.split(glu_in, 2, axis=-1)
        a = a_val * jax.nn.sigmoid(a_gate)
        a = causal_depthwise_conv(a, conv_w[l], conv_b[l])
        a = jax.nn.silu(rms_norm(a, conv_norm_g[l]))
        y_a = a @ w_conv_out[l].astype(a.dtype)

        q = rms_norm(q.reshape(B, S, N_HEADS, HEAD_DIM), q_norm_g[l]).astype(jnp.float32) * HEAD_DIM ** -0.5
        k = rms_norm(k.reshape(B, S, N_HEADS, HEAD_DIM), k_norm_g[l]).astype(jnp.float32)
        v = v.reshape(B, S, N_HEADS, HEAD_DIM).astype(jnp.float32)
        outs, lses = [], []
        for window, dilation in DILATION_GROUPS:
            o_g, lse_g = dilated_window_attention(q, k, v, slopes, window, dilation)
            outs.append(o_g)
            lses.append(lse_g)
        mix = jax.nn.softmax(jnp.stack(lses), axis=0)
        o = jnp.einsum('gbsh,gbshd->bshd', mix, jnp.stack(outs))
        o = o.astype(x.dtype).reshape(B, S, ATTN_DIM)
        y_b = o @ w_attn_out[l].astype(o.dtype)

        g = jax.nn.sigmoid(gate_logits + gate_b[l].astype(gate_logits.dtype))
        g_a, g_b = jnp.split(g, 2, axis=-1)
        x = x + (g_a * y_a + g_b * y_b) @ w_out[l].astype(x.dtype)

        h = rms_norm(x, norm2_g[l])
        u = causal_depthwise_conv(h @ w_up[l].astype(h.dtype), ffn_conv_w[l], ffn_conv_b[l])
        u_val, u_gate = jnp.split(u, 2, axis=-1)
        x = x + (jax.nn.silu(u_gate) * u_val) @ w_down[l].astype(x.dtype)
    return x


MLA_HEADS = 8
MLA_NOPE_DIM = 64
MLA_ROPE_DIM = 32
MLA_QK_DIM = MLA_NOPE_DIM + MLA_ROPE_DIM
MLA_V_DIM = 64
MLA_WIDTH = MLA_HEADS * MLA_V_DIM
MLA_Q_RANK = 384
MLA_KV_RANK = 256
ROPE_THETA = 10000.0
Q_BLOCK = 128
GLA_HEADS = 4
GLA_DV = D_MODEL // 2
GLA_DK = GLA_DV // 2
GLA_HEAD_K = GLA_DK // GLA_HEADS
GLA_HEAD_V = GLA_DV // GLA_HEADS
GLA_GATE_RANK = 16
GLA_GATE_TAU = 16.0
GLA_CHUNK = 64
D_FF_2 = -(-8 * D_MODEL // (3 * 256)) * 256
NORM_EPS = 1e-6
IN_SIZES = (MLA_Q_RANK, MLA_KV_RANK, MLA_ROPE_DIM,
            GLA_DK, GLA_DK, GLA_DV, GLA_GATE_RANK, GLA_DV,
            D_MODEL, D_MODEL)
D_IN = sum(IN_SIZES)


def rmsnorm(x, w):
    xf = x.astype(jnp.float32)
    y = xf * lax.rsqrt(jnp.mean(xf * xf, axis=-1, keepdims=True) + NORM_EPS)
    return (y * w.astype(jnp.float32)).astype(x.dtype)

def rope_tables(positions):
    half = MLA_ROPE_DIM // 2
    inv = 1.0 / (ROPE_THETA ** (jnp.arange(half, dtype=jnp.float32) / half))
    ang = positions.astype(jnp.float32)[..., None] * inv
    return jnp.cos(ang), jnp.sin(ang)

def apply_rope(x, cos, sin):
    x1, x2 = jnp.split(x.astype(jnp.float32), 2, axis=-1)
    return jnp.concatenate([x1 * cos - x2 * sin, x2 * cos + x1 * sin], axis=-1).astype(x.dtype)

def mla(c_q, c_kv, k_rope, cos, sin, norm_cq, w_uq, norm_ckv, w_ukv):
    B, S, _ = c_q.shape
    H = MLA_HEADS
    q = (rmsnorm(c_q, norm_cq) @ w_uq).reshape(B, S, H, MLA_QK_DIM)
    q_nope, q_rope = q[..., :MLA_NOPE_DIM], q[..., MLA_NOPE_DIM:]
    q_rope = apply_rope(q_rope, cos[:, :, None], sin[:, :, None])
    kv = (rmsnorm(c_kv, norm_ckv) @ w_ukv).reshape(B, S, H, MLA_NOPE_DIM + MLA_V_DIM)
    k_nope, v = kv[..., :MLA_NOPE_DIM], kv[..., MLA_NOPE_DIM:]
    k_rope = apply_rope(k_rope, cos, sin)
    k = jnp.concatenate([k_nope, jnp.broadcast_to(k_rope[:, :, None], (B, S, H, MLA_ROPE_DIM)).astype(k_nope.dtype)], axis=-1)
    q = jnp.concatenate([q_nope, q_rope], axis=-1) * (MLA_QK_DIM ** -0.5)
    nb = S // Q_BLOCK
    q_blocks = q.reshape(B, nb, Q_BLOCK, H, MLA_QK_DIM).transpose(1, 0, 2, 3, 4)
    key_idx = jnp.arange(S)

    def attend(args):
        q_blk, start = args
        s = jnp.einsum('bqhd,bkhd->bhqk', q_blk, k).astype(jnp.float32)
        q_idx = start + jnp.arange(Q_BLOCK)
        mask = key_idx[None, :] <= q_idx[:, None]
        s = jnp.where(mask, s, -jnp.inf)
        p = jax.nn.softmax(s, axis=-1).astype(v.dtype)
        return jnp.einsum('bhqk,bkhd->bqhd', p, v)

    o = lax.map(attend, (q_blocks, jnp.arange(nb) * Q_BLOCK))
    return o.transpose(1, 0, 2, 3, 4).reshape(B, S, MLA_WIDTH)

def gla(q, k, v, g_lr, og, w_gate2, b_gate, norm_o):
    B, S, _ = q.shape
    H, C = GLA_HEADS, GLA_CHUNK
    n = S // C
    log_a = jax.nn.log_sigmoid((g_lr @ w_gate2 + b_gate).astype(jnp.float32)) / GLA_GATE_TAU

    def heads(t, d):
        return t.reshape(B, S, H, d).transpose(0, 2, 1, 3).astype(jnp.float32)

    def chunks(t):
        return t.reshape(B, H, n, C, t.shape[-1]).transpose(2, 0, 1, 3, 4)

    qh = heads(q, GLA_HEAD_K) * (GLA_HEAD_K ** -0.5)
    kh = heads(k, GLA_HEAD_K)
    vh = heads(v, GLA_HEAD_V)
    gh = heads(log_a, GLA_HEAD_K)
    bcum = jnp.cumsum(chunks(gh), axis=3)
    causal = jnp.tril(jnp.ones((C, C), dtype=bool))

    def step(state, xs):
        qc, kc, vc, bc = xs
        o_inter = jnp.einsum('bhcd,bhde->bhce', qc * jnp.exp(bc), state)
        diff = bc[:, :, :, None, :] - bc[:, :, None, :, :]
        decay = jnp.exp(jnp.where(causal[:, :, None], diff, -jnp.inf))
        attn = jnp.einsum('bhid,bhjd,bhijd->bhij', qc, kc, decay)
        o_intra = jnp.einsum('bhij,bhje->bhie', attn, vc)
        b_last = bc[:, :, -1:, :]
        k_dec = kc * jnp.exp(b_last - bc)
        state = jnp.exp(b_last[:, :, 0, :])[..., None] * state + jnp.einsum('bhcd,bhce->bhde', k_dec, vc)
        return state, o_inter + o_intra

    state0 = jnp.zeros((B, H, GLA_HEAD_K, GLA_HEAD_V), jnp.float32)
    _, o = lax.scan(step, state0, (chunks(qh), chunks(kh), chunks(vh), bcum))
    o = o.transpose(1, 0, 3, 2, 4).reshape(B, S, H, GLA_HEAD_V)
    o = rmsnorm(o, norm_o).reshape(B, S, GLA_DV)
    o = o * jax.nn.silu(og.astype(jnp.float32))
    return o.astype(q.dtype)

def second_inputs(seed: int = 0) -> dict:
    key = jax.random.key(seed)
    ks = jax.random.split(key, 24)
    L, D = DEPTH, D_MODEL

    def w(k, shape, fan_in):
        return jax.random.normal(k, shape, jnp.float32) * (fan_in ** -0.5)

    def gain(k, shape):
        return 1.0 + 0.02 * jax.random.normal(k, shape, jnp.float32)

    return {
        "x": jax.random.normal(ks[0], (BATCH, SEQ, D), jnp.float32),
        "positions": jnp.broadcast_to(jnp.arange(SEQ, dtype=jnp.int32), (BATCH, SEQ)),
        "ln_mix": gain(ks[1], (L, D)),
        "w_in": w(ks[2], (L, D, D_IN), D),
        "mla_norm_cq": gain(ks[3], (L, MLA_Q_RANK)),
        "mla_w_uq": w(ks[4], (L, MLA_Q_RANK, MLA_HEADS * MLA_QK_DIM), MLA_Q_RANK),
        "mla_norm_ckv": gain(ks[5], (L, MLA_KV_RANK)),
        "mla_w_ukv": w(ks[6], (L, MLA_KV_RANK, MLA_HEADS * (MLA_NOPE_DIM + MLA_V_DIM)), MLA_KV_RANK),
        "mla_w_o": w(ks[7], (L, MLA_WIDTH, D), MLA_WIDTH),
        "gla_w_gate2": w(ks[8], (L, GLA_GATE_RANK, GLA_DK), GLA_GATE_RANK),
        "gla_b_gate": 0.1 * jax.random.normal(ks[9], (L, GLA_DK), jnp.float32),
        "gla_norm": gain(ks[10], (L, GLA_HEAD_V)),
        "gla_w_o": w(ks[11], (L, GLA_DV, D), GLA_DV),
        "w_out": w(ks[12], (L, D, D), D),
        "ln_ffn": gain(ks[13], (L, D)),
        "ffn_w_gate": w(ks[14], (L, D, D_FF_2), D),
        "ffn_w_up": w(ks[15], (L, D, D_FF_2), D),
        "ffn_w_down": w(ks[16], (L, D_FF_2, D), D_FF_2),
        "final_norm": gain(ks[17], (D,)),
    }

def second_block(x, positions, ln_mix, w_in, mla_norm_cq, mla_w_uq, mla_norm_ckv, mla_w_ukv, mla_w_o,
              gla_w_gate2, gla_b_gate, gla_norm, gla_w_o, w_out, ln_ffn, ffn_w_gate, ffn_w_up,
              ffn_w_down, final_norm):
    offsets = np.cumsum(IN_SIZES)[:-1].tolist()
    cos, sin = rope_tables(positions)
    h = x
    for l in range(DEPTH):
        u = rmsnorm(h, ln_mix[l])
        z = u @ w_in[l]
        c_q, c_kv, k_rope, g_q, g_k, g_v, g_lr, g_og, gate_a, gate_b = jnp.split(z, offsets, axis=-1)
        y_a = mla(c_q, c_kv, k_rope, cos, sin, mla_norm_cq[l], mla_w_uq[l], mla_norm_ckv[l], mla_w_ukv[l]) @ mla_w_o[l]
        y_b = gla(g_q, g_k, g_v, g_lr, g_og, gla_w_gate2[l], gla_b_gate[l], gla_norm[l]) @ gla_w_o[l]
        mix = jax.nn.sigmoid(gate_a) * y_a + jax.nn.sigmoid(gate_b) * y_b
        h = h + mix @ w_out[l]
        u = rmsnorm(h, ln_ffn[l])
        h = h + (jax.nn.silu(u @ ffn_w_gate[l]) * (u @ ffn_w_up[l])) @ ffn_w_down[l]
    return rmsnorm(h, final_norm)


def setup_inputs(seed=0):
    out = dict(first_inputs(seed))
    for name, value in second_inputs(seed + 1).items():
        if name != "x":
            out[name + "_2"] = value
    return out


def reference(
    x, norm1_g, w_in, gate_b, conv_w, conv_b, conv_norm_g, w_conv_out, q_norm_g, k_norm_g,
    w_attn_out, w_out, norm2_g, w_up, ffn_conv_w, ffn_conv_b, w_down, positions_2, ln_mix_2,
    w_in_2, mla_norm_cq_2, mla_w_uq_2, mla_norm_ckv_2, mla_w_ukv_2, mla_w_o_2, gla_w_gate2_2,
    gla_b_gate_2, gla_norm_2, gla_w_o_2, w_out_2, ln_ffn_2, ffn_w_gate_2, ffn_w_up_2,
    ffn_w_down_2, final_norm_2,
):
    x = first_block(
        x, norm1_g, w_in, gate_b, conv_w, conv_b, conv_norm_g, w_conv_out, q_norm_g, k_norm_g,
        w_attn_out, w_out, norm2_g, w_up, ffn_conv_w, ffn_conv_b, w_down,
    )
    return second_block(
        x, positions_2, ln_mix_2, w_in_2, mla_norm_cq_2, mla_w_uq_2, mla_norm_ckv_2,
        mla_w_ukv_2, mla_w_o_2, gla_w_gate2_2, gla_b_gate_2, gla_norm_2, gla_w_o_2, w_out_2,
        ln_ffn_2, ffn_w_gate_2, ffn_w_up_2, ffn_w_down_2, final_norm_2,
    )


_drawn_inputs = setup_inputs


def setup_inputs(seed=0):
    import zlib

    import numpy as np

    out = dict(_drawn_inputs(seed))
    spreads = {}
    factors = {'gate_b': 8.0,
     'conv_b': 2.963,
     'q_norm_g': 3.24,
     'k_norm_g': 2.852,
     'ffn_conv_b': 3.359,
     'ln_mix_2': 4.66,
     'mla_norm_cq_2': 8.0,
     'mla_norm_ckv_2': 8.0,
     'gla_b_gate_2': 5.179,
     'gla_norm_2': 8.0,
     'ln_ffn_2': 13.862,
     'final_norm_2': 8.072}
    for name, (base, spread) in spreads.items():
        noise = np.random.default_rng([zlib.crc32(name.encode()), seed]).standard_normal(out[name].shape)
        drawn = base * np.exp(spread * noise) if base else spread * noise
        out[name] = __import__('jax').numpy.asarray(drawn.astype(out[name].dtype))
    for name, factor in factors.items():
        out[name] = (out[name] * factor).astype(out[name].dtype)
    return out
```

```python
from contextlib import ExitStack

import numpy as np

import concourse.bass as bass
from concourse import mybir

F32 = mybir.dt.float32
F32R = mybir.dt.float32r
I32 = mybir.dt.int32
ALU = mybir.AluOpType
ACT = mybir.ActivationFunctionType
AX = mybir.AxisListType

P = 128
S = 256
D = 1024
KD = D // P
FT = 22
NH = 16
MH = 8
CB = 8
CW = CB * P
NRAW = 5
NSL = 5
AHEAD = 3
EPS = 1e-6
NEG = -1e30
TWO_PI = 2.0 * np.pi
C1 = 6.28125
C2 = float(np.float32(np.round((TWO_PI - C1) * 2 ** 19) / 2 ** 19))
C3 = float(np.float32(TWO_PI - C1 - C2))
PI_F = 3.1415925
MAGIC = 12582912.0
LEVELS = (0, 32, 16, 8, 4, 2, 1)


def rng(a, n=P):
    return list(range(a, a + n))


def stream_jobs():
    jobs = []

    def add(key, name, cols, kt):
        jobs.append((key, name, cols, kt))

    for i in range(KD):
        add(("ag", i), "w_in", rng(1024 + i * P), KD)
        add(("av", i), "w_in", rng(i * P), KD)
    for n in range(2):
        add(("v", n), "w_in", rng(4096 + n * 512, 512), KD)
    for i in range(KD):
        add(("q", i), "w_in", rng(2048 + i * P), KD)
        add(("k", i), "w_in", rng(3072 + i * P), KD)
    for i in range(16):
        add(("g", i), "w_in", rng(5120 + i * P), KD)
    for i in range(KD):
        add(("co", i), "w_conv_out", rng(i * P), KD)
    for i in range(KD):
        add(("ao", i), "w_attn_out", rng(i * P), KD)
    for i in range(KD):
        add(("wo", i), "w_out", rng(i * P), KD)
    for i in range(FT):
        add(("ug", i), "w_up", rng(2816 + i * P), KD)
        add(("uv", i), "w_up", rng(i * P), KD)
    for i in range(KD):
        add(("dn", i), "w_down", rng(i * P), FT)
    kr = 640
    for i in range(3):
        add(("cq", i), "w_in_2", rng(i * P), KD)
    for i in range(2):
        add(("ckv", i), "w_in_2", rng(384 + i * P), KD)
    add(("kr", 0), "w_in_2", rng(kr, 32) * 4, KD)
    add(("krs", 0), "w_in_2", (rng(kr + 16, 16) + rng(kr, 16)) * 4, KD)
    add(("glr", 0), "w_in_2", rng(1696, 16) * 8, KD)
    for i in range(2):
        add(("gq", i), "w_in_2", rng(672 + i * P), KD)
    for i in range(2):
        add(("gk", i), "w_in_2", rng(928 + i * P), KD)
    add(("gv", 0), "w_in_2", rng(1184, 512), KD)
    for i in range(4):
        add(("qn", i), "mla_w_uq_2", rng(192 * i, 64) + rng(192 * i + 96, 64), 3)
    for i in range(2):
        add(("qr", i), "mla_w_uq_2", sum((rng(96 * (4 * i + h) + 64, 32) for h in range(4)), []), 3)
        add(("qrs", i), "mla_w_uq_2",
            sum((rng(96 * (4 * i + h) + 80, 16) + rng(96 * (4 * i + h) + 64, 16) for h in range(4)), []), 3)
    for i in range(4):
        add(("kn", i), "mla_w_ukv_2", rng(256 * i, 64) + rng(256 * i + 128, 64), 2)
    add(("mv", 0), "mla_w_ukv_2", sum((rng(128 * h + 64, 64) for h in range(MH)), []), 2)
    for i in range(4):
        add(("og", i), "w_in_2", rng(1712 + i * P), KD)
    for i in range(16):
        add(("g2", i), "w_in_2", rng(2224 + i * P), KD)
    for i in range(KD):
        add(("mo", i), "mla_w_o_2", rng(i * P), 4)
    for i in range(KD):
        add(("go", i), "gla_w_o_2", rng(i * P), 4)
    for i in range(KD):
        add(("wo2", i), "w_out_2", rng(i * P), KD)
    for i in range(FT):
        add(("fg", i), "ffn_w_gate_2", rng(i * P), KD)
        add(("fu", i), "ffn_w_up_2", rng(i * P), KD)
    for i in range(KD):
        add(("fd", i), "ffn_w_down_2", rng(i * P), FT)
    return jobs


def place_jobs():
    at, out = 0, []
    for key, name, cols, kt in stream_jobs():
        w = len(cols) // P
        at += -at % w
        out.append((key, name, cols, kt, at))
        at += kt * w
    return out, -(-at // CB)


VECS = [("norm1_g", 8), ("gate_b", 16), ("conv_b", 8), ("conv_norm_g", 8), ("qg", 1), ("kg", 1),
        ("norm2_g", 8), ("ffn_conv_b", 44), ("ln_mix_2", 8), ("mla_norm_cq_2", 3), ("mla_norm_ckv_2", 2),
        ("gla_b_gate_2", 2), ("gla_norm_2", 1), ("ln_ffn_2", 8), ("final_norm_2", 8),
        ("conv_w", 31 * 8), ("ffn_conv_w", 3 * 44), ("inv", 1), ("sgn", 1), ("eps", 1), ("one", 1)]


def vec_at():
    at, out = 0, {}
    for n, w in VECS:
        out[n] = at
        at += w
    return out, at


class Queue:

    def __init__(self, eng, sem, serial=False):
        self.eng, self.sem, self.n, self.seen, self.serial = eng, sem, 0, {}, serial

    def wait(self, *marks):
        for m in marks:
            if m is None:
                continue
            sem, v, i = m
            if self.seen.get(i, 0) < v:
                self.seen[i] = v
                if self.eng is not None:
                    self.eng.wait_ge(sem, v)

    def do(self, f):
        if self.eng is not None:
            f(self.eng)

    def mark(self, f):
        if self.serial:
            self.wait(self.last())
        self.n += 1
        if self.eng is not None:
            f(self.eng).then_inc(self.sem, 1)
        return self.last()

    def last(self):
        return (self.sem, self.n, self.sem.name) if self.n else None

    def dma(self, s, dst, src, n):
        if self.eng is not None:
            self.eng.dma_start(dst, src).then_inc(s, 16)
        return (s, 16 * n, s.name)


class Bank:
    def __init__(self, t):
        self.t, self.free, self.busy = t, [], False


class Banks:
    def __init__(self, ts):
        self.b, self.i = [Bank(t) for t in ts], 0

    def take(self):
        for _ in self.b:
            b = self.b[self.i]
            self.i = (self.i + 1) % len(self.b)
            if not b.busy:
                b.busy = True
                return b
        raise AssertionError("no free PSUM bank")


def give(bank, *marks):
    bank.free, bank.busy = list(marks), False


def two_blocks(nc, ws, x, vecs, pos, w_gate2, tabs, masks, out):
    V, NV = vec_at()
    placed, n_chunks = place_jobs()
    where = {key: (kt, at, len(cols) // P) for key, _, cols, kt, at in placed}

    made = {}

    def walk(block_engine, who):
        used = set()
        ctx = ExitStack() if made else outer

        def once(name, make):
            while name in used:
                name += "_"
            used.add(name)
            if name not in made:
                made[name] = make(name)
            return made[name]

        def sem(name):
            return once(name, lambda n: outer.enter_context(nc.semaphore(n)))

        def sb(c, name, shape, dt=F32):
            return once(name, lambda n: c.enter_context(nc.sbuf_tensor(n, shape, dt)))

        def psum(name):
            return once(name, lambda n: outer.enter_context(nc.psum_tensor(n, [P, 512], F32)))

        def queue(name, serial=False):
            return Queue(block_engine if who == name else None, sem(name), serial)

        pe, act, dve, pool, sp = queue("s_pe"), queue("s_act"), queue("s_dve"), queue("s_pool", True), queue("s_sp")

        def dma(q, s, dst, src, n):
            return q.dma(s, dst, src, n)

        jb = Banks([psum(f"pj{i}") for i in range(3)])
        xb = Banks([psum(f"px{i}") for i in range(5)])

        raw = sb(ctx, "raw", [P, NRAW, CW])
        whi = sb(ctx, "whi", [P, NSL, CW], F32R)
        wlo = sb(ctx, "wlo", [P, NSL, CW], F32R)
        X = sb(ctx, "X", [P, KD, S])
        hh = sb(ctx, "hh", [P, KD, S], F32R)
        hl = sb(ctx, "hl", [P, KD, S], F32R)
        vc = sb(ctx, "vc", [P, NV])
        hb = sb(ctx, "hb", [P, 16])
        cw5 = sb(ctx, "cw5", [P, 31 * 8])
        qg8 = sb(ctx, "qg8", [P, 1])
        ones = sb(ctx, "ones", [P, P])
        bd = sb(ctx, "bd", [P, P])
        ident = sb(ctx, "ident", [P, P])
        rope = sb(ctx, "rope", [P, 4, S])
        wg2 = sb(ctx, "wg2", [16, S])
        caus = sb(ctx, "caus", [P, S])
        rst = sb(ctx, "rst", [P, 2, 512])
        sq = sb(ctx, "sq", [P, 4, S])

        def vec(name, i=0):
            return vc[:, V[name] + i:V[name] + i + 1]

        s_c = [sem(f"s_c{i}") for i in range(6)]
        m_x = dma(act, s_c[0], X[:, :, :], x.rearrange("p (k s) -> p k s", k=KD), 1)
        m_vc = dma(act, s_c[1], vc[:, :], vecs, 1)
        m_wg2 = dma(act, s_c[2], wg2[:, :], w_gate2, 1)
        m_caus = dma(act, s_c[3], caus[:, :], tabs[NH], 1)
        m_on = pool.mark(lambda e: e.memset(ones[:, :], 1.0))
        m_b0 = pool.mark(lambda e: e.memset(bd[:, :], 0.0))
        m_i0 = pool.mark(lambda e: e.memset(ident[:, :], 0.0))
        pool.wait(m_b0)
        pool.mark(lambda e: e.memset(bd[0:64, 0:64], 1.0))
        m_bd = pool.mark(lambda e: e.memset(bd[64:128, 64:128], 1.0))
        pool.wait(m_i0)
        m_id = pool.mark(lambda e: e.affine_select(out=ident[:, :], in_=ident[:, :], compare_op=ALU.not_equal,
                                                   fill=1.0, base=0, pattern=[[-1, P]], channel_multiplier=1))

        s_raw = [sem(f"s_raw{i}") for i in range(NRAW)]
        m_raw, m_hi, m_lo, m_used = {}, {}, {}, {}
        state = {"load": 0, "prep": 0}

        def load():
            c = state["load"]
            if c >= n_chunks:
                return
            if c >= NRAW:
                sp.wait(m_hi[c - NRAW], m_lo[c - NRAW])
            m_raw[c] = dma(sp, s_raw[c % NRAW], raw[:, c % NRAW, :], ws[c], c // NRAW + 1)
            state["load"] += 1

        def prep():
            c = state["prep"]
            if c >= n_chunks:
                return
            r, h = c % NRAW, c % NSL
            act.wait(m_raw[c])
            if c >= NSL:
                act.wait(m_used[c - NSL], m_hi[c - NSL], m_lo[c - NSL])
            m_hi[c] = act.mark(lambda e: e.activation(whi[:, h, :], raw[:, r, :], ACT.Copy))
            dve.wait(m_hi[c], m_raw[c])
            if c >= NSL:
                dve.wait(m_used[c - NSL], m_lo[c - NSL])
            m_lo[c] = dve.mark(lambda e: e.tensor_tensor(wlo[:, h, :], raw[:, r, :], whi[:, h, :], ALU.subtract))
            state["prep"] += 1
            load()

        for _ in range(NRAW):
            load()

        ends, aside = {}, []
        for key, (kt, at, w) in where.items():
            for b in range(at, at + kt * w, w):
                ends[b // CB] = (key, b)

        def job(key, xh, xl, ready):
            kt, at, w = where[key]
            banks = [jb.take() for _ in range(1 if w == 1 else 2)]
            for b in banks:
                pe.wait(*b.free)
            pe.wait(*ready)
            for k in range(kt):
                blk = at + k * w
                c, o = blk // CB, blk % CB * P
                while state["prep"] <= min(c + AHEAD, n_chunks - 1):
                    prep()
                pe.wait(m_hi[c], m_lo[c])
                h = c % NSL
                H, L = whi[:, h, o:o + w * P], wlo[:, h, o:o + w * P]
                final = ends[c] == (key, blk)
                if w == 1:
                    trio = [(banks[0].t[:, 0:S], H, xh[k]), (banks[0].t[:, 0:S], H, xl[k]), (banks[0].t[:, 0:S], L, xh[k])]
                else:
                    trio = []
                    for t in range(2):
                        ts = slice(t * P, t * P + P)
                        trio += [(banks[t].t[:, :], xh[k][:, ts], H), (banks[t].t[:, :], xh[k][:, ts], L),
                                 (banks[t].t[:, :], xl[k][:, ts], H)]
                for n, (o_, a_, b_) in enumerate(trio):
                    f = (lambda e, o_=o_, a_=a_, b_=b_, s_=(k == 0 and n % 3 == 0), p_=(k == kt - 1 and n % 3 == 2):
                         e.matmul(o_, a_, b_, start=s_, stop=p_))
                    if n == len(trio) - 1 and (final or k == kt - 1):
                        m = pe.mark(f)
                        if final:
                            m_used[c] = m
                    else:
                        pe.do(f)
            for f in aside:
                f()
            return banks, m

        def split(src, hi, lo, ready):
            act.wait(*ready)
            m1 = act.mark(lambda e: e.activation(hi, src, ACT.Copy))
            dve.wait(m1, *ready)
            return dve.mark(lambda e: e.tensor_tensor(lo, src, hi, ALU.subtract))

        sqm = [None] * 4
        state["sq"] = 0
        lnm = [None] * 2
        state["ln"] = 0

        def sum_squares(tiles, ready, bank, col, w, wmark, first):
            for i, t in enumerate(tiles):
                j = state["sq"] % 4
                state["sq"] += 1
                pool_or = pool if i % 3 == 2 else dve
                pool_or.wait(sqm[j], *ready)
                m = pool_or.mark(lambda e, j=j, t=t: e.tensor_tensor(sq[:, j, :], t, t, ALU.mult))
                pe.wait(m, wmark, *bank.free)
                sqm[j] = m2 = pe.mark(lambda e, i=i, j=j: e.matmul(
                    bank.t[:, col:col + S], w, sq[:, j, :], start=(first and i == 0), stop=(i == len(tiles) - 1),
                    skip_group_check=True))
            return m2

        def rstd(bank, n, cols, m):
            j = state["ln"] % 2
            state["ln"] += 1
            L = R = rst[:, j, 0:cols]
            act.wait(m, m_vc)
            if lnm[j] is not None:
                act.wait(*lnm[j])
            m1 = act.mark(lambda e: e.activation(L, bank.t[:, 0:cols], ACT.Ln, bias=vec("eps"), scale=1.0 / n))
            act.wait(m1)
            m2 = act.mark(lambda e: e.activation(R, L, ACT.Exp, scale=-0.5))
            give(bank, m1)
            return R, m2, j

        def norm(src, nt, g, hi, lo, ready, war=()):
            b = xb.take()
            m = sum_squares([src[:, i, :] for i in range(nt)], ready, b, 0, ones[:, :], m_on, True)
            R, mr, j = rstd(b, nt * P, S, m)
            marks = []
            for i in range(nt):
                k = state["sq"] % 4
                state["sq"] += 1
                dve.wait(mr, sqm[k], m_vc, *ready)
                t = sq[:, k, :]
                m1 = dve.mark(lambda e, i=i, t=t: e.scalar_tensor_tensor(
                    out=t, in0=src[:, i, :], scalar=vec(g, i), in1=R, op0=ALU.mult, op1=ALU.mult))
                act.wait(*war)
                sqm[k] = m3 = split(t, hi[:, i, :], lo[:, i, :], [m1])
                marks.append(m3)
            lnm[j] = (m1,)
            return marks

        dve.wait(m_vc)
        m_hb = dve.mark(lambda e: e.tensor_scalar(hb[:, :], vc[:, V["gate_b"]:V["gate_b"] + 16], 0.5, None, ALU.mult))
        m_cw = dve.mark(lambda e: e.tensor_scalar(cw5[:, :], vc[:, V["conv_w"]:V["conv_w"] + 248], 0.5, None, ALU.mult))
        m_qg = dve.mark(lambda e: e.tensor_scalar(qg8[:, :], vec("qg"), 0.125, None, ALU.mult))

        def fence():
            return [q.last() for q in (pe, act, dve, pool)]

        def attention(c, heads, qk, vt, table, hi, lo, fill, ready, sS, sT, war=()):
            sP = sb(c, "sP", [P, 3, 384])
            mx = sb(c, "mx", [P, heads, 8])
            done, bank_s, bank_t, m_pt, m_st = {}, {}, {}, {}, {}
            m_nrm, m_exp, m_pv, m_ptc, m_tr = {}, {}, {}, {}, {}
            opair = {}

            def scores(h):
                b = xb.take()
                pe.wait(*b.free, *ready)
                parts = qk(h)
                n = 2 * len(parts)
                i = 0
                for q, k, marks in parts:
                    pe.wait(*marks)
                    for (o, a, b_) in ((b.t[:, 0:S], q[:, P:S], k[:, 0:S]), (b.t[:, S:S + P], q[:, 0:P], k[:, 0:P])):
                        i += 1
                        f = (lambda e, o=o, a=a, b_=b_, s_=(i == 1), p_=(i >= n - 1):
                             e.matmul(o, a, b_, start=s_, stop=p_, skip_group_check=True))
                        if i == n:
                            m = pe.mark(f)
                        else:
                            pe.do(f)
                bank_s[h] = (b, m)

            def softmax(h):
                b, m = bank_s[h]
                T, mt, rel = table(h)
                j = h % 3
                dve.wait(m, mt, m_exp.get(h - 3))
                dve.mark(lambda e: e.tensor_tensor_reduce(
                    sS[:, j, 0:S], b.t[:, 0:S], T, 1.0, -3e38, ALU.add, ALU.max, mx[:, h, 0:1]))
                m1 = dve.mark(lambda e: e.tensor_tensor_reduce(
                    sS[:, j, S:384], b.t[:, S:384], T[:, P:S], 1.0, -3e38, ALU.add, ALU.max, mx[:, h, 1:2]))
                give(b, m1)
                rel(m1)
                dve.wait(m1)
                m2 = dve.mark(lambda e: e.tensor_scalar(mx[:, h, 2:4], mx[:, h, 0:2], -1.0, None, ALU.mult))
                act.wait(m2, m_nrm.get(h - 3), m_tr.get(h - 3))
                act.mark(lambda e: e.activation(sP[:, j, 0:S], sS[:, j, 0:S], ACT.Exp, bias=mx[:, h, 2:3],
                                                accum_out=mx[:, h, 4:5]))
                m_exp[h] = act.mark(lambda e: e.activation(sP[:, j, S:384], sS[:, j, S:384], ACT.Exp,
                                                           bias=mx[:, h, 3:4], accum_out=mx[:, h, 5:6]))

            def normalise(h):
                j = h % 3
                dve.wait(m_exp[h])
                m4 = dve.mark(lambda e: e.reciprocal(mx[:, h, 6:8], mx[:, h, 4:6]))
                dve.wait(m4)
                dve.mark(lambda e: e.tensor_scalar(sP[:, j, 0:S], sP[:, j, 0:S], mx[:, h, 6:7], None, ALU.mult))
                m_nrm[h] = dve.mark(lambda e: e.tensor_scalar(sP[:, j, S:384], sP[:, j, S:384], mx[:, h, 7:8], None,
                                                              ALU.mult))

            def turn(h):
                j, b = h % 3, xb.take()
                pe.wait(m_nrm[h], m_id, *b.free)
                pe.do(lambda e: e.transpose(b.t[:, 0:P], sP[:, j, S:384], ident[:, :]))
                pe.do(lambda e: e.transpose(b.t[:, P:S], sP[:, j, 0:P], ident[:, :]))
                m_tr[h] = m = pe.mark(lambda e: e.transpose(b.t[:, S:384], sP[:, j, P:S], ident[:, :]))
                act.wait(m, m_pv.get(h - 2), *war)
                m_ptc[h] = act.mark(lambda e: e.activation(sT[:, h % 2, :], b.t[:, 0:384], ACT.Copy))
                give(b, m_ptc[h])

            def values(h):
                j, o = h % 2, 64 * (h % 2)
                if h % 2 == 0:
                    opair[h // 2] = xb.take()
                b = opair[h // 2]
                pe.wait(m_ptc[h], *b.free)
                pe.do(lambda e: e.matmul(b.t[o:o + 64, 0:S], vt[:, 0, 64 * h:64 * h + 64], sT[:, j, 0:S],
                                         start=True, stop=False, skip_group_check=True))
                m_pv[h] = pe.mark(lambda e: e.matmul(b.t[o:o + 64, P:S], vt[:, 1, 64 * h:64 * h + 64],
                                                     sT[:, j, S:384], start=False, stop=True, skip_group_check=True))
                if h % 2:
                    i = h // 2
                    m = split(b.t[:, 0:S], hi[:, i, :], lo[:, i, :], [m_pv[h]])
                    give(b, m)
                    done[i] = m

            for n in range(heads + 4):
                if n < heads:
                    scores(n)
                fill(n)
                if 0 <= n - 1 < heads:
                    softmax(n - 1)
                if 0 <= n - 2 < heads:
                    normalise(n - 2)
                if 0 <= n - 3 < heads:
                    turn(n - 3)
                if 0 <= n - 4 < heads:
                    values(n - 4)
            return [done[i] for i in sorted(done)]

        def add_residual(i, banks, m):
            dve.wait(m, *x_read)
            r = dve.mark(lambda e, i=i: e.scalar_tensor_tensor(
                out=X[:, i, :], in0=banks[0].t[:, 0:S], scalar=0.5, in1=X[:, i, :], op0=ALU.mult, op1=ALU.add))
            give(banks[0], r)
            return r

        x_read = []

        with ExitStack() as c:
            Q = sb(c, "Q", [P, KD, S])
            K = sb(c, "K", [P, KD, S])
            VT = sb(c, "VT", [P, 2, D])
            GA = sb(c, "GA", [P, KD, S])
            GB = sb(c, "GB", [P, KD, S])
            CI = sb(c, "CI", [P, KD, S + 30])
            CA = sb(c, "CA", [P, KD, S])
            ah = sb(c, "ah", [P, KD, S], F32R)
            al = sb(c, "al", [P, KD, S], F32R)
            sg = sb(c, "sg", [P, 3, S])
            tb = sb(c, "tb", [P, 3, S])
            ct = sb(c, "ct", [P, 4, S])

            m_h = norm(X, KD, "norm1_g", hh, hl, [m_x])
            H = [hh[:, i, :] for i in range(KD)]
            L = [hl[:, i, :] for i in range(KD)]
            m_z = pool.mark(lambda e: e.memset(CI[:, :, 0:30], 0.0))
            conv_m = {}
            sgm = [None] * 3

            def conv_dve(i):
                m = None
                for j in range(31):
                    a, w = CI[:, i, j:j + S], cw5[:, j * 8 + i:j * 8 + i + 1]
                    dve.wait(m_ci[i], m_z, m_cw, m)
                    if j == 0:
                        m = dve.mark(lambda e: e.tensor_scalar(CA[:, i, :], a, w, vec("conv_b", i), ALU.mult, ALU.add))
                    else:
                        m = dve.mark(lambda e: e.scalar_tensor_tensor(
                            out=CA[:, i, :], in0=a, scalar=w, in1=CA[:, i, :], op0=ALU.mult, op1=ALU.add))
                    yield
                conv_m[i] = m

            ctm = [None] * 4

            def conv_two(i):
                m = None
                for j in range(31):
                    a, w = CI[:, i, j:j + S], cw5[:, j * 8 + i:j * 8 + i + 1]
                    k = j % 4
                    act.wait(m_ci[i], m_z, m_cw)
                    if j == 0:
                        m = act.mark(lambda e: e.activation(CA[:, i, :], a, ACT.Identity, scale=w, bias=vec("conv_b", i)))
                    else:
                        act.wait(ctm[k])
                        m1 = act.mark(lambda e: e.activation(ct[:, k, :], a, ACT.Copy, scale=w))
                        pool.wait(m1, m)
                        ctm[k] = m = pool.mark(lambda e: e.tensor_tensor(CA[:, i, :], CA[:, i, :], ct[:, k, :], ALU.add))
                    yield
                conv_m[i] = m

            class Work:

                def __init__(self, side):
                    self.side, self.chains = side, []

                def some(self, n):
                    while n > 0 and self.chains:
                        for c in self.chains[:self.side]:
                            if next(c, 0) == 0:
                                self.chains.remove(c)
                            n -= 1

            w1, w2 = Work(2), Work(1)

            def conv_some():
                w1.some(3)
                w2.some(2)

            aside.append(conv_some)
            m_ci = {}
            for i in range(KD):
                bg, m = job(("ag", i), H, L, m_h if i == 0 else [])
                act.wait(m, sgm[i % 3])
                m1 = act.mark(lambda e, i=i, b=bg[0].t: e.activation(sg[:, i % 3, :], b[:, 0:S], ACT.Tanh, scale=0.5))
                give(bg[0], m1)
                bv, m = job(("av", i), H, L, [])
                dve.wait(m1, m)
                sgm[i % 3] = m_ci[i] = dve.mark(lambda e, i=i, b=bv[0].t: e.scalar_tensor_tensor(
                    out=CI[:, i, 30:], in0=sg[:, i % 3, :], scalar=1.0, in1=b[:, 0:S], op0=ALU.add, op1=ALU.mult))
                give(bv[0], m_ci[i])
                if i in (1, 4, 6):
                    w2.chains.append(conv_two(i))
                else:
                    w1.chains.append(conv_dve(i))
            m_v = []
            for n in range(2):
                banks, m = job(("v", n), H, L, [])
                for t in range(2):
                    act.wait(m)
                    m1 = act.mark(lambda e, n=n, t=t, b=banks[t].t: e.activation(
                        VT[:, t, n * 512:n * 512 + 512], b[:, :], ACT.Copy))
                    give(banks[t], m1)
                    m_v.append(m1)
            m_qk = {}
            pend = []

            def head_norm(which, i, buf, m):
                b = xb.take()
                m2 = sum_squares([buf[:, i, :]], [m], b, 0, bd[:, :], m_bd, True)
                R, mr, j = rstd(b, 64, S, m2)
                g = qg8[:, 0:1] if which == "q" else vec("kg")
                dve.wait(mr, m_qg)
                r = dve.mark(lambda e: e.scalar_tensor_tensor(
                    out=buf[:, i, :], in0=buf[:, i, :], scalar=g, in1=R, op0=ALU.mult, op1=ALU.mult))
                lnm[j] = (r,)
                m_qk[which, i] = r

            for i in range(KD):
                for which, buf in (("q", Q), ("k", K)):
                    banks, m = job((which, i), H, L, [])
                    act.wait(m)
                    m1 = act.mark(lambda e, i=i, buf=buf, b=banks[0].t: e.activation(buf[:, i, :], b[:, 0:S], ACT.Copy))
                    give(banks[0], m1)
                    if pend:
                        head_norm(*pend.pop())
                    pend.append((which, i, buf, m1))
            head_norm(*pend.pop())

            m_gate = {}

            def gate_job(n):
                if n >= 16:
                    return
                banks, m = job(("g", n), H, L, [])
                G = GA if n < 8 else GB
                act.wait(m, m_hb)
                m_gate[n] = act.mark(lambda e, b=banks[0].t: e.activation(
                    G[:, n % 8, :], b[:, 0:S], ACT.Tanh, scale=0.5, bias=hb[:, n:n + 1]))
                give(banks[0], m_gate[n])

            s_tb = [sem(f"s_tb{i}") for i in range(3)]
            tbf = {}

            def table1(h):
                if h >= 3:
                    sp.wait(tbf[h - 3])
                m = dma(sp, s_tb[h % 3], tb[:, h % 3, :], tabs[h], h // 3 + 1)

                def rel(mm):
                    tbf[h] = mm
                return tb[:, h % 3, :], m, rel

            def qk1(h):
                o, j = 64 * (h % 2), h // 2
                return [(Q[o:o + 64, j, :], K[o:o + 64, j, :], [m_qk["q", j], m_qk["k", j]])]

            oh, ol = ah, al
            m_o = attention(c, NH, qk1, VT, table1, oh, ol, gate_job, m_v, sb(c, "sS", [P, 3, 384]), sb(c, "sT", [P, 2, 384]))

            M = GB
            m_m = {}
            OH = [oh[:, i, :] for i in range(KD)]
            OL = [ol[:, i, :] for i in range(KD)]
            w1.some(1000)
            w2.some(1000)
            aside.clear()
            gates_done = pe.last()
            b = xb.take()
            m = None
            for i in range(KD):
                m = sum_squares([CA[:, i, :]], [conv_m[i]], b, 0, ones[:, :], m_on, i == 0)
            R, mr, j = rstd(b, D, S, m)
            m_c = []
            for i in range(KD):
                k = i % 3
                dve.wait(mr, conv_m[i])
                m1 = dve.mark(lambda e, i=i: e.scalar_tensor_tensor(
                    out=CA[:, i, :], in0=CA[:, i, :], scalar=vec("conv_norm_g", i), in1=R, op0=ALU.mult, op1=ALU.mult))
                act.wait(m1, sgm[k], m_ci[KD - 1])
                m2 = act.mark(lambda e, i=i, k=k: e.activation(sg[:, k, :], CA[:, i, :], ACT.Tanh, scale=0.5))
                dve.wait(m2)
                m3 = dve.mark(lambda e, i=i, k=k: e.scalar_tensor_tensor(
                    out=CA[:, i, :], in0=sg[:, k, :], scalar=1.0, in1=CA[:, i, :], op0=ALU.add, op1=ALU.mult))
                sgm[k] = m3
                dve.wait(m3)
                m4 = dve.mark(lambda e, i=i: e.tensor_scalar(CA[:, i, :], CA[:, i, :], 0.5, None, ALU.mult))
                act.wait(gates_done)
                dve.wait(gates_done)
                m_c.append(split(CA[:, i, :], hh[:, i, :], hl[:, i, :], [m4]))
            lnm[j] = (m1,)
            m_ya = {}
            for i in range(KD):
                banks, m = job(("co", i), H, L, m_c if i == 0 else [])
                dve.wait(m, m_gate[i])
                m_ya[i] = dve.mark(lambda e, i=i, b=banks[0].t: e.scalar_tensor_tensor(
                    out=GA[:, i, :], in0=GA[:, i, :], scalar=1.0, in1=b[:, 0:S], op0=ALU.add, op1=ALU.mult))
                give(banks[0], m_ya[i])
            co_done = pe.last()
            m_mix = []
            for i in range(KD):
                banks, m = job(("ao", i), OH, OL, m_o if i == 0 else [])
                dve.wait(m, m_gate[8 + i], m_ya[i])
                m1 = dve.mark(lambda e, i=i, b=banks[0].t: e.scalar_tensor_tensor(
                    out=GB[:, i, :], in0=GB[:, i, :], scalar=1.0, in1=b[:, 0:S], op0=ALU.add, op1=ALU.mult))
                give(banks[0], m1)
                dve.wait(m1)
                m2 = dve.mark(lambda e, i=i: e.tensor_tensor(GA[:, i, :], GA[:, i, :], GB[:, i, :], ALU.add))
                act.wait(co_done)
                dve.wait(co_done)
                m_mix.append(split(GA[:, i, :], hh[:, i, :], hl[:, i, :], [m2]))
            m_xr = []
            for i in range(KD):
                banks, m = job(("wo", i), H, L, m_mix if i == 0 else [])
                m_xr.append(add_residual(i, banks, m))
            wall = fence()

        def ffn(keys_g, keys_u, keys_d, with_conv, m_xr, wall, g):
            with ExitStack() as c:
                fh = sb(c, "fh", [P, FT, S], F32R)
                fl = sb(c, "fl", [P, FT, S], F32R)
                ug = sb(c, "ug", [P, 3, S])
                uv = sb(c, "uv", [P, 3, S])
                tt = sb(c, "tt", [P, 3, S])
                act.wait(*wall)
                dve.wait(*wall)
                pool.wait(*wall)
                m_h = norm(X, KD, g, hh, hl, m_xr)
                m_f = []
                fr = {}

                def conv3(key, i, row, buf, free):
                    banks, m = job(key, H, L, m_h if i == 0 else [])
                    b = banks[0].t
                    act.wait(m, free)
                    w = [vec("ffn_conv_w", j * 44 + row) for j in range(3)]
                    m1 = act.mark(lambda e: e.activation(buf, b[:, 0:S], ACT.Identity, scale=w[2], bias=vec("ffn_conv_b", row)))
                    dve.wait(m1)
                    m2 = dve.mark(lambda e: e.scalar_tensor_tensor(
                        out=buf[:, 1:S], in0=b[:, 0:S - 1], scalar=w[1], in1=buf[:, 1:S], op0=ALU.mult, op1=ALU.add))
                    dve.wait(m2)
                    m3 = dve.mark(lambda e: e.scalar_tensor_tensor(
                        out=buf[:, 2:S], in0=b[:, 0:S - 2], scalar=w[0], in1=buf[:, 2:S], op0=ALU.mult, op1=ALU.add))
                    give(banks[0], m3)
                    return m3

                def plain(key, i, row, buf, free):
                    banks, m = job(key, H, L, m_h if i == 0 else [])
                    act.wait(m, free)
                    m1 = act.mark(lambda e: e.activation(buf, banks[0].t[:, 0:S], ACT.Copy))
                    give(banks[0], m1)
                    return m1

                one = conv3 if with_conv else plain
                tail = None

                def finish(i, mg, mv):
                    j = i % 3
                    act.wait(mg, fr.get(("t", i - 3)))
                    mt = act.mark(lambda e: e.activation(tt[:, j, :], ug[:, j, :], ACT.Tanh, scale=0.5))
                    pool.wait(mt, mv, mg)
                    mp = pool.mark(lambda e: e.tensor_tensor(uv[:, j, :], uv[:, j, :], ug[:, j, :], ALU.mult))
                    dve.wait(mp, mt)
                    ms = dve.mark(lambda e: e.scalar_tensor_tensor(
                        out=tt[:, j, :], in0=tt[:, j, :], scalar=1.0, in1=uv[:, j, :], op0=ALU.add, op1=ALU.mult))
                    r = split(tt[:, j, :], fh[:, i, :], fl[:, i, :], [ms])
                    fr["g", i] = mp
                    fr["v", i] = ms
                    fr["t", i] = r
                    m_f.append(r)

                pend = None
                for i in range(FT):
                    mg = one((keys_g, i), i, 22 + i, ug[:, i % 3, :], fr.get(("g", i - 3)))
                    if pend:
                        finish(*pend)
                    mv = one((keys_u, i), 1, i, uv[:, i % 3, :], fr.get(("v", i - 3)))
                    pend = (i, mg, mv)
                finish(*pend)
                FH = [fh[:, i, :] for i in range(FT)]
                FL = [fl[:, i, :] for i in range(FT)]
                m_x2 = []
                for i in range(KD):
                    banks, m = job((keys_d, i), FH, FL, m_f if i == 0 else [])
                    m_x2.append(add_residual(i, banks, m))
                return m_x2, fence()

        m_x2, wall = ffn("ug", "uv", "dn", True, m_xr, wall, "norm2_g")

        with ExitStack() as c:
            qn = sb(c, "qn", [P, 4, S])
            qr = sb(c, "qr", [P, 2, S])
            kn = sb(c, "kn", [P, 4, S])
            krp = sb(c, "krp", [P, S])
            cc = sb(c, "cc", [P, 5, S])
            ch = sb(c, "ch", [P, 5, S], F32R)
            cl = sb(c, "cl", [P, 5, S], F32R)
            mv_ = sb(c, "mv_", [P, 2, 512])
            gv = sb(c, "gv", [P, 2, 512])
            GA = sb(c, "GA2", [P, KD, S])
            GB = sb(c, "GB2", [P, KD, S])
            gq = sb(c, "gq", [P, 2, S])
            gk = sb(c, "gk", [P, 2, S])
            og = sb(c, "og", [P, 4, S])
            glr = sb(c, "glr", [P, S])
            bc = sb(c, "bc", [P, 2, S])
            eb = sb(c, "eb", [P, 2, 2 * S])
            qL = sb(c, "qL", [P, 2, S])
            kL = sb(c, "kL", [P, 2, S])
            at = sb(c, "at", [P, 2, 512])
            tmp = sb(c, "tmp", [P, 2, 512])
            kd = sb(c, "kd", [P, 2, S])
            st = sb(c, "st", [P, 3, 2, P])
            ebl = sb(c, "ebl", [P, 2, 4])
            go_ = sb(c, "go_", [P, 4, S])
            msk = sb(c, "msk", [P, 7, P])
            cm = tmp[:, 0, :]
            ah = sb(c, "ah2", [P, 4, S], F32R)
            al = sb(c, "al2", [P, 4, S], F32R)
            posi = at[:, 0, 0:S].bitcast(I32)

            act.wait(*wall)
            dve.wait(*wall)
            pool.wait(*wall)
            m_h = norm(X, KD, "ln_mix_2", hh, hl, m_x2)
            s_m = [sem("s_m0"), sem("s_m1")]
            act.wait(*wall)
            m_msk = dma(act, s_m[0], msk[:, :, :], masks.rearrange("p (l i) -> p l i", l=7), 1)
            m_pos = dma(act, s_m[1], posi, pos, 1)
            m_cm0 = pool.mark(lambda e: e.memset(cm, 1.0))
            pool.wait(m_cm0)
            m_cm = pool.mark(lambda e: e.memset(cm.rearrange("p (a b) -> p a b", b=64)[:, :, 0:1], 0.0))

            ang, kf, r0, r1 = eb[:, 0, 0:S], eb[:, 0, S:2 * S], eb[:, 1, 0:S], eb[:, 1, S:2 * S]

            def step(f, *w):
                dve.wait(*w)
                return dve.mark(f)

            a = step(lambda e: e.tensor_copy(r0, posi), m_pos)
            a = step(lambda e: e.tensor_scalar(ang, r0, vec("inv"), None, ALU.mult), a)
            a = step(lambda e: e.tensor_scalar(kf, ang, 1.0 / TWO_PI, MAGIC, ALU.mult, ALU.add), a)
            a = step(lambda e: e.tensor_scalar(kf, kf, MAGIC, None, ALU.subtract), a)
            for cst in (C1, C2, C3):
                a = step(lambda e, cst=cst: e.scalar_tensor_tensor(
                    out=ang, in0=kf, scalar=-cst, in1=ang, op0=ALU.mult, op1=ALU.add), a)
            a = step(lambda e: e.tensor_scalar(r0, ang, PI_F, -PI_F, ALU.min, ALU.max), a)
            a2 = step(lambda e: e.tensor_scalar(kf, ang, float(np.pi / 2), -TWO_PI, ALU.is_gt, ALU.mult), a)
            a2 = step(lambda e: e.scalar_tensor_tensor(out=r1, in0=kf, scalar=float(np.pi / 2), in1=ang,
                                                       op0=ALU.add, op1=ALU.add), a2)
            a2 = step(lambda e: e.tensor_scalar(r1, r1, PI_F, -PI_F, ALU.min, ALU.max), a2)
            act.wait(a2)
            act.mark(lambda e: e.activation(rope[:, 1, :], r0, ACT.Sin))
            a3 = act.mark(lambda e: e.activation(rope[:, 0, :], r1, ACT.Sin))
            a4 = step(lambda e: e.tensor_scalar(rope[:, 1, :], rope[:, 1, :], vec("sgn"), None, ALU.mult), a3)
            m_rope = step(lambda e: e.tensor_scalar(rope[:, 2:4, :], rope[:, 0:2, :], 96.0 ** -0.5, None, ALU.mult), a4)

            def copy_out(key, xh, xl, ready, dst, scale=1.0, extra=()):
                banks, m = job(key, xh, xl, ready)
                act.wait(m, *extra)
                m1 = act.mark(lambda e: e.activation(dst, banks[0].t[:, 0:S], ACT.Copy, scale=scale))
                give(banks[0], m1)
                return m1

            m_cc = []
            for i in range(3):
                m_cc.append(copy_out(("cq", i), H, L, m_h, cc[:, i, :]))
            for i in range(2):
                m_cc.append(copy_out(("ckv", i), H, L, [], cc[:, 3 + i, :]))

            def roped(k1, k2, xh, xl, ready, dst, cs, sn, n):
                b1, m1 = job(k1, xh, xl, ready)
                dve.wait(m1, m_rope)
                d1 = dve.mark(lambda e: e.tensor_tensor(dst, b1[0].t[:, 0:S], cs, ALU.mult))
                give(b1[0], d1)
                b2, m2 = job(k2, xh, xl, [])
                dve.wait(m2, rfree.get(n))
                d2 = dve.mark(lambda e: e.tensor_tensor(glr2[:, n, :], b2[0].t[:, 0:S], sn, ALU.mult))
                give(b2[0], d2)
                dve.wait(d1, d2)
                d3 = dve.mark(lambda e: e.tensor_tensor(dst, dst, glr2[:, n, :], ALU.add))
                rfree[n] = d3
                return d3

            rfree = {}
            glr2 = qL
            m_kr = roped(("kr", 0), ("krs", 0), H, L, [], krp[:, :], rope[:, 0, :], rope[:, 1, :], 0)
            m_glr = copy_out(("glr", 0), H, L, [], glr[:, :])
            m_nq = norm(cc[:, 0:3, :], 3, "mla_norm_cq_2", ch[:, 0:3, :], cl[:, 0:3, :], m_cc[0:3])
            m_gq = [copy_out(("gq", i), H, L, [], gq[:, i, :], 0.125) for i in range(2)]
            m_nk = norm(cc[:, 3:5, :], 2, "mla_norm_ckv_2", ch[:, 3:5, :], cl[:, 3:5, :], m_cc[3:5])
            m_gk = [copy_out(("gk", i), H, L, [], gk[:, i, :]) for i in range(2)]
            banks, m = job(("gv", 0), H, L, [])
            m_gv = []
            for t in range(2):
                act.wait(m)
                m1 = act.mark(lambda e, t=t, b=banks[t].t: e.activation(gv[:, t, :], b[:, :], ACT.Copy))
                give(banks[t], m1)
                m_gv.append(m1)
            CH = [ch[:, i, :] for i in range(5)]
            CL = [cl[:, i, :] for i in range(5)]
            m_q, m_k, m_qr = {}, {}, {}
            for i in range(4):
                m_q[i] = copy_out(("qn", i), CH[0:3], CL[0:3], m_nq, qn[:, i, :], 96.0 ** -0.5)
            for i in range(2):
                m_qr[i] = roped(("qr", i), ("qrs", i), CH[0:3], CL[0:3], [], qr[:, i, :], rope[:, 2, :], rope[:, 3, :], 1)
            for i in range(4):
                m_k[i] = copy_out(("kn", i), CH[3:5], CL[3:5], m_nk, kn[:, i, :])
            banks, m = job(("mv", 0), CH[3:5], CL[3:5], [])
            m_mv = []
            for t in range(2):
                act.wait(m)
                m1 = act.mark(lambda e, t=t, b=banks[t].t: e.activation(mv_[:, t, :], b[:, :], ACT.Copy))
                give(banks[t], m1)
                m_mv.append(m1)

            gx, ge = eb[:, 0, :], eb[:, 1, :]
            b = xb.take()
            pe.wait(m_glr, m_wg2, *b.free)
            pe.do(lambda e: e.matmul(b.t[:, 0:S], wg2[:, 0:P], glr[0:16, :], start=True, stop=True, skip_group_check=True))
            m = pe.mark(lambda e: e.matmul(b.t[:, S:2 * S], wg2[:, P:2 * P], glr[0:16, :], start=False, stop=True,
                                           skip_group_check=True))
            dve.wait(m, a3)
            for i in range(2):
                g1 = dve.mark(lambda e, i=i: e.tensor_scalar(gx[:, i * S:i * S + S], b.t[:, i * S:i * S + S],
                                                             vec("gla_b_gate_2", i), None, ALU.add))
            give(b, g1)
            act.wait(g1)
            g2 = act.mark(lambda e: e.activation(ge, gx, ACT.Abs))
            act.wait(g2)
            g3 = act.mark(lambda e: e.activation(ge, ge, ACT.Exp, scale=-1.0))
            act.wait(g3)
            g4 = act.mark(lambda e: e.activation(ge, ge, ACT.Ln, bias=vec("one")))
            g5 = step(lambda e: e.scalar_tensor_tensor(out=gx, in0=gx, scalar=0.0, in1=ge, op0=ALU.min, op1=ALU.subtract), g4)
            bcf = bc[:, :, :].rearrange("p a s -> p (a s)")
            m_bc = step(lambda e: e.tensor_tensor_scan(bcf, cm, gx, 0.0, ALU.mult, ALU.add), g5, m_cm)
            gqf = gq[:, :, :].rearrange("p a s -> p (a s)")
            gkf = gk[:, :, :].rearrange("p a s -> p (a s)")
            qLf = qL[:, :, :].rearrange("p a s -> p (a s)")
            kLf = kL[:, :, :].rearrange("p a s -> p (a s)")
            kdf = kd[:, :, :].rearrange("p a s -> p (a s)")
            gst = {"pe": [], "e": {0: [m_bc], 1: [m_bc]}, "acc": {}, "tmp": {}}

            def pair_products(q_, k_, ready):
                bs = [xb.take(), xb.take()]
                pe.wait(*ready, *bs[0].free, *bs[1].free)
                for par in range(2):
                    o = 64 * par
                    for n in range(4):
                        p_, t = n // 2, n % 2
                        f = (lambda e, n=n, o=o, p_=p_, t=t, b=bs[par].t: e.matmul(
                            b[:, n * P:n * P + P], k_[o:o + 64, p_, t * P:t * P + P], q_[o:o + 64, p_, t * P:t * P + P],
                            start=(n == 0), stop=True, skip_group_check=True))
                        if n == 3:
                            m = pe.mark(f)
                        else:
                            pe.do(f)
                return bs, m

            def level(n):
                s = LEVELS[n]
                if s == 0:
                    bs, m = pair_products(gq, gk, m_gq + m_gk)
                else:
                    E = eb[:, n % 2, :]
                    bv = bcf.rearrange("p (n w) -> p n w", w=2 * s)
                    Ev = E.rearrange("p (n w) -> p n w", w=2 * s)
                    ref = bv[:, :, s - 1:s].to_broadcast([P, 512 // (2 * s), 2 * s])
                    l1 = step(lambda e: e.tensor_tensor(Ev, bv, ref, ALU.subtract), m_bc, *gst["e"][n % 2])
                    act.wait(l1)
                    l2 = act.mark(lambda e: e.activation(E, E, ACT.Abs))
                    act.wait(l2)
                    l3 = act.mark(lambda e: e.activation(E, E, ACT.Exp, scale=-1.0 / 16))
                    pool.wait(l3, m_gk[1], *gst["pe"])
                    l5 = pool.mark(lambda e: e.tensor_tensor(kLf, gkf, E, ALU.mult))
                    l4 = step(lambda e: e.tensor_tensor(qLf, gqf, E, ALU.mult), l3, m_gq[1], *rfree.values(), *gst["pe"])
                    gst["e"][n % 2] = [l4, l5]
                    bs, m = pair_products(qL, kL, [l4, l5])
                    gst["pe"] = [m]
                gst["b"] = (n, bs, m)

            def level_add():
                n, bs, m = gst["b"]
                mb = msk[:, n:n + 1, :].to_broadcast([P, 4, P])
                for par in range(2):
                    bt = bs[par].t[:, :].rearrange("p (a i) -> p a i", a=4)
                    if n == 0:
                        g = step(lambda e: e.tensor_tensor(at[:, par, :].rearrange("p (a i) -> p a i", a=4), bt, mb,
                                                           ALU.mult), m, m_msk)
                        gst["acc"][par] = g
                    else:
                        g = step(lambda e: e.tensor_tensor(tmp[:, par, :].rearrange("p (a i) -> p a i", a=4), bt, mb,
                                                           ALU.mult), m, m_msk, gst["tmp"].get(par))
                        pool.wait(g, gst["acc"][par])
                        gst["acc"][par] = gst["tmp"][par] = pool.mark(lambda e: e.tensor_tensor(
                            at[:, par, :], at[:, par, :], tmp[:, par, :], ALU.add))
                    give(bs[par], g)

            def decays():
                E, E2 = eb[:, 0, :], eb[:, 1, :]
                bv = bcf.rearrange("p (n w) -> p n w", w=64)
                Ev = E.rearrange("p (n w) -> p n w", w=64)
                last = bv[:, :, 63:64]
                l1 = step(lambda e: e.tensor_tensor(Ev, bv, last.to_broadcast([P, 8, 64]), ALU.subtract), m_bc, *gst["e"][0])
                act.wait(l1)
                l2 = act.mark(lambda e: e.activation(E, E, ACT.Exp, scale=-1.0 / 16))
                l3 = step(lambda e: e.tensor_tensor(kLf, gkf, E, ALU.mult), l2, *gst["pe"])
                b = xb.take()
                pe.wait(l3, m_id, *b.free)
                for t in range(2):
                    for p_ in range(2):
                        f = lambda e, t=t, p_=p_: e.transpose(b.t[:, t * S + p_ * P:t * S + p_ * P + P],
                                                              kL[:, p_, t * P:t * P + P], ident[:, :])
                        m = pe.mark(f)
                act.wait(m)
                l4 = act.mark(lambda e: e.activation(kdf, b.t[:, :], ACT.Copy))
                give(b, l4)
                act.wait(*gst["e"][1])
                l5 = act.mark(lambda e: e.activation(E2, bcf, ACT.Exp, scale=1.0 / 16))
                act.mark(lambda e: e.activation(ebl[:, :, :].rearrange("p a c -> p (a c)"),
                                                last.rearrange("p n w -> p (n w)"), ACT.Exp, scale=1.0 / 16))
                l6 = act.last()
                l7 = step(lambda e: e.tensor_tensor(qLf, gqf, E2, ALU.mult), l5, *gst["pe"])
                prev = None
                for ci in range(3):
                    o, t = 64 * (ci % 2), ci // 2
                    b = xb.take()
                    pe.wait(l4, *m_gv, *b.free)
                    for p_ in range(2):
                        f = lambda e, p_=p_, o=o, t=t, b=b: e.matmul(
                            b.t[:, p_ * S:p_ * S + S], kd[o:o + 64, t, p_ * P:p_ * P + P],
                            gv[o:o + 64, t, p_ * S:p_ * S + S], start=(p_ == 0), stop=True, skip_group_check=True)
                        m = pe.mark(f)
                    for p_ in range(2):
                        for hf in range(2):
                            r = slice(64 * hf, 64 * hf + 64)
                            U = b.t[r, p_ * S + hf * P:p_ * S + hf * P + P]
                            if ci == 0:
                                g = step(lambda e, r=r, p_=p_, U=U: e.tensor_copy(st[r, 0, p_, :], U), m)
                            else:
                                g = step(lambda e, r=r, p_=p_, U=U, ci=ci: e.scalar_tensor_tensor(
                                    out=st[r, ci, p_, :], in0=st[r, ci - 1, p_, :], scalar=ebl[r, p_, ci:ci + 1], in1=U,
                                    op0=ALU.mult, op1=ALU.add), m, l6, prev)
                    prev = g
                    give(b, g)
                gst["st"] = (prev, l7)

            def gla_out():
                prev, l7 = gst["st"]
                bs = [xb.take(), xb.take()]
                pe.wait(prev, l7, gst["acc"][0], gst["acc"][1], *m_gv, *bs[0].free, *bs[1].free)
                marks = []
                for par in range(2):
                    b, o = bs[par].t, 64 * par
                    for p_ in range(2):
                        h = 2 * p_ + par
                        for t in range(2):
                            pe.do(lambda e, b=b, p_=p_, t=t, h=h, par=par: e.matmul(
                                b[:, p_ * S + t * P:p_ * S + t * P + P], gv[:, t, h * P:h * P + P],
                                at[:, par, (2 * p_ + t) * P:(2 * p_ + t) * P + P],
                                start=(p_ == 0 and t == 0), stop=False, skip_group_check=True))
                    for p_ in range(2):
                        for ci in range(1, 4):
                            f = (lambda e, b=b, p_=p_, o=o, ci=ci: e.matmul(
                                b[:, p_ * S + ci * 64:p_ * S + ci * 64 + 64], st[o:o + 64, ci - 1, p_, :],
                                qL[o:o + 64, p_, ci * 64:ci * 64 + 64], start=False, stop=True, skip_group_check=True))
                            m = pe.mark(f)
                    for p_ in range(2):
                        h = 2 * p_ + par
                        act.wait(m)
                        marks.append((h, act.mark(lambda e, b=b, h=h, p_=p_: e.activation(
                            go_[:, h, :], b[:, p_ * S:p_ * S + S], ACT.Copy))))
                    give(bs[par], marks[-1][1])
                gst["o"] = dict(marks)

            def gla_norm():
                for pr in range(2):
                    b = xb.take()
                    for n in range(2):
                        h = 2 * pr + n
                        m = sum_squares([go_[:, h, :]], [gst["o"][h]], b, n * S, ones[:, :], m_on, n == 0)
                    R, mr, j = rstd(b, P, 512, m)
                    for n in range(2):
                        h = 2 * pr + n
                        g1 = step(lambda e, h=h, n=n: e.scalar_tensor_tensor(
                            out=go_[:, h, :], in0=go_[:, h, :], scalar=vec("gla_norm_2"), in1=R[:, n * S:n * S + S],
                            op0=ALU.mult, op1=ALU.mult), mr)
                        g2 = step(lambda e, h=h: e.tensor_tensor(go_[:, h, :], go_[:, h, :], og[:, h, :], ALU.mult), g1, m_og[h])
                        act.wait(*uq_done)
                        dve.wait(*uq_done)
                        m_g.append(split(go_[:, h, :], ch[:, h, :], cl[:, h, :], [g2]))
                    lnm[j] = (g1,)

            m_og, m_g = {}, []
            uq_done = [pe.last()]
            level(0)
            for i in range(4):
                banks, m = job(("og", i), H, L, [])
                b = banks[0].t
                act.wait(m)
                m1 = act.mark(lambda e, i=i, b=b: e.activation(og[:, i, :], b[:, 0:S], ACT.Tanh, scale=0.5))
                dve.wait(m1)
                m2 = dve.mark(lambda e, i=i, b=b: e.scalar_tensor_tensor(
                    out=og[:, i, :], in0=og[:, i, :], scalar=1.0, in1=b[:, 0:S], op0=ALU.add, op1=ALU.mult))
                give(banks[0], m2)
                m_og[i] = step(lambda e, i=i: e.tensor_scalar(og[:, i, :], og[:, i, :], 0.5, None, ALU.mult), m2)
                level_add() if i == 0 else None
            m_gate = {}

            def gate2(n):
                banks, m = job(("g2", n), H, L, [])
                G = GA if n < 8 else GB
                act.wait(m)
                m_gate[n] = act.mark(lambda e, b=banks[0].t: e.activation(G[:, n % 8, :], b[:, 0:S], ACT.Tanh, scale=0.5))
                give(banks[0], m_gate[n])

            gate_n = [0]

            def some_gates(k):
                for _ in range(k):
                    if gate_n[0] < 16:
                        gate2(gate_n[0])
                        gate_n[0] += 1

            for n in range(1, 7):
                level(n)
                some_gates(1)
                level_add()
            decays()
            some_gates(1)
            gla_out()
            some_gates(1)
            gla_norm()

            def table2(h):
                return caus[:, :], m_caus, lambda mm: None

            def qk2(h):
                o, j, o2, j2 = 64 * (h % 2), h // 2, 32 * (h % 4), h // 4
                return [(qn[o:o + 64, j, :], kn[o:o + 64, j, :], [m_q[j], m_k[j]]),
                        (qr[o2:o2 + 32, j2, :], krp[o2:o2 + 32, :], [m_qr[j2], m_kr])]

            m_o = attention(c, MH, qk2, mv_, table2, ah, al, lambda n: some_gates(1), m_mv,
                            cc[:, :, :].rearrange("p a s -> p (a s)")[:, 0:1152].rearrange("p (a s) -> p a s", a=3),
                            eb[:, :, :].rearrange("p a s -> p (a s)")[:, 0:768].rearrange("p (a s) -> p a s", a=2),
                            [gst["st"][1]])
            some_gates(16)
            m_ya, m_mix = {}, []
            OH, OL = [ah[:, i, :] for i in range(4)], [al[:, i, :] for i in range(4)]
            for i in range(KD):
                banks, m = job(("mo", i), OH, OL, m_o)
                m_ya[i] = step(lambda e, i=i, b=banks[0].t: e.scalar_tensor_tensor(
                    out=GA[:, i, :], in0=GA[:, i, :], scalar=1.0, in1=b[:, 0:S], op0=ALU.add, op1=ALU.mult), m, m_gate[i])
                give(banks[0], m_ya[i])
            h_done = pe.last()
            for i in range(KD):
                banks, m = job(("go", i), CH[0:4], CL[0:4], m_g)
                m1 = step(lambda e, i=i, b=banks[0].t: e.scalar_tensor_tensor(
                    out=GB[:, i, :], in0=GB[:, i, :], scalar=1.0, in1=b[:, 0:S], op0=ALU.add, op1=ALU.mult), m, m_gate[8 + i])
                give(banks[0], m1)
                m2 = step(lambda e, i=i: e.tensor_tensor(GA[:, i, :], GA[:, i, :], GB[:, i, :], ALU.add), m1, m_ya[i])
                act.wait(h_done)
                dve.wait(h_done)
                m_mix.append(split(GA[:, i, :], hh[:, i, :], hl[:, i, :], [m2]))
            m_xr = []
            for i in range(KD):
                banks, m = job(("wo2", i), H, L, m_mix)
                m_xr.append(add_residual(i, banks, m))
            wall = fence()

        m_x4, wall = ffn("fg", "fu", "fd", False, m_xr, wall, "ln_ffn_2")

        b = xb.take()
        m = sum_squares([X[:, i, :] for i in range(KD)], m_x4, b, 0, ones[:, :], m_on, True)
        R, mr, j = rstd(b, D, S, m)
        s_o = sem("s_o")
        outv = out.rearrange("p (k s) -> p k s", k=KD)
        for i in range(KD):
            dve.wait(mr)
            m1 = dve.mark(lambda e, i=i: e.scalar_tensor_tensor(
                out=X[:, i, :], in0=X[:, i, :], scalar=vec("final_norm_2", i), in1=R, op0=ALU.mult, op1=ALU.mult))
            if i % 2:
                sp.wait(m1)
                mo = dma(sp, s_o, outv[:, i - 1:i + 1, :], X[:, i - 1:i + 1, :], i // 2 + 1)
        sp.wait(mo)

    with ExitStack() as outer:
        block = outer.enter_context(nc.Block())

        @block.tensor
        def _(e):
            walk(e, "s_pe")

        @block.scalar
        def _(e):
            walk(e, "s_act")

        @block.vector
        def _(e):
            walk(e, "s_dve")

        @block.gpsimd
        def _(e):
            walk(e, "s_pool")

        @block.sync
        def _(e):
            walk(e, "s_sp")


def shape_constants():
    p = np.arange(P)[:, None]
    d = P + p - np.arange(S)[None, :]
    count = ((d >= 0) & (d <= 128)).astype(np.float64) + ((d >= 0) & (d % 4 == 0)) + ((d >= 0) & (d % 16 == 0))
    lc = np.where(count > 0, np.log(np.maximum(count, 1)), NEG)
    tabs = np.empty((NH + 1, P, S), np.float32)
    for h in range(NH):
        slope = 2.0 ** (-8.0 * (h + 1) / NH)
        tabs[h] = np.where(count > 0, lc - slope * d, NEG)
    tabs[NH] = np.where(d >= 0, 0.0, NEG)
    j, i = np.arange(P)[:, None], np.arange(P)[None, :]
    ms = np.zeros((P, 7, P), np.float32)
    for n, s in enumerate(LEVELS):
        if s == 0:
            ms[:, n] = j == i
        else:
            ms[:, n] = (j // (2 * s) == i // (2 * s)) & (j % (2 * s) < s) & (i % (2 * s) >= s)
    half = np.arange(16, dtype=np.float32) / np.float32(16)
    inv = (np.float32(1.0) / (np.float32(10000.0) ** half)).astype(np.float32)
    q = np.arange(P)
    return tabs, ms.reshape(P, 7 * P), inv[q % 16], np.where(q % 32 < 16, -1.0, 1.0).astype(np.float32)


def kernel(**inputs):
    import concourse.bacc as bacc
    from concourse.bass_utils import run_bass_kernel_spmd

    a = {k: np.ascontiguousarray(v) for k, v in inputs.items()}
    placed, n_chunks = place_jobs()
    ws = np.zeros((n_chunks, P, CW), np.float32)
    for _, name, cols, kt, at in placed:
        w = a[name][0]
        n = len(cols)
        for k in range(kt):
            b = at + k * (n // P)
            o = b % CB * P
            ws[b // CB, :, o:o + n] = w[k * P:(k + 1) * P][:, cols]
    tabs, ms, inv, sgn = shape_constants()
    V, NV = vec_at()
    vecs = np.zeros((P, NV), np.float32)

    def put(name, rows):
        vecs[:, V[name]:V[name] + rows.shape[0]] = rows.T

    for name in ("norm1_g", "gate_b", "conv_b", "conv_norm_g", "norm2_g", "ffn_conv_b", "ln_mix_2", "mla_norm_cq_2",
                 "mla_norm_ckv_2", "gla_b_gate_2", "gla_norm_2", "ln_ffn_2", "final_norm_2", "conv_w", "ffn_conv_w"):
        put(name, a[name].reshape(-1, P))
    put("qg", np.concatenate([a["q_norm_g"][0]] * 2)[None])
    put("kg", np.concatenate([a["k_norm_g"][0]] * 2)[None])
    put("inv", inv[None])
    put("sgn", sgn[None])
    put("eps", np.full((1, P), EPS, np.float32))
    put("one", np.ones((1, P), np.float32))
    xs = np.ascontiguousarray(a["x"][0].T.reshape(KD, P, S).transpose(1, 0, 2).reshape(P, KD * S))
    feed = {
        "ws": ws, "xs": xs, "vecs": vecs,
        "pos": np.ascontiguousarray(np.broadcast_to(a["positions_2"].reshape(1, S), (P, S))),
        "wgate": a["gla_w_gate2_2"][0], "tabs": tabs, "lmask": ms,
    }
    nc = bacc.Bacc("TRN2", target_bir_lowering=False, num_devices=1)
    args = [nc.dram_tensor(n, v.shape, mybir.dt.from_np(v.dtype), kind="ExternalInput").ap() for n, v in feed.items()]
    out = nc.dram_tensor("out", (P, KD * S), F32, kind="ExternalOutput").ap()
    two_blocks(nc, args[0], args[1], args[2], args[3], args[4], args[5], args[6], out)
    r = run_bass_kernel_spmd(nc, [feed], core_ids=[0])
    y = r.results[0]["out"]
    return np.ascontiguousarray(y.reshape(P, KD, S).transpose(2, 1, 0).reshape(1, S, D))
```

```python
from contextlib import ExitStack

import numpy as np

import concourse.bass as bass
from concourse import mybir

F32 = mybir.dt.float32
F32R = mybir.dt.float32r
I32 = mybir.dt.int32
ALU = mybir.AluOpType
ACT = mybir.ActivationFunctionType
AX = mybir.AxisListType

P = 128
S = 256
D = 1024
KD = D // P
FT = 22
NH = 16
MH = 8
CB = 8
CW = CB * P
NRAW = 4
NSL = 5
AHEAD = 3
EPS = 1e-6
NEG = -1e30
TWO_PI = 2.0 * np.pi
C1 = 6.28125
C2 = float(np.float32(np.round((TWO_PI - C1) * 2 ** 19) / 2 ** 19))
C3 = float(np.float32(TWO_PI - C1 - C2))
PI_F = 3.1415925
MAGIC = 12582912.0
LEVELS = (0, 32, 16, 8, 4, 2, 1)


def rng(a, n=P):
    return list(range(a, a + n))


def stream_jobs():
    jobs = []

    def add(key, name, cols, kt):
        jobs.append((key, name, cols, kt))

    for i in range(KD):
        add(("ag", i), "w_in", rng(1024 + i * P), KD)
        add(("av", i), "w_in", rng(i * P), KD)
    for n in range(2):
        add(("v", n), "w_in", rng(4096 + n * 512, 512), KD)
    for i in range(KD):
        add(("q", i), "w_in", rng(2048 + i * P), KD)
        add(("k", i), "w_in", rng(3072 + i * P), KD)
    for i in range(16):
        add(("g", i), "w_in", rng(5120 + i * P), KD)
    for i in range(KD):
        add(("ao", i), "w_attn_out", rng(i * P), KD)
    for i in range(KD):
        add(("co", i), "w_conv_out", rng(i * P), KD)
    for i in range(KD):
        add(("wo", i), "w_out", rng(i * P), KD)
    for i in range(FT):
        add(("ug", i), "w_up", rng(2816 + i * P), KD)
        add(("uv", i), "w_up", rng(i * P), KD)
    for i in range(KD):
        add(("dn", i), "w_down", rng(i * P), FT)
    kr = 640
    for i in range(3):
        add(("cq", i), "w_in_2", rng(i * P), KD)
    for i in range(2):
        add(("ckv", i), "w_in_2", rng(384 + i * P), KD)
    add(("kr", 0), "w_in_2", rng(kr, 32) * 4, KD)
    add(("krs", 0), "w_in_2", (rng(kr + 16, 16) + rng(kr, 16)) * 4, KD)
    add(("glr", 0), "w_in_2", rng(1696, 16) * 8, KD)
    for i in range(2):
        add(("gq", i), "w_in_2", rng(672 + i * P), KD)
    for i in range(2):
        add(("gk", i), "w_in_2", rng(928 + i * P), KD)
    add(("gv", 0), "w_in_2", rng(1184, 512), KD)
    for i in range(4):
        add(("qn", i), "mla_w_uq_2", rng(192 * i, 64) + rng(192 * i + 96, 64), 3)
    for i in range(2):
        add(("qr", i), "mla_w_uq_2", sum((rng(96 * (4 * i + h) + 64, 32) for h in range(4)), []), 3)
        add(("qrs", i), "mla_w_uq_2",
            sum((rng(96 * (4 * i + h) + 80, 16) + rng(96 * (4 * i + h) + 64, 16) for h in range(4)), []), 3)
    for i in range(4):
        add(("kn", i), "mla_w_ukv_2", rng(256 * i, 64) + rng(256 * i + 128, 64), 2)
    add(("mv", 0), "mla_w_ukv_2", sum((rng(128 * h + 64, 64) for h in range(MH)), []), 2)
    for i in range(4):
        add(("og", i), "w_in_2", rng(1712 + i * P), KD)
    for i in range(16):
        add(("g2", i), "w_in_2", rng(2224 + i * P), KD)
    for i in range(KD):
        add(("mo", i), "mla_w_o_2", rng(i * P), 4)
    for i in range(KD):
        add(("go", i), "gla_w_o_2", rng(i * P), 4)
    for i in range(KD):
        add(("wo2", i), "w_out_2", rng(i * P), KD)
    for i in range(FT):
        add(("fg", i), "ffn_w_gate_2", rng(i * P), KD)
        add(("fu", i), "ffn_w_up_2", rng(i * P), KD)
    for i in range(KD):
        add(("fd", i), "ffn_w_down_2", rng(i * P), FT)
    return jobs


def place_jobs():
    at, out = 0, []
    for key, name, cols, kt in stream_jobs():
        w = len(cols) // P
        at += -at % w
        out.append((key, name, cols, kt, at))
        at += kt * w
    return out, -(-at // CB)


VECS = [("norm1_g", 8), ("gate_b", 16), ("conv_b", 8), ("conv_norm_g", 8), ("qg", 1), ("kg", 1),
        ("norm2_g", 8), ("ffn_conv_b", 44), ("ln_mix_2", 8), ("mla_norm_cq_2", 3), ("mla_norm_ckv_2", 2),
        ("gla_b_gate_2", 2), ("gla_norm_2", 1), ("ln_ffn_2", 8), ("final_norm_2", 8),
        ("conv_w", 31 * 8), ("ffn_conv_w", 3 * 44), ("inv", 1), ("sgn", 1), ("eps", 1), ("one", 1)]


def vec_at():
    at, out = 0, {}
    for n, w in VECS:
        out[n] = at
        at += w
    return out, at


class Queue:

    def __init__(self, eng, sem, serial=False):
        self.eng, self.sem, self.n, self.seen, self.serial = eng, sem, 0, {}, serial

    def wait(self, *marks):
        for m in marks:
            if m is None:
                continue
            sem, v, i = m
            if self.seen.get(i, 0) < v:
                self.seen[i] = v
                if self.eng is not None:
                    self.eng.wait_ge(sem, v)

    def do(self, f):
        if self.eng is not None:
            f(self.eng)

    def mark(self, f):
        if self.serial:
            self.wait(self.last())
        self.n += 1
        if self.eng is not None:
            f(self.eng).then_inc(self.sem, 1)
        return self.last()

    def last(self):
        return (self.sem, self.n, self.sem.name) if self.n else None

    def dma(self, s, dst, src, n):
        if self.eng is not None:
            self.eng.dma_start(dst, src).then_inc(s, 16)
        return (s, 16 * n, s.name)


class Bank:
    def __init__(self, t):
        self.t, self.free, self.busy = t, [], False


class Banks:
    def __init__(self, ts):
        self.b, self.i = [Bank(t) for t in ts], 0

    def take(self):
        for _ in self.b:
            b = self.b[self.i]
            self.i = (self.i + 1) % len(self.b)
            if not b.busy:
                b.busy = True
                return b
        raise AssertionError("no free PSUM bank")


def give(bank, *marks):
    bank.free, bank.busy = list(marks), False


def two_blocks(nc, ws, x, vecs, pos, w_gate2, tabs, masks, out):
    V, NV = vec_at()
    placed, n_chunks = place_jobs()
    where = {key: (kt, at, len(cols) // P) for key, _, cols, kt, at in placed}

    made = {}

    def walk(block_engine, who):
        used = set()
        ctx = ExitStack() if made else outer

        def once(name, make):
            while name in used:
                name += "_"
            used.add(name)
            if name not in made:
                made[name] = make(name)
            return made[name]

        def sem(name):
            return once(name, lambda n: outer.enter_context(nc.semaphore(n)))

        def sb(c, name, shape, dt=F32):
            return once(name, lambda n: c.enter_context(nc.sbuf_tensor(n, shape, dt)))

        def psum(name):
            return once(name, lambda n: outer.enter_context(nc.psum_tensor(n, [P, 512], F32)))

        def queue(name, serial=False):
            return Queue(block_engine if who == name else None, sem(name), serial)

        pe, act, dve, pool, sp = queue("s_pe"), queue("s_act"), queue("s_dve"), queue("s_pool", True), queue("s_sp")

        def dma(q, s, dst, src, n):
            return q.dma(s, dst, src, n)

        xb = Banks([psum(f"px{i}") for i in range(8)])

        raw = sb(ctx, "raw", [P, NRAW, CW])
        whi = sb(ctx, "whi", [P, NSL, CW], F32R)
        wlo = sb(ctx, "wlo", [P, NSL, CW], F32R)
        X = sb(ctx, "X", [P, KD, S])
        hh = sb(ctx, "hh", [P, KD, S], F32R)
        hl = sb(ctx, "hl", [P, KD, S], F32R)
        vc = sb(ctx, "vc", [P, NV])
        hb = sb(ctx, "hb", [P, 16])
        cw5 = sb(ctx, "cw5", [P, 31 * 8])
        qg8 = sb(ctx, "qg8", [P, 1])
        ones = sb(ctx, "ones", [P, P])
        bd = sb(ctx, "bd", [P, P])
        ident = sb(ctx, "ident", [P, P])
        rope = sb(ctx, "rope", [P, 4, S])
        wg2 = sb(ctx, "wg2", [16, S])
        caus = sb(ctx, "caus", [P, S])
        rst = sb(ctx, "rst", [P, 2, 512])
        sq = sb(ctx, "sq", [P, 4, S])
        sqa = sb(ctx, "sqa", [P, 2, S])

        def vec(name, i=0):
            return vc[:, V[name] + i:V[name] + i + 1]

        s_c = [sem(f"s_c{i}") for i in range(6)]
        m_x = dma(act, s_c[0], X[:, :, :], x.rearrange("p (k s) -> p k s", k=KD), 1)
        m_vc = dma(act, s_c[1], vc[:, :], vecs, 1)
        m_wg2 = dma(act, s_c[2], wg2[:, :], w_gate2, 1)
        m_caus = dma(act, s_c[3], caus[:, :], tabs[NH], 1)
        m_on = pool.mark(lambda e: e.memset(ones[:, :], 1.0))
        m_b0 = pool.mark(lambda e: e.memset(bd[:, :], 0.0))
        m_i0 = pool.mark(lambda e: e.memset(ident[:, :], 0.0))
        pool.wait(m_b0)
        pool.mark(lambda e: e.memset(bd[0:64, 0:64], 1.0))
        m_bd = pool.mark(lambda e: e.memset(bd[64:128, 64:128], 1.0))
        pool.wait(m_i0)
        m_id = pool.mark(lambda e: e.affine_select(out=ident[:, :], in_=ident[:, :], compare_op=ALU.not_equal,
                                                   fill=1.0, base=0, pattern=[[-1, P]], channel_multiplier=1))

        s_raw = [sem(f"s_raw{i}") for i in range(NRAW)]
        m_raw, m_hi, m_lo, m_used = {}, {}, {}, {}
        state = {"load": 0, "high": 0, "low": 0}

        def load():
            c = state["load"]
            if c >= n_chunks:
                return
            if c >= NRAW:
                sp.wait(m_hi[c - NRAW], m_lo[c - NRAW])
            m_raw[c] = dma(sp, s_raw[c % NRAW], raw[:, c % NRAW, :], ws[c], c // NRAW + 1)
            state["load"] += 1

        def high():
            c = state["high"]
            state["high"] += 1
            r, h = c % NRAW, c % NSL
            act.wait(m_raw[c])
            if c >= NSL:
                act.wait(m_used[c - NSL], m_lo[c - NSL])
            m_hi[c] = act.mark(lambda e: e.activation(whi[:, h, :], raw[:, r, :], ACT.Copy))

        def low():
            c = state["low"]
            state["low"] += 1
            r, h = c % NRAW, c % NSL
            dve.wait(m_hi[c], m_raw[c])
            if c >= NSL:
                dve.wait(m_used[c - NSL])
            m_lo[c] = dve.mark(lambda e: e.tensor_tensor(wlo[:, h, :], raw[:, r, :], whi[:, h, :], ALU.subtract))
            load()

        for _ in range(NRAW):
            load()

        ends, aside, due = {}, [], [[] for _ in range(4)]

        def later(n, f):
            due[n].append(f)

        def settle():
            for d in due:
                while d:
                    d.pop(0)()

        for key, (kt, at, w) in where.items():
            for b in range(at, at + kt * w, w):
                ends[b // CB] = (key, b)

        def job(key, xh, xl, ready):
            kt, at, w = where[key]
            banks = [xb.take() for _ in range(1 if w == 1 else 2)]
            for b in banks:
                pe.wait(*b.free)
            if len(ready) != kt:
                pe.wait(*ready)
            for k in range(kt):
                if len(ready) == kt:
                    pe.wait(ready[k])
                blk = at + k * w
                c, o = blk // CB, blk % CB * P
                while state["low"] <= min(c + AHEAD, n_chunks - 1):
                    while state["high"] <= min(state["low"] + 1, n_chunks - 1):
                        high()
                    low()
                pe.wait(m_hi[c], m_lo[c])
                h = c % NSL
                H, L = whi[:, h, o:o + w * P], wlo[:, h, o:o + w * P]
                final = ends[c] == (key, blk)
                if w == 1:
                    trio = [(banks[0].t[:, 0:S], H, xh[k]), (banks[0].t[:, 0:S], H, xl[k]), (banks[0].t[:, 0:S], L, xh[k])]
                else:
                    trio = []
                    for t in range(2):
                        ts = slice(t * P, t * P + P)
                        trio += [(banks[t].t[:, :], xh[k][:, ts], H), (banks[t].t[:, :], xh[k][:, ts], L),
                                 (banks[t].t[:, :], xl[k][:, ts], H)]
                for n, (o_, a_, b_) in enumerate(trio):
                    f = (lambda e, o_=o_, a_=a_, b_=b_, s_=(k == 0 and n % 3 == 0), p_=(k == kt - 1 and n % 3 == 2):
                         e.matmul(o_, a_, b_, start=s_, stop=p_))
                    if n == len(trio) - 1 and (final or k == kt - 1):
                        m = pe.mark(f)
                        if final:
                            m_used[c] = m
                    else:
                        pe.do(f)
            for f in aside:
                f(kt * w / 8)
            due.append([])
            for f in due.pop(0):
                f()
            return banks, m

        def split(src, hi, lo, ready, q=dve):
            act.wait(*ready)
            m1 = act.mark(lambda e: e.activation(hi, src, ACT.Copy))
            q.wait(m1, *ready)
            return q.mark(lambda e: e.tensor_tensor(lo, src, hi, ALU.subtract))

        sqm = [None] * 4
        accm = [None] * 2
        state.update(sq=0, acc=0, ln=0)
        lnm = [None] * 2

        def square(tile, marks, q):
            j = state["sq"] % 4
            state["sq"] += 1
            q.wait(sqm[j], *marks)
            if q is act:
                return j, act.mark(lambda e: e.activation(sq[:, j, :], tile, ACT.Square))
            return j, q.mark(lambda e: e.tensor_tensor(sq[:, j, :], tile, tile, ALU.mult))

        class Squares:

            def __init__(self, n):
                self.n, self.i, self.j, self.m = n, 0, state["acc"] % 2, None
                state["acc"] += 1

            def add(self, tile, marks):
                self.i += 1
                acc = sqa[:, self.j, :]
                if self.i == self.n:
                    j, m = square(tile, marks, act)
                    self.bank = b = xb.take()
                    pe.wait(*b.free, m_on)
                    if self.n > 1:
                        pe.wait(self.m)
                        accm[self.j] = pe.mark(lambda e: e.matmul(
                            b.t[:, 0:S], ones[:, :], acc, start=True, stop=False, skip_group_check=True))
                    pe.wait(m)
                    sqm[j] = self.m = pe.mark(lambda e: e.matmul(
                        b.t[:, 0:S], ones[:, :], sq[:, j, :], start=(self.n == 1), stop=True, skip_group_check=True))
                elif self.i == 1:
                    act.wait(accm[self.j], *marks)
                    self.m = act.mark(lambda e: e.activation(acc, tile, ACT.Square))
                else:
                    j, m = square(tile, marks, act)
                    pool.wait(m, self.m)
                    sqm[j] = self.m = pool.mark(lambda e: e.tensor_tensor(acc, acc, sq[:, j, :], ALU.add))

        def rstd(bank, n, cols, m):
            j = state["ln"] % 2
            state["ln"] += 1
            L = R = rst[:, j, 0:cols]
            act.wait(m, m_vc)
            if lnm[j] is not None:
                act.wait(*lnm[j])
            m1 = act.mark(lambda e: e.activation(L, bank.t[:, 0:cols], ACT.Ln, bias=vec("eps"), scale=1.0 / n))
            act.wait(m1)
            m2 = act.mark(lambda e: e.activation(R, L, ACT.Exp, scale=-0.5))
            give(bank, m1)
            return R, m2, j

        def log_tables():
            act.do(lambda e: e.preload_act_table_set("natural_log_exp_and_others"))

        def norm(src, nt, g, hi, lo, ready, sums=None):
            if sums is None:
                sums = Squares(nt)
                for i in range(nt):
                    sums.add(src[:, i, :], [ready[i % len(ready)]])
            R, mr, j = rstd(sums.bank, nt * P, S, sums.m)
            marks = []
            for i in range(nt):
                k = state["sq"] % 4
                state["sq"] += 1
                dve.wait(mr, sqm[k], m_vc, *ready)
                t = sq[:, k, :]
                m1 = dve.mark(lambda e: e.scalar_tensor_tensor(
                    out=t, in0=src[:, i, :], scalar=vec(g, i), in1=R, op0=ALU.mult, op1=ALU.mult))
                sqm[k] = m3 = split(t, hi[:, i, :], lo[:, i, :], [m1], pool if i % 2 else dve)
                marks.append(m3)
            lnm[j] = (m1,)
            return marks

        dve.wait(m_vc)
        m_hb = dve.mark(lambda e: e.tensor_scalar(hb[:, :], vc[:, V["gate_b"]:V["gate_b"] + 16], 0.5, None, ALU.mult))
        m_cw = dve.mark(lambda e: e.tensor_scalar(cw5[:, :], vc[:, V["conv_w"]:V["conv_w"] + 248], 0.5, None, ALU.mult))
        m_qg = dve.mark(lambda e: e.tensor_scalar(qg8[:, :], vec("qg"), 0.125, None, ALU.mult))

        def fence():
            return [q.last() for q in (pe, act, dve, pool)]

        def attention(c, heads, qk, vt, table, hi, lo, fill, ready, sS, sT, war=()):
            sP = sb(c, "sP", [P, 3, 384])
            mx = sb(c, "mx", [P, heads, 8])
            done, bank_s, bank_t, m_pt, m_st = {}, {}, {}, {}, {}
            m_nrm, m_exp, m_pv, m_ptc, m_tr = {}, {}, {}, {}, {}
            opair, m_max = {}, {}

            def scores(h):
                b = xb.take()
                pe.wait(*b.free, *ready)
                parts = qk(h)
                n = 2 * len(parts)
                i = 0
                for q, k, marks in parts:
                    pe.wait(*marks)
                    for (o, a, b_) in ((b.t[:, 0:S], q[:, P:S], k[:, 0:S]), (b.t[:, S:S + P], q[:, 0:P], k[:, 0:P])):
                        i += 1
                        f = (lambda e, o=o, a=a, b_=b_, s_=(i == 1), p_=(i >= n - 1):
                             e.matmul(o, a, b_, start=s_, stop=p_, skip_group_check=True))
                        if i == n:
                            m = pe.mark(f)
                        else:
                            pe.do(f)
                bank_s[h] = (b, m)

            def softmax(h):
                b, m = bank_s[h]
                T, mt, rel = table(h)
                j = h % 3
                dve.wait(m, mt, m_exp.get(h - 3))
                dve.mark(lambda e: e.tensor_tensor_reduce(
                    sS[:, j, 0:S], b.t[:, 0:S], T, 1.0, -3e38, ALU.add, ALU.max, mx[:, h, 0:1]))
                m1 = dve.mark(lambda e: e.tensor_tensor_reduce(
                    sS[:, j, S:384], b.t[:, S:384], T[:, P:S], 1.0, -3e38, ALU.add, ALU.max, mx[:, h, 1:2]))
                give(b, m1)
                rel(m1)
                dve.wait(m1)
                m2 = dve.mark(lambda e: e.tensor_scalar(mx[:, h, 2:4], mx[:, h, 0:2], -1.0, None, ALU.mult))
                m_max[h] = m2

            def exps(h):
                j = h % 3
                act.wait(m_max[h], m_nrm.get(h - 3), m_tr.get(h - 3))
                act.mark(lambda e: e.activation(sP[:, j, 0:S], sS[:, j, 0:S], ACT.Exp, bias=mx[:, h, 2:3],
                                                accum_out=mx[:, h, 4:5]))
                m_exp[h] = act.mark(lambda e: e.activation(sP[:, j, S:384], sS[:, j, S:384], ACT.Exp,
                                                           bias=mx[:, h, 3:4], accum_out=mx[:, h, 5:6]))

            def normalise(h):
                j = h % 3
                dve.wait(m_exp[h])
                m4 = dve.mark(lambda e: e.reciprocal(mx[:, h, 6:8], mx[:, h, 4:6]))
                dve.wait(m4)
                dve.mark(lambda e: e.tensor_scalar(sP[:, j, 0:S], sP[:, j, 0:S], mx[:, h, 6:7], None, ALU.mult))
                m_nrm[h] = dve.mark(lambda e: e.tensor_scalar(sP[:, j, S:384], sP[:, j, S:384], mx[:, h, 7:8], None,
                                                              ALU.mult))

            def turn(h):
                j, b = h % 3, xb.take()
                pe.wait(m_nrm[h], m_id, *b.free)
                pe.do(lambda e: e.transpose(b.t[:, 0:P], sP[:, j, S:384], ident[:, :]))
                pe.do(lambda e: e.transpose(b.t[:, P:S], sP[:, j, 0:P], ident[:, :]))
                m_tr[h] = m = pe.mark(lambda e: e.transpose(b.t[:, S:384], sP[:, j, P:S], ident[:, :]))
                act.wait(m, m_pv.get(h - 2), *war)
                m_ptc[h] = act.mark(lambda e: e.activation(sT[:, h % 2, :], b.t[:, 0:384], ACT.Copy))
                give(b, m_ptc[h])

            def values(h):
                j, o = h % 2, 64 * (h % 2)
                if h % 2 == 0:
                    opair[h // 2] = xb.take()
                b = opair[h // 2]
                pe.wait(m_ptc[h], *b.free)
                pe.do(lambda e: e.matmul(b.t[o:o + 64, 0:S], vt[:, 0, 64 * h:64 * h + 64], sT[:, j, 0:S],
                                         start=True, stop=False, skip_group_check=True))
                m_pv[h] = pe.mark(lambda e: e.matmul(b.t[o:o + 64, P:S], vt[:, 1, 64 * h:64 * h + 64],
                                                     sT[:, j, S:384], start=False, stop=True, skip_group_check=True))
                if h % 2:
                    i = h // 2
                    act.wait(m_pv[h])
                    m1 = act.mark(lambda e: e.activation(hi[:, i, :], b.t[:, 0:S], ACT.Copy))

                    def rest():
                        dve.wait(m1)
                        done[i] = dve.mark(lambda e: e.tensor_tensor(lo[:, i, :], b.t[:, 0:S], hi[:, i, :], ALU.subtract))
                        give(b, done[i])
                    pending.append(rest)

            pending = []
            for n in range(heads + 5):
                if n < heads:
                    scores(n)
                if 0 <= n - 1 < heads:
                    softmax(n - 1)
                if 0 <= n - 2 < heads:
                    exps(n - 2)
                if 0 <= n - 3 < heads:
                    normalise(n - 3)
                while pending:
                    pending.pop()()
                if 0 <= n - 5 < heads:
                    values(n - 5)
                fill(n)
                if 0 <= n - 4 < heads:
                    turn(n - 4)
            while pending:
                pending.pop()()
            return [done[i] for i in sorted(done)]

        def add_residual(i, banks, m, sums):
            dve.wait(m)
            r = dve.mark(lambda e, i=i: e.scalar_tensor_tensor(
                out=X[:, i, :], in0=banks[0].t[:, 0:S], scalar=0.5, in1=X[:, i, :], op0=ALU.mult, op1=ALU.add))
            give(banks[0], r)
            if i == KD - 2:
                log_tables()
            sums.add(X[:, i, :], [r])
            return r

        with ExitStack() as c:
            Q = sb(c, "Q", [P, KD, S])
            K = sb(c, "K", [P, KD, S])
            VT = sb(c, "VT", [P, 2, D])
            GA = sb(c, "GA", [P, KD, S])
            GB = sb(c, "GB", [P, KD, S])
            CI = sb(c, "CI", [P, KD, S + 30])
            CA = sb(c, "CA", [P, KD, S])
            ah = sb(c, "ah", [P, KD, S], F32R)
            al = sb(c, "al", [P, KD, S], F32R)
            sg = sb(c, "sg", [P, 3, S])
            tb = sb(c, "tb", [P, 3, S])
            ct = sb(c, "ct", [P, 4, S])

            m_h = norm(X, KD, "norm1_g", hh, hl, [m_x])
            H = [hh[:, i, :] for i in range(KD)]
            L = [hl[:, i, :] for i in range(KD)]
            m_z = pool.mark(lambda e: e.memset(CI[:, :, 0:30], 0.0))
            conv_m = {}
            sgm = [None] * 3

            def conv_dve(i):
                m = None
                for j in range(31):
                    a, w = CI[:, i, j:j + S], cw5[:, j * 8 + i:j * 8 + i + 1]
                    dve.wait(m_ci[i], m_z, m_cw, m)
                    if j == 0:
                        m = dve.mark(lambda e: e.tensor_scalar(CA[:, i, :], a, w, vec("conv_b", i), ALU.mult, ALU.add))
                    else:
                        m = dve.mark(lambda e: e.scalar_tensor_tensor(
                            out=CA[:, i, :], in0=a, scalar=w, in1=CA[:, i, :], op0=ALU.mult, op1=ALU.add))
                    yield
                conv_m[i] = m

            ctm = [None] * 4

            def conv_two(i):
                m = None
                for j in range(31):
                    a, w = CI[:, i, j:j + S], cw5[:, j * 8 + i:j * 8 + i + 1]
                    k = j % 4
                    act.wait(m_ci[i], m_z, m_cw)
                    if j == 0:
                        m = act.mark(lambda e: e.activation(CA[:, i, :], a, ACT.Identity, scale=w, bias=vec("conv_b", i)))
                    else:
                        act.wait(ctm[k])
                        m1 = act.mark(lambda e: e.activation(ct[:, k, :], a, ACT.Copy, scale=w))
                        pool.wait(m1, m)
                        ctm[k] = m = pool.mark(lambda e: e.tensor_tensor(CA[:, i, :], CA[:, i, :], ct[:, k, :], ALU.add))
                    yield
                conv_m[i] = m

            class Work:

                def __init__(self, side):
                    self.side, self.chains = side, []

                def some(self, n):
                    while n > 0 and self.chains:
                        for c in self.chains[:self.side]:
                            if next(c, 0) == 0:
                                self.chains.remove(c)
                            n -= 1

            w1, w2 = Work(2), Work(1)

            quota, owed = [4.0, 2.0], [0.0, 0.0]

            def conv_some(part):
                for n, w in enumerate((w1, w2)):
                    owed[n] += quota[n] * part
                    w.some(int(owed[n]))
                    owed[n] -= int(owed[n])

            aside.append(conv_some)
            m_ci = {}
            for i in range(KD):
                bg, m = job(("ag", i), H, L, m_h)
                act.wait(m, sgm[i % 3])
                m1 = act.mark(lambda e, i=i, b=bg[0].t: e.activation(sg[:, i % 3, :], b[:, 0:S], ACT.Tanh, scale=0.5))
                give(bg[0], m1)
                bv, m = job(("av", i), H, L, [])
                dve.wait(m1, m)
                sgm[i % 3] = m_ci[i] = dve.mark(lambda e, i=i, b=bv[0].t: e.scalar_tensor_tensor(
                    out=CI[:, i, 30:], in0=sg[:, i % 3, :], scalar=1.0, in1=b[:, 0:S], op0=ALU.add, op1=ALU.mult))
                give(bv[0], m_ci[i])
                if i in (1, 4, 6):
                    w2.chains.append(conv_two(i))
                else:
                    w1.chains.append(conv_dve(i))
            m_v = []
            for n in range(2):
                banks, m = job(("v", n), H, L, [])
                for t in range(2):
                    act.wait(m)
                    m1 = act.mark(lambda e, n=n, t=t, b=banks[t].t: e.activation(
                        VT[:, t, n * 512:n * 512 + 512], b[:, :], ACT.Copy))
                    give(banks[t], m1)
                    m_v.append(m1)
            quota[:] = [2.0, 1.5]
            log_tables()
            m_qk = {}

            def head_norm(which, i, buf, m):
                n, ms = square(buf[:, i, :], [m], pool)

                def sums():
                    b = xb.take()
                    pe.wait(ms, m_bd, *b.free)
                    m2 = sqm[n] = pe.mark(lambda e: e.matmul(b.t[:, 0:S], bd[:, :], sq[:, n, :], start=True, stop=True))
                    R, mr, j = rstd(b, 64, S, m2)

                    def scale():
                        g = qg8[:, 0:1] if which == "q" else vec("kg")
                        dve.wait(mr, m_qg)
                        r = dve.mark(lambda e: e.scalar_tensor_tensor(
                            out=buf[:, i, :], in0=buf[:, i, :], scalar=g, in1=R, op0=ALU.mult, op1=ALU.mult))
                        lnm[j] = (r,)
                        m_qk[which, i] = r
                    later(0, scale)
                later(1, sums)

            for i in range(KD):
                for which, buf in (("q", Q), ("k", K)):
                    banks, m = job((which, i), H, L, [])
                    act.wait(m)
                    m1 = act.mark(lambda e, i=i, buf=buf, b=banks[0].t: e.activation(buf[:, i, :], b[:, 0:S], ACT.Copy))
                    give(banks[0], m1)
                    head_norm(which, i, buf, m1)

            settle()
            m_gate = {}

            def gate_job(n):
                if n >= 16:
                    return
                banks, m = job(("g", n), H, L, [])
                G = GA if n < 8 else GB
                act.wait(m, m_hb)
                m_gate[n] = act.mark(lambda e, b=banks[0].t: e.activation(
                    G[:, n % 8, :], b[:, 0:S], ACT.Tanh, scale=0.5, bias=hb[:, n:n + 1]))
                give(banks[0], m_gate[n])

            s_tb = [sem(f"s_tb{i}") for i in range(3)]
            tbm = {h: dma(sp, s_tb[h], tb[:, h, :], tabs[h], 1) for h in range(3)}

            def table1(h):
                def rel(mm):
                    if h + 3 < NH:
                        sp.wait(mm)
                        tbm[h + 3] = dma(sp, s_tb[h % 3], tb[:, h % 3, :], tabs[h + 3], (h + 3) // 3 + 1)
                return tb[:, h % 3, :], tbm[h], rel

            def qk1(h):
                o, j = 64 * (h % 2), h // 2
                return [(Q[o:o + 64, j, :], K[o:o + 64, j, :], [m_qk["q", j], m_qk["k", j]])]

            oh, ol = ah, al
            m_o = attention(c, NH, qk1, VT, table1, oh, ol, gate_job, m_v, sb(c, "sS", [P, 3, 384]), sb(c, "sT", [P, 2, 384]))

            w1.some(1000)
            w2.some(1000)
            aside.clear()
            gates_done = pe.last()
            log_tables()
            cs = Squares(KD)
            for i in (0, 2, 1, 4, 3, 5, 6, 7):
                cs.add(CA[:, i, :], [conv_m[i]])
            R, mr, j = rstd(cs.bank, D, S, cs.m)
            m_c = {}

            def silu(i):
                k = i % 3
                dve.wait(mr, conv_m[i])
                m1 = dve.mark(lambda e: e.scalar_tensor_tensor(
                    out=CA[:, i, :], in0=CA[:, i, :], scalar=vec("conv_norm_g", i), in1=R, op0=ALU.mult, op1=ALU.mult))
                lnm[j] = (m1,)
                act.wait(m1, sgm[k], m_ci[KD - 1])
                m2 = act.mark(lambda e: e.activation(sg[:, k, :], CA[:, i, :], ACT.Tanh, scale=0.5))
                dve.wait(m2)
                sgm[k] = m3 = dve.mark(lambda e: e.scalar_tensor_tensor(
                    out=CA[:, i, :], in0=sg[:, k, :], scalar=1.0, in1=CA[:, i, :], op0=ALU.add, op1=ALU.mult))
                act.wait(gates_done)
                q = pool if i % 2 else dve
                q.wait(gates_done)
                m_c[i] = split(CA[:, i, :], hh[:, i, :], hl[:, i, :], [m3], q)

            OH = [oh[:, i, :] for i in range(KD)]
            OL = [ol[:, i, :] for i in range(KD)]
            m_yb = {}
            for i in range(KD):
                banks, m = job(("ao", i), OH, OL, m_o)
                dve.wait(m, m_gate[8 + i])
                m_yb[i] = dve.mark(lambda e: e.scalar_tensor_tensor(
                    out=GB[:, i, :], in0=GB[:, i, :], scalar=1.0, in1=banks[0].t[:, 0:S], op0=ALU.add, op1=ALU.mult))
                give(banks[0], m_yb[i])
                for n in (2 * i, 2 * i + 1):
                    if n < KD:
                        silu(n)
            ao_done = pe.last()
            m_mix = []
            for i in range(KD):
                banks, m = job(("co", i), H, L, [m_c[n] for n in range(KD)])
                dve.wait(m, m_gate[i])
                m1 = dve.mark(lambda e: e.scalar_tensor_tensor(
                    out=GA[:, i, :], in0=GA[:, i, :], scalar=1.0, in1=banks[0].t[:, 0:S], op0=ALU.add, op1=ALU.mult))
                give(banks[0], m1)
                dve.wait(m1, m_yb[i])
                m2 = dve.mark(lambda e: e.scalar_tensor_tensor(
                    out=GA[:, i, :], in0=GA[:, i, :], scalar=0.5, in1=GB[:, i, :], op0=ALU.mult, op1=ALU.add))
                act.wait(ao_done)
                pool.wait(ao_done)
                m_mix.append(split(GA[:, i, :], oh[:, i, :], ol[:, i, :], [m2], pool))
            m_xr, sums = [], Squares(KD)
            for i in range(KD):
                banks, m = job(("wo", i), OH, OL, m_mix)
                m_xr.append(add_residual(i, banks, m, sums))
            wall = fence()

        def ffn(keys_g, keys_u, keys_d, with_conv, m_xr, wall, sums, g):
            with ExitStack() as c:
                fh = sb(c, "fh", [P, FT, S], F32R)
                fl = sb(c, "fl", [P, FT, S], F32R)
                ug = sb(c, "ug", [P, 3, S])
                uv = sb(c, "uv", [P, 3, S])
                tt = sb(c, "tt", [P, 3, S])
                m_h = norm(X, KD, g, hh, hl, m_xr, sums)
                act.wait(*wall)
                dve.wait(*wall)
                pool.wait(*wall)
                m_f = []
                fr = {}

                def conv3(key, i, row, buf, free):
                    banks, m = job(key, H, L, m_h)
                    b = banks[0].t
                    act.wait(m, free)
                    w = [vec("ffn_conv_w", j * 44 + row) for j in range(3)]
                    m1 = act.mark(lambda e: e.activation(buf, b[:, 0:S], ACT.Identity, scale=w[2], bias=vec("ffn_conv_b", row)))
                    dve.wait(m1)
                    m2 = dve.mark(lambda e: e.scalar_tensor_tensor(
                        out=buf[:, 1:S], in0=b[:, 0:S - 1], scalar=w[1], in1=buf[:, 1:S], op0=ALU.mult, op1=ALU.add))
                    dve.wait(m2)
                    m3 = dve.mark(lambda e: e.scalar_tensor_tensor(
                        out=buf[:, 2:S], in0=b[:, 0:S - 2], scalar=w[0], in1=buf[:, 2:S], op0=ALU.mult, op1=ALU.add))
                    give(banks[0], m3)
                    return m3

                def plain(key, i, row, buf, free):
                    banks, m = job(key, H, L, m_h)
                    act.wait(m, free)
                    m1 = act.mark(lambda e: e.activation(buf, banks[0].t[:, 0:S], ACT.Copy))
                    give(banks[0], m1)
                    return m1

                one = conv3 if with_conv else plain

                def finish(i, mg, mv):
                    j = i % 3
                    act.wait(mg, fr.get(("t", i - 3)))
                    mt = act.mark(lambda e: e.activation(tt[:, j, :], ug[:, j, :], ACT.Tanh, scale=0.5))
                    pool.wait(mg, mv)
                    mp = fr["g", i] = pool.mark(lambda e: e.tensor_tensor(uv[:, j, :], uv[:, j, :], ug[:, j, :], ALU.mult))

                    def gated():
                        dve.wait(mp, mt)
                        ms = fr["v", i] = dve.mark(lambda e: e.scalar_tensor_tensor(
                            out=tt[:, j, :], in0=tt[:, j, :], scalar=1.0, in1=uv[:, j, :], op0=ALU.add, op1=ALU.mult))
                        act.wait(ms)
                        m1 = act.mark(lambda e: e.activation(fh[:, i, :], tt[:, j, :], ACT.Copy))

                        def rest():
                            dve.wait(m1)
                            r = fr["t", i] = dve.mark(lambda e: e.tensor_tensor(
                                fl[:, i, :], tt[:, j, :], fh[:, i, :], ALU.subtract))
                            m_f.append(r)
                        later(0, rest)
                    later(0, gated)

                for i in range(FT):
                    mg = one((keys_g, i), i, 22 + i, ug[:, i % 3, :], fr.get(("g", i - 3)))
                    mv = one((keys_u, i), 1, i, uv[:, i % 3, :], fr.get(("v", i - 3)))
                    finish(i, mg, mv)
                settle()
                FH = [fh[:, i, :] for i in range(FT)]
                FL = [fl[:, i, :] for i in range(FT)]
                m_x2, sums = [], Squares(KD)
                for i in range(KD):
                    banks, m = job((keys_d, i), FH, FL, m_f)
                    m_x2.append(add_residual(i, banks, m, sums))
                return m_x2, fence(), sums

        m_x2, wall, sums = ffn("ug", "uv", "dn", True, m_xr, wall, sums, "norm2_g")

        with ExitStack() as c:
            qn = sb(c, "qn", [P, 4, S])
            qr = sb(c, "qr", [P, 2, S])
            kn = sb(c, "kn", [P, 4, S])
            krp = sb(c, "krp", [P, S])
            cc = sb(c, "cc", [P, 5, S])
            ch = sb(c, "ch", [P, 5, S], F32R)
            cl = sb(c, "cl", [P, 5, S], F32R)
            mv_ = sb(c, "mv_", [P, 2, 512])
            gv = sb(c, "gv", [P, 2, 512])
            GA = sb(c, "GA2", [P, KD, S])
            GB = sb(c, "GB2", [P, KD, S])
            gq = sb(c, "gq", [P, 2, S])
            gk = sb(c, "gk", [P, 2, S])
            og = sb(c, "og", [P, 4, S])
            glr = sb(c, "glr", [P, S])
            bc = sb(c, "bc", [P, 2, S])
            eb = sb(c, "eb", [P, 2, 2 * S])
            qL = sb(c, "qL", [P, 2, S])
            kL = sb(c, "kL", [P, 2, S])
            at = sb(c, "at", [P, 2, 512])
            tmp = sb(c, "tmp", [P, 2, 512])
            kd = sb(c, "kd", [P, 2, S])
            st = sb(c, "st", [P, 3, 2, P])
            ebl = sb(c, "ebl", [P, 2, 4])
            go_ = sb(c, "go_", [P, 4, S])
            msk = sb(c, "msk", [P, 7, P])
            cm = tmp[:, 0, :]
            ah = sb(c, "ah2", [P, 4, S], F32R)
            al = sb(c, "al2", [P, 4, S], F32R)
            posi = at[:, 0, 0:S].bitcast(I32)

            m_h = norm(X, KD, "ln_mix_2", hh, hl, m_x2, sums)
            act.wait(*wall)
            dve.wait(*wall)
            pool.wait(*wall)
            s_m = [sem("s_m0"), sem("s_m1")]
            act.wait(*wall)
            m_msk = dma(act, s_m[0], msk[:, :, :], masks.rearrange("p (l i) -> p l i", l=7), 1)
            m_pos = dma(act, s_m[1], posi, pos, 1)
            m_cm0 = pool.mark(lambda e: e.memset(cm, 1.0))
            pool.wait(m_cm0)
            m_cm = pool.mark(lambda e: e.memset(cm.rearrange("p (a b) -> p a b", b=64)[:, :, 0:1], 0.0))

            ang, kf, r0, r1 = eb[:, 0, 0:S], eb[:, 0, S:2 * S], eb[:, 1, 0:S], eb[:, 1, S:2 * S]

            def step(f, *w):
                dve.wait(*w)
                return dve.mark(f)

            a = step(lambda e: e.tensor_copy(r0, posi), m_pos)
            a = step(lambda e: e.tensor_scalar(ang, r0, vec("inv"), None, ALU.mult), a)
            a = step(lambda e: e.tensor_scalar(kf, ang, 1.0 / TWO_PI, MAGIC, ALU.mult, ALU.add), a)
            a = step(lambda e: e.tensor_scalar(kf, kf, MAGIC, None, ALU.subtract), a)
            for cst in (C1, C2, C3):
                a = step(lambda e, cst=cst: e.scalar_tensor_tensor(
                    out=ang, in0=kf, scalar=-cst, in1=ang, op0=ALU.mult, op1=ALU.add), a)
            a = step(lambda e: e.tensor_scalar(r0, ang, PI_F, -PI_F, ALU.min, ALU.max), a)
            a2 = step(lambda e: e.tensor_scalar(kf, ang, float(np.pi / 2), -TWO_PI, ALU.is_gt, ALU.mult), a)
            a2 = step(lambda e: e.scalar_tensor_tensor(out=r1, in0=kf, scalar=float(np.pi / 2), in1=ang,
                                                       op0=ALU.add, op1=ALU.add), a2)
            a2 = step(lambda e: e.tensor_scalar(r1, r1, PI_F, -PI_F, ALU.min, ALU.max), a2)
            act.wait(a2)
            act.mark(lambda e: e.activation(rope[:, 1, :], r0, ACT.Sin))
            a3 = act.mark(lambda e: e.activation(rope[:, 0, :], r1, ACT.Sin))
            a4 = step(lambda e: e.tensor_scalar(rope[:, 1, :], rope[:, 1, :], vec("sgn"), None, ALU.mult), a3)
            m_rope = step(lambda e: e.tensor_scalar(rope[:, 2:4, :], rope[:, 0:2, :], 96.0 ** -0.5, None, ALU.mult), a4)

            def copy_out(key, xh, xl, ready, dst, scale=1.0, extra=()):
                banks, m = job(key, xh, xl, ready)
                act.wait(m, *extra)
                m1 = act.mark(lambda e: e.activation(dst, banks[0].t[:, 0:S], ACT.Copy, scale=scale))
                give(banks[0], m1)
                return m1

            m_cc = []
            for i in range(3):
                m_cc.append(copy_out(("cq", i), H, L, m_h, cc[:, i, :]))
            for i in range(2):
                m_cc.append(copy_out(("ckv", i), H, L, [], cc[:, 3 + i, :]))

            def roped(k1, k2, xh, xl, ready, dst, cs, sn, n):
                b1, m1 = job(k1, xh, xl, ready)
                dve.wait(m1, m_rope)
                d1 = dve.mark(lambda e: e.tensor_tensor(dst, b1[0].t[:, 0:S], cs, ALU.mult))
                give(b1[0], d1)
                b2, m2 = job(k2, xh, xl, [])
                dve.wait(m2, rfree.get(n))
                d2 = dve.mark(lambda e: e.tensor_tensor(glr2[:, n, :], b2[0].t[:, 0:S], sn, ALU.mult))
                give(b2[0], d2)
                dve.wait(d1, d2)
                d3 = dve.mark(lambda e: e.tensor_tensor(dst, dst, glr2[:, n, :], ALU.add))
                rfree[n] = d3
                return d3

            rfree = {}
            glr2 = qL
            m_kr = roped(("kr", 0), ("krs", 0), H, L, [], krp[:, :], rope[:, 0, :], rope[:, 1, :], 0)
            m_glr = copy_out(("glr", 0), H, L, [], glr[:, :])
            m_nq = norm(cc[:, 0:3, :], 3, "mla_norm_cq_2", ch[:, 0:3, :], cl[:, 0:3, :], m_cc[0:3])
            m_gq = [copy_out(("gq", i), H, L, [], gq[:, i, :], 0.125) for i in range(2)]
            m_nk = norm(cc[:, 3:5, :], 2, "mla_norm_ckv_2", ch[:, 3:5, :], cl[:, 3:5, :], m_cc[3:5])
            m_gk = [copy_out(("gk", i), H, L, [], gk[:, i, :]) for i in range(2)]
            banks, m = job(("gv", 0), H, L, [])
            m_gv = []
            for t in range(2):
                act.wait(m)
                m1 = act.mark(lambda e, t=t, b=banks[t].t: e.activation(gv[:, t, :], b[:, :], ACT.Copy))
                give(banks[t], m1)
                m_gv.append(m1)
            CH = [ch[:, i, :] for i in range(5)]
            CL = [cl[:, i, :] for i in range(5)]
            m_q, m_k, m_qr = {}, {}, {}
            for i in range(4):
                m_q[i] = copy_out(("qn", i), CH[0:3], CL[0:3], m_nq, qn[:, i, :], 96.0 ** -0.5)
            for i in range(2):
                m_qr[i] = roped(("qr", i), ("qrs", i), CH[0:3], CL[0:3], [], qr[:, i, :], rope[:, 2, :], rope[:, 3, :], 1)
            for i in range(4):
                m_k[i] = copy_out(("kn", i), CH[3:5], CL[3:5], m_nk, kn[:, i, :])
            banks, m = job(("mv", 0), CH[3:5], CL[3:5], [])
            m_mv = []
            for t in range(2):
                act.wait(m)
                m1 = act.mark(lambda e, t=t, b=banks[t].t: e.activation(mv_[:, t, :], b[:, :], ACT.Copy))
                give(banks[t], m1)
                m_mv.append(m1)

            gx, ge = eb[:, 0, :], eb[:, 1, :]
            b = xb.take()
            pe.wait(m_glr, m_wg2, *b.free)
            pe.do(lambda e: e.matmul(b.t[:, 0:S], wg2[:, 0:P], glr[0:16, :], start=True, stop=True, skip_group_check=True))
            m = pe.mark(lambda e: e.matmul(b.t[:, S:2 * S], wg2[:, P:2 * P], glr[0:16, :], start=False, stop=True,
                                           skip_group_check=True))
            dve.wait(m, a3)
            for i in range(2):
                g1 = dve.mark(lambda e, i=i: e.tensor_scalar(gx[:, i * S:i * S + S], b.t[:, i * S:i * S + S],
                                                             vec("gla_b_gate_2", i), None, ALU.add))
            give(b, g1)
            act.wait(g1)
            g2 = act.mark(lambda e: e.activation(ge, gx, ACT.Abs))
            act.wait(g2)
            g3 = act.mark(lambda e: e.activation(ge, ge, ACT.Exp, scale=-1.0))
            act.wait(g3)
            g4 = act.mark(lambda e: e.activation(ge, ge, ACT.Ln, bias=vec("one")))
            g5 = step(lambda e: e.scalar_tensor_tensor(out=gx, in0=gx, scalar=0.0, in1=ge, op0=ALU.min, op1=ALU.subtract), g4)
            bcf = bc[:, :, :].rearrange("p a s -> p (a s)")
            m_bc = step(lambda e: e.tensor_tensor_scan(bcf, cm, gx, 0.0, ALU.mult, ALU.add), g5, m_cm)
            gqf = gq[:, :, :].rearrange("p a s -> p (a s)")
            gkf = gk[:, :, :].rearrange("p a s -> p (a s)")
            qLf = qL[:, :, :].rearrange("p a s -> p (a s)")
            kLf = kL[:, :, :].rearrange("p a s -> p (a s)")
            kdf = kd[:, :, :].rearrange("p a s -> p (a s)")
            gst = {"pe": [], "e": {0: [m_bc], 1: [m_bc]}, "acc": {}, "tmp": {}}

            def pair_products(q_, k_, ready):
                bs = [xb.take(), xb.take()]
                pe.wait(*ready, *bs[0].free, *bs[1].free)
                for par in range(2):
                    o = 64 * par
                    for n in range(4):
                        p_, t = n // 2, n % 2
                        f = (lambda e, n=n, o=o, p_=p_, t=t, b=bs[par].t: e.matmul(
                            b[:, n * P:n * P + P], k_[o:o + 64, p_, t * P:t * P + P], q_[o:o + 64, p_, t * P:t * P + P],
                            start=(n == 0), stop=True, skip_group_check=True))
                        if n == 3:
                            m = pe.mark(f)
                        else:
                            pe.do(f)
                return bs, m

            def level(n):
                s = LEVELS[n]
                if s == 0:
                    bs, m = pair_products(gq, gk, m_gq + m_gk)
                else:
                    E = eb[:, n % 2, :]
                    bv = bcf.rearrange("p (n w) -> p n w", w=2 * s)
                    Ev = E.rearrange("p (n w) -> p n w", w=2 * s)
                    ref = bv[:, :, s - 1:s].to_broadcast([P, 512 // (2 * s), 2 * s])
                    l1 = step(lambda e: e.tensor_tensor(Ev, bv, ref, ALU.subtract), m_bc, *gst["e"][n % 2])
                    act.wait(l1)
                    l2 = act.mark(lambda e: e.activation(E, E, ACT.Abs))
                    act.wait(l2)
                    l3 = act.mark(lambda e: e.activation(E, E, ACT.Exp, scale=-1.0 / 16))
                    pool.wait(l3, m_gk[1], *gst["pe"])
                    l5 = pool.mark(lambda e: e.tensor_tensor(kLf, gkf, E, ALU.mult))
                    l4 = step(lambda e: e.tensor_tensor(qLf, gqf, E, ALU.mult), l3, m_gq[1], *rfree.values(), *gst["pe"])
                    gst["e"][n % 2] = [l4, l5]
                    bs, m = pair_products(qL, kL, [l4, l5])
                    gst["pe"] = [m]
                gst["b"] = (n, bs, m)

            def level_add():
                n, bs, m = gst["b"]
                mb = msk[:, n:n + 1, :].to_broadcast([P, 4, P])
                for par in range(2):
                    bt = bs[par].t[:, :].rearrange("p (a i) -> p a i", a=4)
                    if n == 0:
                        g = step(lambda e: e.tensor_tensor(at[:, par, :].rearrange("p (a i) -> p a i", a=4), bt, mb,
                                                           ALU.mult), m, m_msk)
                        gst["acc"][par] = g
                    else:
                        g = step(lambda e: e.tensor_tensor(tmp[:, par, :].rearrange("p (a i) -> p a i", a=4), bt, mb,
                                                           ALU.mult), m, m_msk, gst["tmp"].get(par))
                        pool.wait(g, gst["acc"][par])
                        gst["acc"][par] = gst["tmp"][par] = pool.mark(lambda e: e.tensor_tensor(
                            at[:, par, :], at[:, par, :], tmp[:, par, :], ALU.add))
                    give(bs[par], g)

            def decays():
                E, E2 = eb[:, 0, :], eb[:, 1, :]
                bv = bcf.rearrange("p (n w) -> p n w", w=64)
                Ev = E.rearrange("p (n w) -> p n w", w=64)
                last = bv[:, :, 63:64]
                l1 = step(lambda e: e.tensor_tensor(Ev, bv, last.to_broadcast([P, 8, 64]), ALU.subtract), m_bc, *gst["e"][0])
                act.wait(l1)
                l2 = act.mark(lambda e: e.activation(E, E, ACT.Exp, scale=-1.0 / 16))
                l3 = step(lambda e: e.tensor_tensor(kLf, gkf, E, ALU.mult), l2, *gst["pe"])
                b = xb.take()
                pe.wait(l3, m_id, *b.free)
                for t in range(2):
                    for p_ in range(2):
                        f = lambda e, t=t, p_=p_: e.transpose(b.t[:, t * S + p_ * P:t * S + p_ * P + P],
                                                              kL[:, p_, t * P:t * P + P], ident[:, :])
                        m = pe.mark(f)
                act.wait(m)
                l4 = act.mark(lambda e: e.activation(kdf, b.t[:, :], ACT.Copy))
                give(b, l4)
                act.wait(*gst["e"][1])
                l5 = act.mark(lambda e: e.activation(E2, bcf, ACT.Exp, scale=1.0 / 16))
                act.mark(lambda e: e.activation(ebl[:, :, :].rearrange("p a c -> p (a c)"),
                                                last.rearrange("p n w -> p (n w)"), ACT.Exp, scale=1.0 / 16))
                l6 = act.last()
                l7 = step(lambda e: e.tensor_tensor(qLf, gqf, E2, ALU.mult), l5, *gst["pe"])
                prev = None
                for ci in range(3):
                    o, t = 64 * (ci % 2), ci // 2
                    b = xb.take()
                    pe.wait(l4, *m_gv, *b.free)
                    for p_ in range(2):
                        f = lambda e, p_=p_, o=o, t=t, b=b: e.matmul(
                            b.t[:, p_ * S:p_ * S + S], kd[o:o + 64, t, p_ * P:p_ * P + P],
                            gv[o:o + 64, t, p_ * S:p_ * S + S], start=(p_ == 0), stop=True, skip_group_check=True)
                        m = pe.mark(f)
                    for p_ in range(2):
                        for hf in range(2):
                            r = slice(64 * hf, 64 * hf + 64)
                            U = b.t[r, p_ * S + hf * P:p_ * S + hf * P + P]
                            if ci == 0:
                                g = step(lambda e, r=r, p_=p_, U=U: e.tensor_copy(st[r, 0, p_, :], U), m)
                            else:
                                g = step(lambda e, r=r, p_=p_, U=U, ci=ci: e.scalar_tensor_tensor(
                                    out=st[r, ci, p_, :], in0=st[r, ci - 1, p_, :], scalar=ebl[r, p_, ci:ci + 1], in1=U,
                                    op0=ALU.mult, op1=ALU.add), m, l6, prev)
                    prev = g
                    give(b, g)
                gst["st"] = (prev, l7)

            def gla_out():
                prev, l7 = gst["st"]
                bs = [xb.take(), xb.take()]
                pe.wait(prev, l7, gst["acc"][0], gst["acc"][1], *m_gv, *bs[0].free, *bs[1].free)
                marks = []
                for par in range(2):
                    b, o = bs[par].t, 64 * par
                    for p_ in range(2):
                        h = 2 * p_ + par
                        for t in range(2):
                            pe.do(lambda e, b=b, p_=p_, t=t, h=h, par=par: e.matmul(
                                b[:, p_ * S + t * P:p_ * S + t * P + P], gv[:, t, h * P:h * P + P],
                                at[:, par, (2 * p_ + t) * P:(2 * p_ + t) * P + P],
                                start=(p_ == 0 and t == 0), stop=False, skip_group_check=True))
                    for p_ in range(2):
                        for ci in range(1, 4):
                            f = (lambda e, b=b, p_=p_, o=o, ci=ci: e.matmul(
                                b[:, p_ * S + ci * 64:p_ * S + ci * 64 + 64], st[o:o + 64, ci - 1, p_, :],
                                qL[o:o + 64, p_, ci * 64:ci * 64 + 64], start=False, stop=True, skip_group_check=True))
                            m = pe.mark(f)
                    for p_ in range(2):
                        h = 2 * p_ + par
                        act.wait(m)
                        marks.append((h, act.mark(lambda e, b=b, h=h, p_=p_: e.activation(
                            go_[:, h, :], b[:, p_ * S:p_ * S + S], ACT.Copy))))
                    give(bs[par], marks[-1][1])
                gst["o"] = dict(marks)

            def gla_norm():
                for pr in range(2):
                    b = xb.take()
                    for n in range(2):
                        h = 2 * pr + n
                        q_, ms = square(go_[:, h, :], [gst["o"][h]], pool)
                        pe.wait(ms, m_on, *b.free)
                        m = sqm[q_] = pe.mark(lambda e: e.matmul(b.t[:, n * S:n * S + S], ones[:, :], sq[:, q_, :],
                                                                 start=(n == 0), stop=True, skip_group_check=True))
                    R, mr, j = rstd(b, P, 512, m)
                    for n in range(2):
                        h = 2 * pr + n
                        g1 = step(lambda e, h=h, n=n: e.scalar_tensor_tensor(
                            out=go_[:, h, :], in0=go_[:, h, :], scalar=vec("gla_norm_2"), in1=R[:, n * S:n * S + S],
                            op0=ALU.mult, op1=ALU.mult), mr)
                        g2 = step(lambda e, h=h: e.tensor_tensor(go_[:, h, :], go_[:, h, :], og[:, h, :], ALU.mult), g1, m_og[h])
                        act.wait(*uq_done)
                        dve.wait(*uq_done)
                        m_g.append(split(go_[:, h, :], ch[:, h, :], cl[:, h, :], [g2]))
                    lnm[j] = (g1,)

            m_og, m_g = {}, []
            uq_done = [pe.last()]
            level(0)
            for i in range(4):
                banks, m = job(("og", i), H, L, [])
                b = banks[0].t
                act.wait(m)
                m1 = act.mark(lambda e, i=i, b=b: e.activation(og[:, i, :], b[:, 0:S], ACT.Tanh, scale=0.5))
                dve.wait(m1)
                m2 = dve.mark(lambda e, i=i, b=b: e.scalar_tensor_tensor(
                    out=og[:, i, :], in0=og[:, i, :], scalar=1.0, in1=b[:, 0:S], op0=ALU.add, op1=ALU.mult))
                give(banks[0], m2)
                m_og[i] = step(lambda e, i=i: e.tensor_scalar(og[:, i, :], og[:, i, :], 0.5, None, ALU.mult), m2)
                level_add() if i == 0 else None
            m_gate = {}

            def gate2(n):
                banks, m = job(("g2", n), H, L, [])
                G = GA if n < 8 else GB
                act.wait(m)
                m_gate[n] = act.mark(lambda e, b=banks[0].t: e.activation(G[:, n % 8, :], b[:, 0:S], ACT.Tanh, scale=0.5))
                give(banks[0], m_gate[n])

            gate_n = [0]

            def some_gates(k):
                for _ in range(k):
                    if gate_n[0] < 16:
                        gate2(gate_n[0])
                        gate_n[0] += 1

            for n in range(1, 7):
                level(n)
                some_gates(1)
                level_add()
            decays()
            some_gates(1)
            gla_out()
            some_gates(1)
            gla_norm()

            def table2(h):
                return caus[:, :], m_caus, lambda mm: None

            def qk2(h):
                o, j, o2, j2 = 64 * (h % 2), h // 2, 32 * (h % 4), h // 4
                return [(qn[o:o + 64, j, :], kn[o:o + 64, j, :], [m_q[j], m_k[j]]),
                        (qr[o2:o2 + 32, j2, :], krp[o2:o2 + 32, :], [m_qr[j2], m_kr])]

            m_o = attention(c, MH, qk2, mv_, table2, ah, al, lambda n: some_gates(1), m_mv,
                            cc[:, :, :].rearrange("p a s -> p (a s)")[:, 0:1152].rearrange("p (a s) -> p a s", a=3),
                            eb[:, :, :].rearrange("p a s -> p (a s)")[:, 0:768].rearrange("p (a s) -> p a s", a=2),
                            [gst["st"][1]])
            some_gates(16)
            m_ya, m_mix = {}, []
            OH, OL = [ah[:, i, :] for i in range(4)], [al[:, i, :] for i in range(4)]
            for i in range(KD):
                banks, m = job(("mo", i), OH, OL, m_o)
                m_ya[i] = step(lambda e, i=i, b=banks[0].t: e.scalar_tensor_tensor(
                    out=GA[:, i, :], in0=GA[:, i, :], scalar=1.0, in1=b[:, 0:S], op0=ALU.add, op1=ALU.mult), m, m_gate[i])
                give(banks[0], m_ya[i])
            h_done = pe.last()
            for i in range(KD):
                banks, m = job(("go", i), CH[0:4], CL[0:4], m_g)
                m1 = step(lambda e, i=i, b=banks[0].t: e.scalar_tensor_tensor(
                    out=GB[:, i, :], in0=GB[:, i, :], scalar=1.0, in1=b[:, 0:S], op0=ALU.add, op1=ALU.mult), m, m_gate[8 + i])
                give(banks[0], m1)
                m2 = step(lambda e, i=i: e.tensor_tensor(GA[:, i, :], GA[:, i, :], GB[:, i, :], ALU.add), m1, m_ya[i])
                act.wait(h_done)
                dve.wait(h_done)
                m_mix.append(split(GA[:, i, :], hh[:, i, :], hl[:, i, :], [m2]))
            m_xr, sums = [], Squares(KD)
            for i in range(KD):
                banks, m = job(("wo2", i), H, L, m_mix)
                m_xr.append(add_residual(i, banks, m, sums))
            wall = fence()

        m_x4, wall, sums = ffn("fg", "fu", "fd", False, m_xr, wall, sums, "ln_ffn_2")

        R, mr, j = rstd(sums.bank, D, S, sums.m)
        s_o = sem("s_o")
        outv = out.rearrange("p (k s) -> p k s", k=KD)
        for i in range(KD):
            dve.wait(mr)
            m1 = dve.mark(lambda e, i=i: e.scalar_tensor_tensor(
                out=X[:, i, :], in0=X[:, i, :], scalar=vec("final_norm_2", i), in1=R, op0=ALU.mult, op1=ALU.mult))
            if i % 2:
                sp.wait(m1)
                mo = dma(sp, s_o, outv[:, i - 1:i + 1, :], X[:, i - 1:i + 1, :], i // 2 + 1)
        sp.wait(mo)

    with ExitStack() as outer:
        block = outer.enter_context(nc.Block())

        @block.tensor
        def _(e):
            walk(e, "s_pe")

        @block.scalar
        def _(e):
            walk(e, "s_act")

        @block.vector
        def _(e):
            walk(e, "s_dve")

        @block.gpsimd
        def _(e):
            walk(e, "s_pool")

        @block.sync
        def _(e):
            walk(e, "s_sp")


def shape_constants():
    p = np.arange(P)[:, None]
    d = P + p - np.arange(S)[None, :]
    count = ((d >= 0) & (d <= 128)).astype(np.float64) + ((d >= 0) & (d % 4 == 0)) + ((d >= 0) & (d % 16 == 0))
    lc = np.where(count > 0, np.log(np.maximum(count, 1)), NEG)
    tabs = np.empty((NH + 1, P, S), np.float32)
    for h in range(NH):
        slope = 2.0 ** (-8.0 * (h + 1) / NH)
        tabs[h] = np.where(count > 0, lc - slope * d, NEG)
    tabs[NH] = np.where(d >= 0, 0.0, NEG)
    j, i = np.arange(P)[:, None], np.arange(P)[None, :]
    ms = np.zeros((P, 7, P), np.float32)
    for n, s in enumerate(LEVELS):
        if s == 0:
            ms[:, n] = j == i
        else:
            ms[:, n] = (j // (2 * s) == i // (2 * s)) & (j % (2 * s) < s) & (i % (2 * s) >= s)
    half = np.arange(16, dtype=np.float32) / np.float32(16)
    inv = (np.float32(1.0) / (np.float32(10000.0) ** half)).astype(np.float32)
    q = np.arange(P)
    return tabs, ms.reshape(P, 7 * P), inv[q % 16], np.where(q % 32 < 16, -1.0, 1.0).astype(np.float32)


def kernel(**inputs):
    import concourse.bacc as bacc
    from concourse.bass_utils import run_bass_kernel_spmd

    a = {k: np.ascontiguousarray(v) for k, v in inputs.items()}
    placed, n_chunks = place_jobs()
    ws = np.zeros((n_chunks, P, CW), np.float32)
    for _, name, cols, kt, at in placed:
        w = a[name][0]
        n = len(cols)
        for k in range(kt):
            b = at + k * (n // P)
            o = b % CB * P
            ws[b // CB, :, o:o + n] = w[k * P:(k + 1) * P][:, cols]
    tabs, ms, inv, sgn = shape_constants()
    V, NV = vec_at()
    vecs = np.zeros((P, NV), np.float32)

    def put(name, rows):
        vecs[:, V[name]:V[name] + rows.shape[0]] = rows.T

    for name in ("norm1_g", "gate_b", "conv_b", "conv_norm_g", "norm2_g", "ffn_conv_b", "ln_mix_2", "mla_norm_cq_2",
                 "mla_norm_ckv_2", "gla_b_gate_2", "gla_norm_2", "ln_ffn_2", "final_norm_2", "conv_w", "ffn_conv_w"):
        put(name, a[name].reshape(-1, P))
    put("qg", np.concatenate([a["q_norm_g"][0]] * 2)[None])
    put("kg", np.concatenate([a["k_norm_g"][0]] * 2)[None])
    put("inv", inv[None])
    put("sgn", sgn[None])
    put("eps", np.full((1, P), EPS, np.float32))
    put("one", np.ones((1, P), np.float32))
    xs = np.ascontiguousarray(a["x"][0].T.reshape(KD, P, S).transpose(1, 0, 2).reshape(P, KD * S))
    feed = {
        "ws": ws, "xs": xs, "vecs": vecs,
        "pos": np.ascontiguousarray(np.broadcast_to(a["positions_2"].reshape(1, S), (P, S))),
        "wgate": a["gla_w_gate2_2"][0], "tabs": tabs, "lmask": ms,
    }
    nc = bacc.Bacc("TRN2", target_bir_lowering=False, num_devices=1)
    args = [nc.dram_tensor(n, v.shape, mybir.dt.from_np(v.dtype), kind="ExternalInput").ap() for n, v in feed.items()]
    out = nc.dram_tensor("out", (P, KD * S), F32, kind="ExternalOutput").ap()
    two_blocks(nc, args[0], args[1], args[2], args[3], args[4], args[5], args[6], out)
    r = run_bass_kernel_spmd(nc, [feed], core_ids=[0])
    y = r.results[0]["out"]
    return np.ascontiguousarray(y.reshape(P, KD, S).transpose(2, 1, 0).reshape(1, S, D))
```

```python
from contextlib import ExitStack

import numpy as np

import concourse.bass as bass
from concourse import mybir

F32 = mybir.dt.float32
F32R = mybir.dt.float32r
I32 = mybir.dt.int32
ALU = mybir.AluOpType
ACT = mybir.ActivationFunctionType
AX = mybir.AxisListType

P = 128
S = 256
D = 1024
KD = D // P
FT = 22
NH = 16
MH = 8
CB = 8
CW = CB * P
NRAW = 4
NSL = 5
AHEAD = 3
NB = 5
NSQ = 6
QK0 = 5
FIRST = 4
EARLY = 1
PACE = 1.1
PACE2 = 1.0
POOL_END = 64
POOL_EACH = 4
EPS = 1e-6
NEG = -1e30
TWO_PI = 2.0 * np.pi
C1 = 6.28125
C2 = float(np.float32(np.round((TWO_PI - C1) * 2 ** 19) / 2 ** 19))
C3 = float(np.float32(TWO_PI - C1 - C2))
PI_F = 3.1415925
MAGIC = 12582912.0
LEVELS = (0, 32, 16, 8, 4, 2, 1)


def rng(a, n=P):
    return list(range(a, a + n))


def stream_jobs():
    jobs = []

    def add(key, name, cols, kt):
        jobs.append((key, name, cols, kt))

    for i in range(KD):
        add(("ag", i), "w_in", rng(1024 + i * P), KD)
        add(("av", i), "w_in", rng(i * P), KD)
    for n in range(2):
        add(("v", n), "w_in", rng(4096 + n * 512, 512), KD)
    for i in range(KD):
        add(("q", i), "w_in", rng(2048 + i * P), KD)
        add(("k", i), "w_in", rng(3072 + i * P), KD)
    for i in range(16):
        add(("g", i), "w_in", rng(5120 + i * P), KD)
    for i in range(KD):
        add(("ao", i), "w_attn_out", rng(i * P), KD)
    for i in range(KD):
        add(("co", i), "w_conv_out", rng(i * P), KD)
    for i in range(KD):
        add(("wo", i), "w_out", rng(i * P), KD)
    for i in range(FT):
        add(("ug", i), "w_up", rng(2816 + i * P), KD)
        add(("uv", i), "w_up", rng(i * P), KD)
    for i in range(KD):
        add(("dn", i), "w_down", rng(i * P), FT)
    kr = 640
    for i in range(3):
        add(("cq", i), "w_in_2", rng(i * P), KD)
    for i in range(2):
        add(("ckv", i), "w_in_2", rng(384 + i * P), KD)
    add(("kr", 0), "w_in_2", rng(kr, 32) + rng(kr + 16, 16) + rng(kr, 16) + rng(1696, 16) * 4, KD)
    for i in range(2):
        add(("gq", i), "w_in_2", rng(672 + i * P), KD)
    for i in range(2):
        add(("gk", i), "w_in_2", rng(928 + i * P), KD)
    add(("gv", 0), "w_in_2", rng(1184, 512), KD)
    for i in range(4):
        add(("qn", i), "mla_w_uq_2", rng(192 * i, 64) + rng(192 * i + 96, 64), 3)
    for i in range(2):
        add(("qr", i), "mla_w_uq_2", sum((rng(96 * (4 * i + h) + 64, 32) for h in range(4)), []), 3)
        add(("qrs", i), "mla_w_uq_2",
            sum((rng(96 * (4 * i + h) + 80, 16) + rng(96 * (4 * i + h) + 64, 16) for h in range(4)), []), 3)
    for i in range(4):
        add(("kn", i), "mla_w_ukv_2", rng(256 * i, 64) + rng(256 * i + 128, 64), 2)
    add(("mv", 0), "mla_w_ukv_2", sum((rng(128 * h + 64, 64) for h in range(MH)), []), 2)
    for i in range(4):
        add(("og", i), "w_in_2", rng(1712 + i * P), KD)
    for i in range(16):
        add(("g2", i), "w_in_2", rng(2224 + i * P), KD)
    for i in range(KD):
        add(("go", i), "gla_w_o_2", rng(i * P), 4)
    for i in range(KD):
        add(("mo", i), "mla_w_o_2", rng(i * P), 4)
    for i in range(KD):
        add(("wo2", i), "w_out_2", rng(i * P), KD)
    for i in range(FT):
        add(("fg", i), "ffn_w_gate_2", rng(i * P), KD)
        add(("fu", i), "ffn_w_up_2", rng(i * P), KD)
    for i in range(KD):
        add(("fd", i), "ffn_w_down_2", rng(i * P), FT)
    return jobs


def place_jobs():
    at, out = 0, []
    for key, name, cols, kt in stream_jobs():
        w = len(cols) // P
        at += -at % w
        out.append((key, name, cols, kt, at))
        at += kt * w
    return out, -(-at // CB)


VECS = [("norm1_g", 8), ("gate_b", 16), ("conv_b", 8), ("conv_norm_g", 8), ("qg", 1), ("kg", 1),
        ("norm2_g", 8), ("ffn_conv_b", 44), ("ln_mix_2", 8), ("mla_norm_cq_2", 3), ("mla_norm_ckv_2", 2),
        ("gla_b_gate_2", 2), ("gla_norm_2", 1), ("ln_ffn_2", 8), ("final_norm_2", 8),
        ("conv_w", 31 * 8), ("ffn_conv_w", 3 * 44), ("inv", 1), ("sgn", 1), ("eps", 1), ("one", 1), ("sel", P)]


def vec_at():
    at, out = 0, {}
    for n, w in VECS:
        out[n] = at
        at += w
    return out, at


class Queue:

    def __init__(self, eng, sem, serial=False):
        self.eng, self.sem, self.n, self.seen, self.serial = eng, sem, 0, {}, serial

    def wait(self, *marks):
        for m in marks:
            if m is None:
                continue
            sem, v, i = m
            if self.seen.get(i, 0) < v:
                self.seen[i] = v
                if self.eng is not None:
                    self.eng.wait_ge(sem, v)

    def do(self, f):
        if self.eng is not None:
            f(self.eng)

    def mark(self, f):
        if self.serial:
            self.wait(self.last())
        self.n += 1
        if self.eng is not None:
            f(self.eng).then_inc(self.sem, 1)
        return self.last()

    def last(self):
        return (self.sem, self.n, self.sem.name) if self.n else None

    def dma(self, s, dst, src, n):
        if self.eng is not None:
            self.eng.dma_start(dst, src).then_inc(s, 16)
        return (s, 16 * n, s.name)


class Bank:
    def __init__(self, t):
        self.t, self.free, self.home = t, [], None


class Banks:

    def __init__(self, ts):
        self.idle = [Bank(t) for t in ts]
        for b in self.idle:
            b.home = self

    def take(self):
        return self.idle.pop(0)


def give(bank, *marks):
    assert bank not in bank.home.idle
    bank.free = list(marks)
    bank.home.idle.append(bank)


def two_blocks(nc, ws, x, vecs, pos, w_gate2, tabs, masks, out):
    V, NV = vec_at()
    placed, n_chunks = place_jobs()
    where = {key: (kt, at, len(cols) // P) for key, _, cols, kt, at in placed}

    made = {}

    def walk(block_engine, who):
        used = set()
        ctx = ExitStack() if made else outer

        def once(name, make):
            while name in used:
                name += "_"
            used.add(name)
            if name not in made:
                made[name] = make(name)
            return made[name]

        def sem(name):
            return once(name, lambda n: outer.enter_context(nc.semaphore(n)))

        def sb(c, name, shape, dt=F32):
            return once(name, lambda n: c.enter_context(nc.sbuf_tensor(n, shape, dt)))

        def psum(name):
            return once(name, lambda n: outer.enter_context(nc.psum_tensor(n, [P, 512], F32)))

        def queue(name, serial=False):
            return Queue(block_engine if who == name else None, sem(name), serial)

        pe, act, dve, pool, sp = queue("s_pe"), queue("s_act"), queue("s_dve"), queue("s_pool", True), queue("s_sp")

        def dma(q, s, dst, src, n):
            return q.dma(s, dst, src, n)

        xb = Banks([psum(f"px{i}") for i in range(8)])

        raw = sb(ctx, "raw", [P, NRAW, CW])
        whi = sb(ctx, "whi", [P, NSL, CW], F32R)
        wlo = sb(ctx, "wlo", [P, NSL, CW], F32R)
        X = sb(ctx, "X", [P, KD, S])
        hh = sb(ctx, "hh", [P, KD, S], F32R)
        hl = sb(ctx, "hl", [P, KD, S], F32R)
        vc = sb(ctx, "vc", [P, NV])
        hb = sb(ctx, "hb", [P, 16])
        cw5 = sb(ctx, "cw5", [P, 31 * 8])
        qg8 = sb(ctx, "qg8", [P, 1])
        cg5 = sb(ctx, "cg5", [P, 8])
        ones = sb(ctx, "ones", [P, P])
        bd = sb(ctx, "bd", [P, P])
        ident = sb(ctx, "ident", [P, P])
        rope = sb(ctx, "rope", [P, 4, S])
        wg2 = sb(ctx, "wg2", [80, S])
        caus = sb(ctx, "caus", [P, S])
        rst = sb(ctx, "rst", [P, 2, 512])
        sq = sb(ctx, "sq", [P, NSQ, S])
        sqa = sb(ctx, "sqa", [P, 2, S])

        def log_tables():
            act.do(lambda e: e.preload_act_table_set("natural_log_exp_and_others"))

        def vec(name, i=0):
            return vc[:, V[name] + i:V[name] + i + 1]

        log_tables()
        s_c = [sem(f"s_c{i}") for i in range(6)]
        xv = x.rearrange("p (k s) -> p k s", k=KD)
        m_x0 = dma(act, s_c[0], X[:, 0:4, :], xv[:, 0:4, :], 1)
        m_x1 = dma(sp, s_c[4], X[:, 4:8, :], xv[:, 4:8, :], 1)
        m_vc = dma(act, s_c[1], vc[:, :], vecs, 1)
        m_on = pool.mark(lambda e: e.memset(ones[:, :], 1.0))
        m_b0 = pool.mark(lambda e: e.memset(bd[:, :], 0.0))
        m_i0 = pool.mark(lambda e: e.memset(ident[:, :], 0.0))
        pool.wait(m_b0)
        pool.mark(lambda e: e.memset(bd[0:64, 0:64], 1.0))
        m_bd = pool.mark(lambda e: e.memset(bd[64:128, 64:128], 1.0))
        pool.wait(m_i0)
        m_id = pool.mark(lambda e: e.affine_select(out=ident[:, :], in_=ident[:, :], compare_op=ALU.not_equal,
                                                   fill=1.0, base=0, pattern=[[-1, P]], channel_multiplier=1))

        s_raw = [sem(f"s_raw{i}") for i in range(NRAW)]
        m_raw, m_hi, m_lo, m_used = {}, {}, {}, {}
        state = {"load": 0, "high": 0, "low": 0}

        def load():
            c = state["load"]
            if c >= n_chunks:
                return
            if c >= NRAW:
                sp.wait(m_hi[c - NRAW], m_lo[c - NRAW])
            m_raw[c] = dma(sp, s_raw[c % NRAW], raw[:, c % NRAW, :], ws[c], c // NRAW + 1)
            state["load"] += 1

        def high():
            c = state["high"]
            state["high"] += 1
            r, h = c % NRAW, c % NSL
            act.wait(m_raw[c])
            if c >= NSL:
                act.wait(m_used[c - NSL], m_lo[c - NSL])
            m_hi[c] = act.mark(lambda e: e.activation(whi[:, h, :], raw[:, r, :], ACT.Copy))

        def low():
            c = state["low"]
            state["low"] += 1
            r, h = c % NRAW, c % NSL
            q = pool if c < POOL_END and c % POOL_EACH == POOL_EACH - 1 else dve
            q.wait(m_hi[c], m_raw[c])
            if c >= NSL:
                q.wait(m_used[c - NSL])
            m_lo[c] = q.mark(lambda e: e.tensor_tensor(wlo[:, h, :], raw[:, r, :], whi[:, h, :], ALU.subtract))
            load()

        for _ in range(NRAW):
            load()

        ends, aside, due = {}, [], [[] for _ in range(4)]

        def later(n, f):
            due[n].append(f)

        def settle():
            for d in due:
                while d:
                    d.pop(0)()

        for key, (kt, at, w) in where.items():
            for b in range(at, at + kt * w, w):
                ends[b // CB] = (key, b)

        def job(key, xh, xl, ready, taken=None):
            kt, at, w = where[key]
            banks = [xb.take() for _ in range(1 if w == 1 else 2)]
            for b in banks:
                pe.wait(*b.free)
            if len(ready) != kt:
                pe.wait(*ready)
            for k in range(kt):
                if len(ready) == kt:
                    pe.wait(ready[k])
                blk = at + k * w
                c, o = blk // CB, blk % CB * P
                while state["low"] <= min(c + min(AHEAD, 1 + blk // 4), n_chunks - 1):
                    while state["high"] <= min(state["low"] + 1, n_chunks - 1):
                        high()
                    low()
                pe.wait(m_hi[c], m_lo[c])
                h = c % NSL
                H, L = whi[:, h, o:o + w * P], wlo[:, h, o:o + w * P]
                final = ends[c] == (key, blk)
                if w == 1:
                    trio = [(banks[0].t[:, 0:S], H, xh[k]), (banks[0].t[:, 0:S], H, xl[k]), (banks[0].t[:, 0:S], L, xh[k])]
                else:
                    trio = []
                    for t in range(2):
                        ts = slice(t * P, t * P + P)
                        trio += [(banks[t].t[:, :], xh[k][:, ts], H), (banks[t].t[:, :], xh[k][:, ts], L),
                                 (banks[t].t[:, :], xl[k][:, ts], H)]
                for n, (o_, a_, b_) in enumerate(trio):
                    f = (lambda e, o_=o_, a_=a_, b_=b_, s_=(k == 0 and n % 3 == 0), p_=(k == kt - 1 and n % 3 == 2):
                         e.matmul(o_, a_, b_, start=s_, stop=p_))
                    if n == len(trio) - 1 and (final or k == kt - 1 or taken is not None):
                        m = pe.mark(f)
                        if taken is not None:
                            taken.append(m)
                        if final:
                            m_used[c] = m
                    else:
                        pe.do(f)
                if (k + 1) * w % CB == 0 or k == kt - 1:
                    for f in aside:
                        f(((k * w % CB) + w) / CB)
            due.append([])
            for f in due.pop(0):
                f()
            return banks, m

        def split(src, hi, lo, ready, q=dve):
            act.wait(*ready)
            m1 = act.mark(lambda e: e.activation(hi, src, ACT.Copy))
            q.wait(m1, *ready)
            return q.mark(lambda e: e.tensor_tensor(lo, src, hi, ALU.subtract))

        sqm = [None] * NSQ
        accm = [None] * 2
        state.update(sq=0, acc=0, ln=0)
        lnm = [None] * 2

        def square(tile, marks, q):
            j = state["sq"] % NSQ
            state["sq"] += 1
            q.wait(sqm[j], *marks)
            if q is act:
                return j, act.mark(lambda e: e.activation(sq[:, j, :], tile, ACT.Square))
            return j, q.mark(lambda e: e.tensor_tensor(sq[:, j, :], tile, tile, ALU.mult))

        class Squares:

            def __init__(self, n, adder=pool, hold=False):
                self.adder, self.hold = adder, hold
                self.n, self.i, self.j, self.m = n, 0, state["acc"] % 2, None
                state["acc"] += 1

            def add(self, tile, marks):
                self.i += 1
                acc = sqa[:, self.j, :]
                if self.i == self.n:
                    self.tail = square(tile, marks, act)
                    if not self.hold:
                        self.end()
                elif self.i == 1:
                    act.wait(accm[self.j], *marks)
                    self.m = act.mark(lambda e: e.activation(acc, tile, ACT.Square))
                else:
                    j, m = square(tile, marks, act)
                    self.adder.wait(m, self.m)
                    sqm[j] = self.m = self.adder.mark(lambda e: e.tensor_tensor(acc, acc, sq[:, j, :], ALU.add))

            def end(self):
                j, m = self.tail
                self.bank = b = xb.take()
                pe.wait(*b.free, m_on)
                if self.n > 1:
                    pe.wait(self.m)
                    accm[self.j] = pe.mark(lambda e: e.matmul(
                        b.t[:, 0:S], ones[:, :], sqa[:, self.j, :], start=True, stop=False, skip_group_check=True))
                pe.wait(m)
                sqm[j] = self.m = pe.mark(lambda e: e.matmul(
                    b.t[:, 0:S], ones[:, :], sq[:, j, :], start=(self.n == 1), stop=True, skip_group_check=True))

        def rstd(bank, n, cols, m, exact_ln=False):
            j = state["ln"] % 2
            state["ln"] += 1
            L = R = rst[:, j, 0:cols]
            if exact_ln:
                act.do(lambda e: e.preload_act_table_set("natural_log"))
            act.wait(m, m_vc)
            if lnm[j] is not None:
                act.wait(*lnm[j])
            m1 = act.mark(lambda e: e.activation(L, bank.t[:, 0:cols], ACT.Ln, bias=vec("eps"), scale=1.0 / n))
            act.wait(m1)
            m2 = act.mark(lambda e: e.activation(R, L, ACT.Exp, scale=-0.5))
            give(bank, m1)
            return R, m2, j

        def norm(src, nt, g, hi, lo, ready, sums=None, exact_ln=False):
            if sums is None:
                sums = Squares(nt)
                for i in range(nt):
                    sums.add(src[:, i, :], [ready[i % len(ready)]])
            R, mr, j = rstd(sums.bank, nt * P, S, sums.m, exact_ln)
            marks = []

            def low_part(i, k, mh):
                q = pool if i % 2 else dve
                q.wait(mh)
                sqm[k] = q.mark(lambda e: e.tensor_tensor(lo[:, i, :], sq[:, k, :], hi[:, i, :], ALU.subtract))
                marks.append(sqm[k])

            prev = None
            for i in range(nt):
                k = state["sq"] % NSQ
                state["sq"] += 1
                dve.wait(mr, sqm[k], m_vc, *ready)
                m1 = dve.mark(lambda e, i=i, k=k: e.scalar_tensor_tensor(
                    out=sq[:, k, :], in0=src[:, i, :], scalar=vec(g, i), in1=R, op0=ALU.mult, op1=ALU.mult))
                act.wait(m1, *ready)
                mh = act.mark(lambda e, i=i, k=k: e.activation(hi[:, i, :], sq[:, k, :], ACT.Copy))
                if prev:
                    low_part(*prev)
                prev = (i, k, mh)
            low_part(*prev)
            lnm[j] = (m1,)
            return marks

        def fence():
            return [q.last() for q in (pe, act, dve, pool)]

        def attention(c, heads, qk, vt, table, hi, lo, fill, ready, sS, sT, sP, war=()):
            mx = sb(c, "mx", [P, heads, 8])
            done, bank_s, bank_t, m_pt, m_st = {}, {}, {}, {}, {}
            m_nrm, m_exp, m_pv, m_ptc, m_tr = {}, {}, {}, {}, {}
            opair, m_max = {}, {}

            def scores(h):
                b = xb.take()
                pe.wait(*b.free, *ready)
                parts = qk(h)
                n = 2 * len(parts)
                i = 0
                for q, k, marks in parts:
                    pe.wait(*marks)
                    for (o, a, b_) in ((b.t[:, 0:S], q[:, P:S], k[:, 0:S]), (b.t[:, S:S + P], q[:, 0:P], k[:, 0:P])):
                        i += 1
                        f = (lambda e, o=o, a=a, b_=b_, s_=(i == 1), p_=(i >= n - 1):
                             e.matmul(o, a, b_, start=s_, stop=p_, skip_group_check=True))
                        if i == n:
                            m = pe.mark(f)
                        else:
                            pe.do(f)
                bank_s[h] = (b, m)

            def softmax(h):
                b, m = bank_s[h]
                T, mt, rel = table(h)
                j = h % 3
                dve.wait(m, mt, m_exp.get(h - 3))
                dve.mark(lambda e: e.tensor_tensor_reduce(
                    sS[:, j, 0:S], b.t[:, 0:S], T, 1.0, -3e38, ALU.add, ALU.max, mx[:, h, 0:1]))
                m1 = dve.mark(lambda e: e.tensor_tensor_reduce(
                    sS[:, j, S:384], b.t[:, S:384], T[:, P:S], 1.0, -3e38, ALU.add, ALU.max, mx[:, h, 1:2]))
                give(b, m1)
                rel(m1)
                dve.wait(m1)
                m2 = dve.mark(lambda e: e.tensor_scalar(mx[:, h, 2:4], mx[:, h, 0:2], -1.0, None, ALU.mult))
                m_max[h] = m2

            def exps(h):
                j = h % 3
                act.wait(m_max[h], m_nrm.get(h - 3), m_tr.get(h - 3))
                act.mark(lambda e: e.activation(sP[:, j, 0:S], sS[:, j, 0:S], ACT.Exp, bias=mx[:, h, 2:3],
                                                accum_out=mx[:, h, 4:5]))
                m_exp[h] = act.mark(lambda e: e.activation(sP[:, j, S:384], sS[:, j, S:384], ACT.Exp,
                                                           bias=mx[:, h, 3:4], accum_out=mx[:, h, 5:6]))

            def normalise(h):
                j = h % 3
                dve.wait(m_exp[h])
                m4 = dve.mark(lambda e: e.reciprocal(mx[:, h, 6:8], mx[:, h, 4:6]))
                dve.wait(m4)
                dve.mark(lambda e: e.tensor_scalar(sP[:, j, 0:S], sP[:, j, 0:S], mx[:, h, 6:7], None, ALU.mult))
                m_nrm[h] = dve.mark(lambda e: e.tensor_scalar(sP[:, j, S:384], sP[:, j, S:384], mx[:, h, 7:8], None,
                                                              ALU.mult))

            def turn(h):
                j, b = h % 3, xb.take()
                pe.wait(m_nrm[h], m_id, *b.free)
                pe.do(lambda e: e.transpose(b.t[:, 0:P], sP[:, j, S:384], ident[:, :]))
                pe.do(lambda e: e.transpose(b.t[:, P:S], sP[:, j, 0:P], ident[:, :]))
                m_tr[h] = m = pe.mark(lambda e: e.transpose(b.t[:, S:384], sP[:, j, P:S], ident[:, :]))
                act.wait(m, m_pv.get(h - 2), *war)
                m_ptc[h] = act.mark(lambda e: e.activation(sT[:, h % 2, :], b.t[:, 0:384], ACT.Copy))
                give(b, m_ptc[h])

            def values(h):
                j, o = h % 2, 64 * (h % 2)
                if h % 2 == 0:
                    opair[h // 2] = xb.take()
                b = opair[h // 2]
                pe.wait(m_ptc[h], *b.free)
                pe.do(lambda e: e.matmul(b.t[o:o + 64, 0:S], vt[:, 0, 64 * h:64 * h + 64], sT[:, j, 0:S],
                                         start=True, stop=False, skip_group_check=True))
                m_pv[h] = pe.mark(lambda e: e.matmul(b.t[o:o + 64, P:S], vt[:, 1, 64 * h:64 * h + 64],
                                                     sT[:, j, S:384], start=False, stop=True, skip_group_check=True))
                if h % 2:
                    i = h // 2
                    act.wait(m_pv[h])
                    m1 = act.mark(lambda e: e.activation(hi[:, i, :], b.t[:, 0:S], ACT.Copy))

                    def rest():
                        dve.wait(m1)
                        done[i] = dve.mark(lambda e: e.tensor_tensor(lo[:, i, :], b.t[:, 0:S], hi[:, i, :], ALU.subtract))
                        give(b, done[i])
                    pending.append(rest)

            pending = []
            for n in range(heads + 5):
                if n < heads:
                    scores(n)
                if 0 <= n - 1 < heads:
                    softmax(n - 1)
                if 0 <= n - 2 < heads:
                    exps(n - 2)
                if 0 <= n - 3 < heads:
                    normalise(n - 3)
                while pending:
                    pending.pop()()
                fill(n)
                if 0 <= n - 5 < heads:
                    values(n - 5)
                if 0 <= n - 4 < heads:
                    turn(n - 4)
            while pending:
                pending.pop()()
            return [done[i] for i in sorted(done)]

        H = [hh[:, i, :] for i in range(KD)]
        L = [hl[:, i, :] for i in range(KD)]

        def add_residual(i, banks, m, sums, g=None, free=None, xg=None):
            dve.wait(m)
            r = dve.mark(lambda e, i=i: e.scalar_tensor_tensor(
                out=X[:, i, :], in0=banks[0].t[:, 0:S], scalar=0.5, in1=X[:, i, :], op0=ALU.mult, op1=ALU.add))
            give(banks[0], r)
            if i == KD - 2:
                log_tables()
            if g:
                act.wait(r, free)
                mh = act.mark(lambda e: e.activation(hh[:, i, :], X[:, i, :], ACT.Copy, scale=vec(g, i)))

                def low_part():
                    dve.wait(mh, free)
                    xg[i] = dve.mark(lambda e: e.scalar_tensor_tensor(
                        out=hl[:, i, :], in0=X[:, i, :], scalar=vec(g, i), in1=hh[:, i, :], op0=ALU.mult,
                        op1=ALU.subtract))
                sums.add(X[:, i, :], [r])
                if i < KD - 1:
                    later(0, low_part)
                else:
                    low_part()
            else:
                sums.add(X[:, i, :], [r])
            return r

        def first_jobs(keys, g, xg, m_x, sums, evac, early):
            taken, marks, slot, held = [], [], {}, []

            def scaled_tile(i):
                k = slot[i] = state["sq"] % NSQ
                state["sq"] += 1
                dve.wait(mr, sqm[k], m_x[i])
                lnm[j] = (dve.mark(lambda e: e.scalar_tensor_tensor(
                    out=sq[:, k, :], in0=X[:, i, :], scalar=vec(g, i), in1=R, op0=ALU.mult, op1=ALU.mult)),)
                slot[i] = (k, lnm[j][0])

            for n, key in enumerate(keys):
                final = n == len(keys) - 1
                banks, m = job(key, H, L, [xg[i] for i in range(KD)] if n == 0 else [], taken if final else None)
                if n == 0:
                    sums.end()
                    R, mr, j = rstd(sums.bank, D, S, sums.m)
                if n == 0:
                    for i in range(4):
                        scaled_tile(i)
                elif n == 1:
                    for i in range(4, NSQ):
                        scaled_tile(i)
                held.append((n, banks, m))
                if n < early:
                    evac(*held.pop(), R, mr)
            last = None

            def low_part(i, k, mh):
                q = pool if i % 2 else dve
                q.wait(mh, taken[i])
                sqm[k] = q.mark(lambda e: e.tensor_tensor(hl[:, i, :], sq[:, k, :], hh[:, i, :], ALU.subtract))
                marks.append(sqm[k])
                if i + NSQ < KD:
                    scaled_tile(i + NSQ)

            for i in range(KD):
                k, mt = slot[i]
                act.wait(mt, taken[i])
                mh = act.mark(lambda e, i=i, k=k: e.activation(hh[:, i, :], sq[:, k, :], ACT.Copy))
                if last:
                    low_part(*last)
                last = (i, k, mh)
            low_part(*last)
            for h in held:
                evac(*h, R, mr)
            return marks

        with ExitStack() as c:
            Q = sb(c, "Q", [P, KD, S])
            K = sb(c, "K", [P, KD, S])
            VT = sb(c, "VT", [P, 2, D])
            GA = sb(c, "GA", [P, KD, S])
            GB = sb(c, "GB", [P, KD, S])
            CI = sb(c, "CI", [P, KD, S + 30])
            CA = sb(c, "CA", [P, KD, S])
            ah = sb(c, "ah", [P, KD, S], F32R)
            al = sb(c, "al", [P, KD, S], F32R)
            sg = sb(c, "sg", [P, 3, S])
            tb = sb(c, "tb", [P, 3, S])
            ct = sb(c, "ct", [P, 4, S])

            sums = Squares(KD, dve)
            for i in range(KD):
                sums.add(X[:, i, :], [m_x0 if i < 4 else m_x1])
            for _ in range(2):
                high()
                low()

            dve.wait(m_vc)
            m_hb = dve.mark(lambda e: e.tensor_scalar(hb[:, :], vc[:, V["gate_b"]:V["gate_b"] + 16], 0.5, None, ALU.mult))
            m_cw = dve.mark(lambda e: e.tensor_scalar(cw5[:, :], vc[:, V["conv_w"]:V["conv_w"] + 248], 0.5, None, ALU.mult))
            m_cg = dve.mark(lambda e: e.tensor_scalar(cg5[:, :], vc[:, V["conv_norm_g"]:V["conv_norm_g"] + 8], 0.5, None,
                                                      ALU.mult))
            m_qg = dve.mark(lambda e: e.tensor_scalar(qg8[:, :], vec("qg"), 0.125, None, ALU.mult))

            m_h = norm(X, KD, "norm1_g", hh, hl, [m_x1], sums)
            m_z = pool.mark(lambda e: e.memset(CI[:, :, 0:30], 0.0))
            conv_m = {}
            sgm = [None] * 3
            cs = Squares(KD)

            def conv_ready(i, m):
                conv_m[i] = m
                if len(conv_m) < KD:
                    later(1, lambda: cs.add(CA[:, i, :], [m]))

            def conv_dve(i):
                m = None
                for j in range(31):
                    a, w = CI[:, i, j:j + S], cw5[:, j * 8 + i:j * 8 + i + 1]
                    dve.wait(m_ci[i], m_z, m_cw, m)
                    if j == 0:
                        m = dve.mark(lambda e: e.tensor_scalar(CA[:, i, :], a, w, vec("conv_b", i), ALU.mult, ALU.add))
                    else:
                        m = dve.mark(lambda e: e.scalar_tensor_tensor(
                            out=CA[:, i, :], in0=a, scalar=w, in1=CA[:, i, :], op0=ALU.mult, op1=ALU.add))
                    if j < 30:
                        yield
                conv_ready(i, m)
                yield

            ctm = [None] * 4

            def conv_two(i):
                m = None
                for j in range(31):
                    a, w = CI[:, i, j:j + S], cw5[:, j * 8 + i:j * 8 + i + 1]
                    k = j % 4
                    act.wait(m_ci[i], m_z, m_cw)
                    if j == 0:
                        m = act.mark(lambda e: e.activation(CA[:, i, :], a, ACT.Identity, scale=w, bias=vec("conv_b", i)))
                    else:
                        act.wait(ctm[k])
                        m1 = act.mark(lambda e: e.activation(ct[:, k, :], a, ACT.Copy, scale=w))
                        pool.wait(m1, m)
                        ctm[k] = m = pool.mark(lambda e: e.tensor_tensor(CA[:, i, :], CA[:, i, :], ct[:, k, :], ALU.add))
                    if j < 30:
                        yield
                conv_ready(i, m)
                yield

            class Work:

                def __init__(self, side):
                    self.side, self.chains = side, []

                def some(self, n):
                    while n > 0 and self.chains:
                        for c in self.chains[:self.side]:
                            if next(c, 0) == 0:
                                self.chains.remove(c)
                            n -= 1

            w1, w2 = Work(2), Work(1)

            quota, owed = [4.0, 2.0], [0.0, 0.0]

            def conv_some(part):
                for n, w in enumerate((w1, w2)):
                    owed[n] += quota[n] * part
                    w.some(int(owed[n]))
                    owed[n] -= int(owed[n])

            aside.append(conv_some)
            m_ci = {}
            for i in range(KD):
                bg, m = job(("ag", i), H, L, m_h)
                act.wait(m, sgm[i % 3])
                m1 = act.mark(lambda e, i=i, b=bg[0].t: e.activation(sg[:, i % 3, :], b[:, 0:S], ACT.Tanh, scale=0.5))
                give(bg[0], m1)
                bv, m = job(("av", i), H, L, [])
                dve.wait(m1, m)
                sgm[i % 3] = m_ci[i] = dve.mark(lambda e, i=i, b=bv[0].t: e.scalar_tensor_tensor(
                    out=CI[:, i, 30:], in0=sg[:, i % 3, :], scalar=1.0, in1=b[:, 0:S], op0=ALU.add, op1=ALU.mult))
                give(bv[0], m_ci[i])
                if i in (1, 4, 6):
                    w2.chains.append(conv_two(i))
                else:
                    w1.chains.append(conv_dve(i))
            m_v = []
            for n in range(2):
                banks, m = job(("v", n), H, L, [])
                for t in range(2):
                    act.wait(m)
                    m1 = act.mark(lambda e, n=n, t=t, b=banks[t].t: e.activation(
                        VT[:, t, n * 512:n * 512 + 512], b[:, :], ACT.Copy))
                    give(banks[t], m1)
                    m_v.append(m1)
            quota[:] = [2.3, 1.7]
            log_tables()
            m_qk = {}

            def head_norm(which, i, buf, m):
                n, ms = square(buf[:, i, :], [m], pool)

                def sums():
                    b = xb.take()
                    pe.wait(ms, m_bd, *b.free)
                    m2 = sqm[n] = pe.mark(lambda e: e.matmul(b.t[:, 0:S], bd[:, :], sq[:, n, :], start=True, stop=True))
                    R, mr, j = rstd(b, 64, S, m2)

                    def scale():
                        g = qg8[:, 0:1] if which == "q" else vec("kg")
                        dve.wait(mr, m_qg)
                        r = dve.mark(lambda e: e.scalar_tensor_tensor(
                            out=buf[:, i, :], in0=buf[:, i, :], scalar=g, in1=R, op0=ALU.mult, op1=ALU.mult))
                        lnm[j] = (r,)
                        m_qk[which, i] = r
                    later(0, scale)
                later(1, sums)

            def qk_job(which, i):
                buf = Q if which == "q" else K
                banks, m = job((which, i), H, L, [])
                act.wait(m)
                m1 = act.mark(lambda e: e.activation(buf[:, i, :], banks[0].t[:, 0:S], ACT.Copy))
                give(banks[0], m1)
                head_norm(which, i, buf, m1)

            for i in range(QK0):
                qk_job("q", i)
                qk_job("k", i)
            m_gate = {}

            def gate_job(n):
                banks, m = job(("g", n), H, L, [])
                G = GA if n < 8 else GB

                def out():
                    act.wait(m, m_hb)
                    m_gate[n] = act.mark(lambda e, b=banks[0].t: e.activation(
                        G[:, n % 8, :], b[:, 0:S], ACT.Tanh, scale=0.5, bias=hb[:, n:n + 1]))
                    give(banks[0], m_gate[n])
                if n:
                    out()
                else:
                    later(0, out)

            s_tb = [sem(f"s_tb{i}") for i in range(3)]
            tbm = {h: dma(sp, s_tb[h], tb[:, h, :], tabs[h], 1) for h in range(3)}

            def table1(h):
                def rel(mm):
                    if h + 3 < NH:
                        sp.wait(mm)
                        tbm[h + 3] = dma(sp, s_tb[h % 3], tb[:, h % 3, :], tabs[h + 3], (h + 3) // 3 + 1)
                return tb[:, h % 3, :], tbm[h], rel

            def qk1(h):
                o, j = 64 * (h % 2), h // 2
                return [(Q[o:o + 64, j, :], K[o:o + 64, j, :], [m_qk["q", j], m_qk["k", j]])]

            oh, ol = ah, al
            fills = [lambda i=i, w=w: qk_job(w, i) for i in range(QK0, KD) for w in ("q", "k")]
            fills += [lambda n=n: gate_job(n) for n in range(16)]

            def fill1(n):
                for _ in range(1 + (len(fills) > NH + 5 - n)):
                    if fills:
                        fills.pop(0)()
                if n == NH + 4:
                    log_tables()

            m_o = attention(c, NH, qk1, VT, table1, oh, ol, fill1, m_v, sb(c, "sS", [P, 3, 384]),
                            sb(c, "sT", [P, 2, 384]), sb(c, "sP", [P, 3, 384]))

            gates_done = pe.last()
            m_c, norm_c = {}, {}

            def silu(i):
                k = i % 3
                R, mr, j = norm_c["r"]
                pool.wait(mr, conv_m[i])
                m1 = pool.mark(lambda e: e.tensor_tensor(CA[:, i, :], CA[:, i, :], R, ALU.mult))
                lnm[j] = (m1,)
                act.wait(m1, sgm[k], m_ci[KD - 1], m_cg)
                m2 = act.mark(lambda e: e.activation(sg[:, k, :], CA[:, i, :], ACT.Tanh, scale=cg5[:, i:i + 1]))

                def out():
                    dve.wait(m2)
                    sgm[k] = m3 = dve.mark(lambda e: e.scalar_tensor_tensor(
                        out=CA[:, i, :], in0=sg[:, k, :], scalar=1.0, in1=CA[:, i, :], op0=ALU.add, op1=ALU.mult))
                    act.wait(gates_done, m3)
                    m4 = act.mark(lambda e: e.activation(hh[:, i, :], CA[:, i, :], ACT.Copy, scale=vec("conv_norm_g", i)))

                    def low_part():
                        dve.wait(gates_done, m4)
                        m_c[i] = dve.mark(lambda e: e.scalar_tensor_tensor(
                            out=hl[:, i, :], in0=CA[:, i, :], scalar=vec("conv_norm_g", i), in1=hh[:, i, :],
                            op0=ALU.mult, op1=ALU.subtract))
                    later(0, low_part)
                later(0, out)

            def last_square():
                last_c = list(conv_m)[-1]
                cs.add(CA[:, last_c, :], [conv_m[last_c]])
                norm_c["r"] = rstd(cs.bank, D, S, cs.m)

            OH = [oh[:, i, :] for i in range(KD)]
            OL = [ol[:, i, :] for i in range(KD)]
            m_yb = {}
            silus = [0, 0, 0, 2, 2, 2, 2, 0]
            for i in range(KD):
                banks, m = job(("ao", i), OH, OL, m_o)
                dve.wait(m, m_gate[8 + i])
                m_yb[i] = dve.mark(lambda e: e.scalar_tensor_tensor(
                    out=GB[:, i, :], in0=GB[:, i, :], scalar=1.0, in1=banks[0].t[:, 0:S], op0=ALU.add, op1=ALU.mult))
                give(banks[0], m_yb[i])
                if i == 0:
                    w1.some(1000)
                    w2.some(1000)
                    aside.clear()
                if i == 2:
                    last_square()
                for n in range(sum(silus[:i]), sum(silus[:i + 1])):
                    silu(n)
            settle()
            ao_done = pe.last()
            m_mix = []
            for i in range(KD):
                banks, m = job(("co", i), H, L, [m_c[n] for n in range(KD)])
                dve.wait(m, m_gate[i])
                m1 = dve.mark(lambda e: e.scalar_tensor_tensor(
                    out=GA[:, i, :], in0=GA[:, i, :], scalar=1.0, in1=banks[0].t[:, 0:S], op0=ALU.add, op1=ALU.mult))
                give(banks[0], m1)
                dve.wait(m1, m_yb[i])
                m2 = dve.mark(lambda e: e.scalar_tensor_tensor(
                    out=GA[:, i, :], in0=GA[:, i, :], scalar=0.5, in1=GB[:, i, :], op0=ALU.mult, op1=ALU.add))
                act.wait(ao_done)
                pool.wait(ao_done)
                m_mix.append(split(GA[:, i, :], oh[:, i, :], ol[:, i, :], [m2], pool))
            co_done = pe.last()
            m_xr, xg, sums = [], {}, Squares(KD, hold=True)
            for i in range(KD):
                banks, m = job(("wo", i), OH, OL, m_mix)
                m_xr.append(add_residual(i, banks, m, sums, "norm2_g", co_done, xg))
            wall = fence()

        def step(f, *w):
            dve.wait(*w)
            return dve.mark(f)

        rp = {}

        def rotary_tables(buf, free):
            ang, kf, r0, r1 = (buf[:, n, :] for n in range(4))
            posi = buf[:, 4, :].bitcast(I32)
            st_ = {}

            def start():
                act.wait(*free)
                dve.wait(*free)
                st_["a"] = dma(act, sem("s_pos"), posi, pos, 1)

            def on(key, src, f):
                def go():
                    st_[key] = step(f, st_[src])
                return go

            out = [start, on("a", "a", lambda e: e.tensor_copy(r0, posi)),
                   on("a", "a", lambda e: e.tensor_scalar(ang, r0, vec("inv"), None, ALU.mult)),
                   on("a", "a", lambda e: e.tensor_scalar(kf, ang, 1.0 / TWO_PI, MAGIC, ALU.mult, ALU.add)),
                   on("a", "a", lambda e: e.tensor_scalar(kf, kf, MAGIC, None, ALU.subtract))]
            for cst in (C1, C2, C3):
                out.append(on("a", "a", lambda e, cst=cst: e.scalar_tensor_tensor(
                    out=ang, in0=kf, scalar=-cst, in1=ang, op0=ALU.mult, op1=ALU.add)))
            out += [on("r0", "a", lambda e: e.tensor_scalar(r0, ang, PI_F, -PI_F, ALU.min, ALU.max)),
                    on("b", "r0", lambda e: e.tensor_scalar(kf, ang, float(np.pi / 2), -TWO_PI, ALU.is_gt, ALU.mult)),
                    on("b", "b", lambda e: e.scalar_tensor_tensor(out=r1, in0=kf, scalar=float(np.pi / 2), in1=ang,
                                                                  op0=ALU.add, op1=ALU.add)),
                    on("b", "b", lambda e: e.tensor_scalar(r1, r1, PI_F, -PI_F, ALU.min, ALU.max))]

            def sines():
                act.wait(st_["b"])
                act.mark(lambda e: e.activation(rope[:, 1, :], r0, ACT.Sin))
                st_["s"] = act.mark(lambda e: e.activation(rope[:, 0, :], r1, ACT.Sin))

            def finish():
                a4 = step(lambda e: e.tensor_scalar(rope[:, 1, :], rope[:, 1, :], vec("sgn"), None, ALU.mult), st_["s"])
                rp["m"] = step(lambda e: e.tensor_scalar(rope[:, 2:4, :], rope[:, 0:2, :], 96.0 ** -0.5, None,
                                                         ALU.mult), a4)
            return out + [sines, finish]

        def ffn(keys_g, keys_u, keys_d, with_conv, m_xr, xg, wall, sums, g, g_next):
            with ExitStack() as c:
                fh = sb(c, "fh", [P, FT, S], F32R)
                fl = sb(c, "fl", [P, FT, S], F32R)
                ug = sb(c, "ug", [P, NB, S])
                uv = sb(c, "uv", [P, NB, S])
                tt = sb(c, "tt", [P, NB, S])
                act.wait(*wall)
                dve.wait(*wall)
                pool.wait(*wall)
                m_f = []
                fr = {}

                def conv3(banks, m, row, buf, free, R=None, z=None):
                    b = banks[0].t
                    if R is not None:
                        m = dve.mark(lambda e: e.tensor_tensor(z, banks[0].t[:, 0:S], R, ALU.mult))
                        b = z
                    act.wait(m, free)
                    w = [vec("ffn_conv_w", j * 44 + row) for j in range(3)]
                    m1 = act.mark(lambda e: e.activation(buf, b[:, 0:S], ACT.Identity, scale=w[2], bias=vec("ffn_conv_b", row)))
                    dve.wait(m1)
                    m2 = dve.mark(lambda e: e.scalar_tensor_tensor(
                        out=buf[:, 1:S], in0=b[:, 0:S - 1], scalar=w[1], in1=buf[:, 1:S], op0=ALU.mult, op1=ALU.add))
                    dve.wait(m2)
                    m3 = dve.mark(lambda e: e.scalar_tensor_tensor(
                        out=buf[:, 2:S], in0=b[:, 0:S - 2], scalar=w[0], in1=buf[:, 2:S], op0=ALU.mult, op1=ALU.add))
                    give(banks[0], m3)
                    return m3

                def plain(banks, m, row, buf, free, R=None, z=None):
                    if R is not None:
                        m1 = dve.mark(lambda e: e.tensor_tensor(buf, banks[0].t[:, 0:S], R, ALU.mult))
                    else:
                        act.wait(m, free)
                        m1 = act.mark(lambda e: e.activation(buf, banks[0].t[:, 0:S], ACT.Copy))
                    give(banks[0], m1)
                    return m1

                one = conv3 if with_conv else plain

                def finish(i, mg, mv):
                    j = i % NB
                    act.wait(mg, fr.get(("t", i - NB)))
                    mt = act.mark(lambda e: e.activation(tt[:, j, :], ug[:, j, :], ACT.Tanh, scale=0.5))
                    pool.wait(mg, mv)
                    mp = fr["g", i] = pool.mark(lambda e: e.tensor_tensor(uv[:, j, :], uv[:, j, :], ug[:, j, :], ALU.mult))

                    def gated():
                        dve.wait(mp, mt)
                        ms = fr["v", i] = dve.mark(lambda e: e.scalar_tensor_tensor(
                            out=tt[:, j, :], in0=tt[:, j, :], scalar=1.0, in1=uv[:, j, :], op0=ALU.add, op1=ALU.mult))

                        def rest():
                            q = pool if i < FT - 2 else dve
                            act.wait(ms)
                            m1 = act.mark(lambda e: e.activation(fh[:, i, :], tt[:, j, :], ACT.Copy))
                            q.wait(m1)
                            r = fr["t", i] = q.mark(lambda e: e.tensor_tensor(
                                fl[:, i, :], tt[:, j, :], fh[:, i, :], ALU.subtract))
                            m_f.append(r)
                        later(0, rest)
                    later(0, gated)

                def out(n, banks, m, R=None, mr=None):
                    i, j = n // 2, n // 2 % NB
                    if R is not None:
                        dve.wait(m, mr)
                    if n % 2 == 0:
                        gm[i] = one(banks, m, 22 + i, ug[:, j, :], fr.get(("g", i - NB)), R, tt[:, i, :] if i < 2 else None)
                    else:
                        mv = one(banks, m, i, uv[:, j, :], fr.get(("v", i - NB)), R, tt[:, 2 + i, :] if i < 2 else None)
                        later(0, lambda: finish(i, gm[i], mv))

                gm = {}
                keys = [(k, i) for i in range(FT) for k in (keys_g, keys_u)]
                m_h = first_jobs(keys[:FIRST], g, xg, m_xr, sums, out, EARLY)
                for n in range(FIRST, 2 * FT):
                    banks, m = job(keys[n], H, L, m_h)
                    out(n, banks, m)
                settle()
                FH = [fh[:, i, :] for i in range(FT)]
                FL = [fl[:, i, :] for i in range(FT)]
                m_x2, xg, sums = [], {}, Squares(KD, hold=bool(g_next))
                h_done = pe.last()
                side = rotary_tables(ug, [fr["g", n] for n in range(FT - NB, FT)]) if with_conv else []
                for i in range(KD):
                    banks, m = job((keys_d, i), FH, FL, m_f)
                    m_x2.append(add_residual(i, banks, m, sums, g_next, h_done, xg))
                    for _ in range(3):
                        if side and i < 6:
                            side.pop(0)()
                return m_x2, xg, fence(), sums

        m_x2, xg, wall, sums = ffn("ug", "uv", "dn", True, m_xr, xg, wall, sums, "norm2_g", "ln_mix_2")

        with ExitStack() as c:
            qn = sb(c, "qn", [P, 4, S])
            qr = sb(c, "qr", [P, 2, S])
            kn = sb(c, "kn", [P, 4, S])
            krp = sb(c, "krp", [P, S])
            cc = sb(c, "cc", [P, 5, S])
            ch = sb(c, "ch", [P, 5, S], F32R)
            cl = sb(c, "cl", [P, 5, S], F32R)
            mv_ = sb(c, "mv_", [P, 2, 512])
            gv = sb(c, "gv", [P, 2, 512])
            GA = sb(c, "GA2", [P, KD, S])
            GB = sb(c, "GB2", [P, KD, S])
            gq = sb(c, "gq", [P, 2, S])
            gk = sb(c, "gk", [P, 2, S])
            og = sb(c, "og", [P, 4, S])
            glr = sb(c, "glr", [P, S])
            bc = sb(c, "bc", [P, 2, S])
            eb = sb(c, "eb", [P, 2, 2 * S])
            qL = sb(c, "qL", [P, 2, S])
            kL = sb(c, "kL", [P, 2, S])
            att = sb(c, "att", [P, 4, 512])
            at, tmp = att[:, 0:2, :], att[:, 2:4, :]
            kd = sb(c, "kd", [P, 2, S])
            st = sb(c, "st", [P, 3, 2, P])
            ebl = sb(c, "ebl", [P, 2, 4])
            go_ = sb(c, "go_", [P, 4, S])
            msk = sb(c, "msk", [P, 7, P])
            cm = tmp[:, 0, :]
            mh3 = sb(c, "mh3", [P, 6, S], F32R)
            ah = sb(c, "ah2", [P, 4, S], F32R)
            al = sb(c, "al2", [P, 4, S], F32R)

            act.wait(*wall)
            dve.wait(*wall)
            pool.wait(*wall)
            s_m = [sem("s_m0")]
            m_wg2 = dma(act, s_c[2], wg2[64:80, :], w_gate2, 1)
            m_caus = dma(act, s_c[3], caus[:, :], tabs[NH], 1)
            act.wait(*wall)
            m_msk = dma(act, s_m[0], msk[:, :, :], masks.rearrange("p (l i) -> p l i", l=7), 1)
            m_cm0 = pool.mark(lambda e: e.memset(cm, 1.0))
            pool.wait(m_cm0)
            m_cm = pool.mark(lambda e: e.memset(cm.rearrange("p (a b) -> p a b", b=64)[:, :, 0:1], 0.0))

            m_rope = rp["m"]

            def copy_out(key, xh, xl, ready, dst, scale=1.0, extra=()):
                banks, m = job(key, xh, xl, ready)
                act.wait(m, *extra)
                m1 = act.mark(lambda e: e.activation(dst, banks[0].t[:, 0:S], ACT.Copy, scale=scale))
                give(banks[0], m1)
                return m1

            m_cc = []
            sum_q, sum_k = Squares(3, hold=True), Squares(2, hold=True)

            def cc_out(n, banks, m, R, mr):
                m_cc.append(step(lambda e: e.tensor_tensor(cc[:, n, :], banks[0].t[:, 0:S], R, ALU.mult), m, mr))
                give(banks[0], m_cc[n])

            m_h = first_jobs([("cq", 0), ("cq", 1), ("cq", 2), ("ckv", 0)], "ln_mix_2", xg, m_x2, sums, cc_out, EARLY)
            for i in range(3):
                sum_q.add(cc[:, i, :], [m_cc[i]])
            sum_k.add(cc[:, 3, :], [m_cc[3]])
            m_cc.append(copy_out(("ckv", 1), H, L, m_h, cc[:, 4, :]))
            sum_k.add(cc[:, 4, :], [m_cc[4]])
            sum_q.end()

            def roped(k1, k2, xh, xl, ready, dst, cs, sn, n):
                b1, m1 = job(k1, xh, xl, ready)
                dve.wait(m1, m_rope)
                d1 = dve.mark(lambda e: e.tensor_tensor(dst, b1[0].t[:, 0:S], cs, ALU.mult))
                give(b1[0], d1)
                b2, m2 = job(k2, xh, xl, [])
                dve.wait(m2, rfree.get(n))
                d2 = dve.mark(lambda e: e.tensor_tensor(glr2[:, n, :], b2[0].t[:, 0:S], sn, ALU.mult))
                give(b2[0], d2)
                dve.wait(d1, d2)
                d3 = dve.mark(lambda e: e.tensor_tensor(dst, dst, glr2[:, n, :], ALU.add))
                rfree[n] = d3
                return d3

            rfree = {}
            glr2 = kd
            banks, m = job(("kr", 0), H, L, [])
            act.wait(m)
            m_glr = act.mark(lambda e, b=banks[0].t: e.activation(glr[64:80, :], b[64:80, 0:S], ACT.Copy))
            m_kt = step(lambda e, b=banks[0].t: e.tensor_tensor(glr[0:32, :], b[0:32, 0:S], rope[0:32, 0, :], ALU.mult),
                        m, m_glr, m_rope)
            m_kt = step(lambda e, b=banks[0].t: e.tensor_tensor(glr[32:64, :], b[32:64, 0:S], rope[32:64, 1, :], ALU.mult))
            give(banks[0], m_kt)

            def rotary_keys():
                b = xb.take()
                pe.wait(m_kt, m_vc, *b.free)
                m = pe.mark(lambda e: e.matmul(b.t[:, 0:S], vc[0:64, V["sel"]:V["sel"] + P], glr[0:64, :],
                                               start=True, stop=True))
                act.wait(m)
                mk = act.mark(lambda e: e.activation(krp[:, :], b.t[:, 0:S], ACT.Copy))
                give(b, mk)
                return mk
            sum_k.end()
            m_nq = norm(cc[:, 0:3, :], 3, "mla_norm_cq_2", ch[:, 0:3, :], cl[:, 0:3, :], m_cc[0:3], sum_q)

            gx, ge = eb[:, 0, :], eb[:, 1, :]
            bcf = bc[:, :, :].rearrange("p a s -> p (a s)")
            gqf = gq[:, :, :].rearrange("p a s -> p (a s)")
            gkf = gk[:, :, :].rearrange("p a s -> p (a s)")
            QL = [qL[:, :, :], go_[:, 0:2, :]]
            KL = [kL[:, :, :], go_[:, 2:4, :]]
            QLf = [q_.rearrange("p a s -> p (a s)") for q_ in QL]
            KLf = [k_.rearrange("p a s -> p (a s)") for k_ in KL]
            kdf = kd[:, :, :].rearrange("p a s -> p (a s)")
            gst = {"e": {}, "acc": {}, "tmp": {}, "lv": {}, "qk": {}}

            def decay_logits():
                b = xb.take()
                pe.wait(m_glr, m_wg2, *b.free)
                pe.do(lambda e: e.matmul(b.t[:, 0:S], wg2[64:80, 0:P], glr[64:80, :], start=True, stop=True,
                                         skip_group_check=True))
                m = pe.mark(lambda e: e.matmul(b.t[:, S:2 * S], wg2[64:80, P:2 * P], glr[64:80, :], start=False, stop=True,
                                               skip_group_check=True))
                dve.wait(m)
                for i in range(2):
                    g1 = dve.mark(lambda e, i=i: e.tensor_scalar(gx[:, i * S:i * S + S], b.t[:, i * S:i * S + S],
                                                                 vec("gla_b_gate_2", i), None, ALU.add))
                give(b, g1)
                act.wait(g1)
                gst["x"] = act.mark(lambda e: e.activation(ge, gx, ACT.Abs))

            def decay_soft():
                act.wait(gst["x"])
                g3 = act.mark(lambda e: e.activation(ge, ge, ACT.Exp, scale=-1.0))
                act.wait(g3)
                gst["x"] = act.mark(lambda e: e.activation(ge, ge, ACT.Ln, bias=vec("one")))

            def decay_sums():
                g5 = step(lambda e: e.scalar_tensor_tensor(out=gx, in0=gx, scalar=0.0, in1=ge, op0=ALU.min,
                                                           op1=ALU.subtract), gst["x"])
                return step(lambda e: e.tensor_tensor_scan(bcf, cm, gx, 0.0, ALU.mult, ALU.add), g5, m_cm)

            m_gq, m_gk = [], []
            m_gq.append(copy_out(("gq", 0), H, L, [], gq[:, 0, :], 0.125))
            decay_logits()
            m_kr = rotary_keys()
            m_gq.append(copy_out(("gq", 1), H, L, [], gq[:, 1, :], 0.125))
            m_nk = norm(cc[:, 3:5, :], 2, "mla_norm_ckv_2", ch[:, 3:5, :], cl[:, 3:5, :], m_cc[3:5], sum_k,
                        exact_ln=True)
            decay_soft()
            m_gk.append(copy_out(("gk", 0), H, L, [], gk[:, 0, :]))
            m_bc = decay_sums()
            m_gk.append(copy_out(("gk", 1), H, L, [], gk[:, 1, :]))
            gst["e"] = {0: [m_bc], 1: [m_bc]}

            def ebuf(n):
                return eb[:, n % 2, :]

            def factors(n):
                s = LEVELS[n]
                bv = bcf.rearrange("p (n w) -> p n w", w=2 * s)
                E = ebuf(n)
                Ev = E.rearrange("p (n w) -> p n w", w=2 * s)
                ref = bv[:, :, s - 1:s].to_broadcast([P, 512 // (2 * s), 2 * s])
                l1 = step(lambda e: e.tensor_tensor(Ev, bv, ref, ALU.subtract), m_bc, *gst["e"][n % 2])
                act.wait(l1)
                l2 = act.mark(lambda e: e.activation(E, E, ACT.Abs))
                act.wait(l2)
                gst["f"] = act.mark(lambda e: e.activation(E, E, ACT.Exp, scale=-1.0 / 16))

            def scaled_keys(n):
                E, l3 = ebuf(n), gst["f"]
                pool.wait(l3, m_gk[1], gst["lv"].get(n - 2))
                gst["kl"] = pool.mark(lambda e: e.tensor_tensor(KLf[n % 2], gkf, E, ALU.mult))

            def scaled_queries(n):
                E, l3 = ebuf(n), gst["f"]
                l4 = step(lambda e: e.tensor_tensor(QLf[n % 2], gqf, E, ALU.mult), l3, m_gq[1], gst["lv"].get(n - 2))
                gst["e"][n % 2] = gst["qk"][n] = [l4, gst["kl"]]

            def products(n):
                if n == 0:
                    q_, k_, ready = gq, gk, m_gq + m_gk
                else:
                    q_, k_, ready = QL[n % 2], KL[n % 2], gst["qk"][n]
                bs = [xb.take(), xb.take()]
                pe.wait(*ready, *bs[0].free, *bs[1].free)
                for par in range(2):
                    o = 64 * par
                    for i in range(4):
                        p_, t = i // 2, i % 2
                        f = (lambda e, i=i, o=o, p_=p_, t=t, b=bs[par].t: e.matmul(
                            b[:, i * P:i * P + P], k_[o:o + 64, p_, t * P:t * P + P], q_[o:o + 64, p_, t * P:t * P + P],
                            start=(i == 0), stop=True, skip_group_check=True))
                        if i == 3:
                            m = pe.mark(f)
                        else:
                            pe.do(f)
                gst["lv"][n] = m
                gst["b", n] = bs

            def level_add(n):
                bs, m = gst["b", n], gst["lv"][n]
                mb = msk[:, n:n + 1, :].to_broadcast([P, 4, P])
                for par in range(2):
                    bt = bs[par].t[:, :].rearrange("p (a i) -> p a i", a=4)
                    if n == 0:
                        g = step(lambda e: e.tensor_tensor(at[:, par, :].rearrange("p (a i) -> p a i", a=4), bt, mb,
                                                           ALU.mult), m, m_msk)
                        gst["acc"][par] = g
                    else:
                        g = step(lambda e: e.tensor_tensor(tmp[:, par, :].rearrange("p (a i) -> p a i", a=4), bt, mb,
                                                           ALU.mult), m, m_msk, gst["tmp"].get(par))
                        pool.wait(g, gst["acc"][par])
                        gst["acc"][par] = gst["tmp"][par] = pool.mark(lambda e: e.tensor_tensor(
                            at[:, par, :], at[:, par, :], tmp[:, par, :], ALU.add))
                    give(bs[par], g)

            bv64 = bcf.rearrange("p (n w) -> p n w", w=64)
            last = bv64[:, :, 63:64]

            def decays():
                E, E2 = eb[:, 1, :], eb[:, 0, :]
                l1 = step(lambda e: e.tensor_tensor(E.rearrange("p (n w) -> p n w", w=64), bv64,
                                                    last.to_broadcast([P, 8, 64]), ALU.subtract), m_bc, *gst["e"][1])
                act.wait(l1)
                gst["d"] = act.mark(lambda e: e.activation(E, E, ACT.Exp, scale=-1.0 / 16))
                act.wait(*gst["e"][0])
                gst["d2"] = act.mark(lambda e: e.activation(E2, bcf, ACT.Exp, scale=1.0 / 16))
                gst["d3"] = act.mark(lambda e: e.activation(ebl[:, :, :].rearrange("p a c -> p (a c)"),
                                                            last.rearrange("p n w -> p (n w)"), ACT.Exp, scale=1.0 / 16))

            def decayed():
                E, E2 = eb[:, 1, :], eb[:, 0, :]
                gst["k"] = step(lambda e: e.tensor_tensor(KLf[1], gkf, E, ALU.mult), gst["d"], gst["lv"][5])
                gst["q"] = step(lambda e: e.tensor_tensor(qL[:, :, :].rearrange("p a s -> p (a s)"), gqf, E2, ALU.mult),
                                gst["d2"], gst["lv"][6])

            def turn_keys():
                b = xb.take()
                pe.wait(gst["k"], m_id, *b.free)
                for t in range(2):
                    for p_ in range(2):
                        m = pe.mark(lambda e, t=t, p_=p_: e.transpose(b.t[:, t * S + p_ * P:t * S + p_ * P + P],
                                                                      KL[1][:, p_, t * P:t * P + P], ident[:, :]))
                act.wait(m, *rfree.values())
                gst["kt"] = m
                gst["kd"] = act.mark(lambda e: e.activation(kdf, b.t[:, :], ACT.Copy))
                give(b, gst["kd"])

            def chunk_sums():
                for ci in range(3):
                    o, t = 64 * (ci % 2), ci // 2
                    b = xb.take()
                    pe.wait(gst["kd"], *m_gv, *b.free)
                    for p_ in range(2):
                        m = pe.mark(lambda e, p_=p_, o=o, t=t, b=b: e.matmul(
                            b.t[:, p_ * S:p_ * S + S], kd[o:o + 64, t, p_ * P:p_ * P + P],
                            gv[o:o + 64, t, p_ * S:p_ * S + S], start=(p_ == 0), stop=True, skip_group_check=True))
                    gst["u", ci] = (b, m)

            def states():
                prev = None
                for ci in range(3):
                    b, m = gst["u", ci]
                    now = []
                    for p_ in range(2):
                        for hf in range(2):
                            r = slice(64 * hf, 64 * hf + 64)
                            U = b.t[r, p_ * S + hf * P:p_ * S + hf * P + P]
                            if ci == 0:
                                g = step(lambda e, r=r, p_=p_, U=U: e.tensor_copy(st[r, 0, p_, :], U), m)
                            else:
                                g = step(lambda e, r=r, p_=p_, U=U, ci=ci: e.scalar_tensor_tensor(
                                    out=st[r, ci, p_, :], in0=st[r, ci - 1, p_, :], scalar=ebl[r, p_, ci:ci + 1], in1=U,
                                    op0=ALU.mult, op1=ALU.add), m, gst["d3"], prev)
                    prev = g
                    give(b, g)
                gst["st"] = prev

            def gla_out():
                bs = [xb.take(), xb.take()]
                pe.wait(gst["st"], gst["q"], gst["acc"][0], gst["acc"][1], *m_gv, *bs[0].free, *bs[1].free)
                marks = []
                for par in range(2):
                    b, o = bs[par].t, 64 * par
                    for p_ in range(2):
                        h = 2 * p_ + par
                        for t in range(2):
                            pe.do(lambda e, b=b, p_=p_, t=t, h=h, par=par: e.matmul(
                                b[:, p_ * S + t * P:p_ * S + t * P + P], gv[:, t, h * P:h * P + P],
                                at[:, par, (2 * p_ + t) * P:(2 * p_ + t) * P + P],
                                start=(p_ == 0 and t == 0), stop=False, skip_group_check=True))
                    for p_ in range(2):
                        for ci in range(1, 4):
                            f = (lambda e, b=b, p_=p_, o=o, ci=ci: e.matmul(
                                b[:, p_ * S + ci * 64:p_ * S + ci * 64 + 64], st[o:o + 64, ci - 1, p_, :],
                                qL[o:o + 64, p_, ci * 64:ci * 64 + 64], start=False, stop=True, skip_group_check=True))
                            m = pe.mark(f)
                    for p_ in range(2):
                        h = 2 * p_ + par
                        act.wait(m)
                        marks.append((h, act.mark(lambda e, b=b, h=h, p_=p_: e.activation(
                            go_[:, h, :], b[:, p_ * S:p_ * S + S], ACT.Copy))))
                    give(bs[par], marks[-1][1])
                gst["o"] = dict(marks)

            def gla_squares():
                for h in range(4):
                    gst["sq", h] = square(go_[:, h, :], [gst["o"][h]], act)

            def gla_sums():
                log_tables()
                for pr in range(2):
                    b = xb.take()
                    for n in range(2):
                        q_, ms = gst["sq", 2 * pr + n]
                        pe.wait(ms, m_on, *b.free)
                        m = sqm[q_] = pe.mark(lambda e: e.matmul(b.t[:, n * S:n * S + S], ones[:, :], sq[:, q_, :],
                                                                 start=(n == 0), stop=True, skip_group_check=True))
                    gst["r", pr] = rstd(b, P, 512, m)

            def gla_norm(pr):
                R, mr, j = gst["r", pr]
                for n in range(2):
                    h = 2 * pr + n
                    g1 = step(lambda e, h=h, n=n: e.scalar_tensor_tensor(
                        out=go_[:, h, :], in0=go_[:, h, :], scalar=vec("gla_norm_2"), in1=R[:, n * S:n * S + S],
                        op0=ALU.mult, op1=ALU.mult), mr)
                    pool.wait(g1, m_og[h])
                    g2 = pool.mark(lambda e, h=h: e.tensor_tensor(go_[:, h, :], go_[:, h, :], og[:, h, :], ALU.mult))
                    act.wait(*uq_done)
                    dve.wait(*uq_done)
                    gst["g", h] = g2
                lnm[j] = (g1,)

            def gla_parts():
                act.wait(*uq_done)
                pool.wait(*uq_done)
                for h in range(4):
                    m_g.append(split(go_[:, h, :], ch[:, h, :], cl[:, h, :], [gst["g", h]], pool if h % 2 else dve))

            def stage(n):
                if n + 1 < 7:
                    factors(n + 1)
                elif n == 6:
                    decays()
                if n < 7:
                    products(n)
                if n + 1 < 7:
                    scaled_keys(n + 1)
                if n > 0:
                    level_add(n - 1)
                if n + 1 < 7:
                    scaled_queries(n + 1)
                elif n == 6:
                    decayed()

            stages = [lambda n=n: stage(n) for n in range(1, 7)]
            stages += [lambda: (stage(7), turn_keys()), chunk_sums, states, gla_out, gla_squares, gla_sums,
                       lambda: gla_norm(0), lambda: gla_norm(1), gla_parts]
            owed2 = [0.0]

            def tick(part):
                owed2[0] += part
                pace = PACE if len(stages) > 9 else PACE2
                while owed2[0] > pace and stages:
                    owed2[0] -= pace
                    stages.pop(0)()

            banks, m = job(("gv", 0), H, L, [])
            m_gv = []
            for t in range(2):
                act.wait(m)
                m1 = act.mark(lambda e, t=t, b=banks[t].t: e.activation(gv[:, t, :], b[:, :], ACT.Copy))
                give(banks[t], m1)
                m_gv.append(m1)
            factors(1)
            products(0)
            scaled_keys(1)
            scaled_queries(1)
            CH = [ch[:, i, :] for i in range(5)]
            CL = [cl[:, i, :] for i in range(5)]
            m_q, m_k, m_qr = {}, {}, {}
            for i in range(4):
                m_q[i] = copy_out(("qn", i), CH[0:3], CL[0:3], m_nq, qn[:, i, :], 96.0 ** -0.5)
                tick(0.375)
            for i in range(2):
                m_qr[i] = roped(("qr", i), ("qrs", i), CH[0:3], CL[0:3], [], qr[:, i, :], rope[:, 2, :], rope[:, 3, :], 1)
                tick(0.75)
            for i in range(4):
                m_k[i] = copy_out(("kn", i), CH[3:5], CL[3:5], m_nk, kn[:, i, :])
                tick(0.25)
            banks, m = job(("mv", 0), CH[3:5], CL[3:5], [])
            m_mv = []
            for t in range(2):
                act.wait(m)
                m1 = act.mark(lambda e, t=t, b=banks[t].t: e.activation(mv_[:, t, :], b[:, :], ACT.Copy))
                give(banks[t], m1)
                m_mv.append(m1)
            uq_done = [pe.last()]
            tick(1)
            m_og, m_g = {}, []
            for i in range(4):
                banks, m = job(("og", i), H, L, [])
                b = banks[0].t
                act.wait(m)
                m1 = act.mark(lambda e, i=i, b=b: e.activation(og[:, i, :], b[:, 0:S], ACT.Tanh, scale=0.5))
                dve.wait(m1)
                m2 = dve.mark(lambda e, i=i, b=b: e.scalar_tensor_tensor(
                    out=og[:, i, :], in0=og[:, i, :], scalar=1.0, in1=b[:, 0:S], op0=ALU.add, op1=ALU.mult))
                give(banks[0], m2)
                m_og[i] = m2
                tick(1)
            m_gate = {}

            def gate2(n):
                banks, m = job(("g2", n), H, L, [])
                G = GA if n < 8 else GB
                act.wait(m)
                m_gate[n] = act.mark(lambda e, b=banks[0].t: e.activation(G[:, n % 8, :], b[:, 0:S], ACT.Tanh, scale=0.5))
                give(banks[0], m_gate[n])

            def go_job(i):
                banks, m = job(("go", i), CH[0:4], CL[0:4], m_g)
                m_gate[8 + i] = step(lambda e, i=i, b=banks[0].t: e.scalar_tensor_tensor(
                    out=GB[:, i, :], in0=GB[:, i, :], scalar=1.0, in1=b[:, 0:S], op0=ALU.add, op1=ALU.mult), m, m_gate[8 + i])
                give(banks[0], m_gate[8 + i])

            fills = [lambda n=n: gate2(n) for n in range(16)]
            while stages:
                fills.pop(0)()
                tick(1)
            fills += [lambda i=i: (go_job(i), go_job(i + 1)) for i in range(0, KD, 2)]

            def fill2(n):
                if fills:
                    fills.pop(0)()

            def table2(h):
                return caus[:, :], m_caus, lambda mm: None

            def qk2(h):
                o, j, o2, j2 = 64 * (h % 2), h // 2, 32 * (h % 4), h // 4
                return [(qn[o:o + 64, j, :], kn[o:o + 64, j, :], [m_q[j], m_k[j]]),
                        (qr[o2:o2 + 32, j2, :], krp[o2:o2 + 32, :], [m_qr[j2], m_kr])]

            m_o = attention(c, MH, qk2, mv_, table2, ah, al, fill2, m_mv,
                            cc[:, :, :].rearrange("p a s -> p (a s)")[:, 0:1152].rearrange("p (a s) -> p a s", a=3),
                            eb[:, :, :].rearrange("p a s -> p (a s)")[:, 0:768].rearrange("p (a s) -> p a s", a=2),
                            att[:, :, :].rearrange("p a s -> p (a s)")[:, 0:1152].rearrange("p (a s) -> p a s", a=3),
                            [gst["q"]])
            while fills:
                fill2(0)
            go_done = pe.last()
            m_mix = []
            MH_ = [ch[:, i, :] if i < 5 else mh3[:, i - 5, :] for i in range(KD)]
            ML_ = [cl[:, i, :] if i < 5 else mh3[:, i - 2, :] for i in range(KD)]
            OH, OL = [ah[:, i, :] for i in range(4)], [al[:, i, :] for i in range(4)]
            for i in range(KD):
                banks, m = job(("mo", i), OH, OL, m_o)
                m1 = step(lambda e, i=i, b=banks[0].t: e.scalar_tensor_tensor(
                    out=GA[:, i, :], in0=GA[:, i, :], scalar=1.0, in1=b[:, 0:S], op0=ALU.add, op1=ALU.mult), m, m_gate[i])
                give(banks[0], m1)
                m2 = step(lambda e, i=i: e.scalar_tensor_tensor(
                    out=GA[:, i, :], in0=GB[:, i, :], scalar=0.5, in1=GA[:, i, :], op0=ALU.mult, op1=ALU.add),
                    m1, m_gate[8 + i])
                act.wait(go_done)
                pool.wait(go_done)
                m_mix.append(split(GA[:, i, :], MH_[i], ML_[i], [m2], pool))
            m_xr, xg, sums = [], {}, Squares(KD, hold=True)
            for i in range(KD):
                banks, m = job(("wo2", i), MH_, ML_, m_mix)
                m_xr.append(add_residual(i, banks, m, sums, "ln_ffn_2", go_done, xg))
            wall = fence()

        m_x4, _, wall, sums = ffn("fg", "fu", "fd", False, m_xr, xg, wall, sums, "ln_ffn_2", None)

        R, mr, j = rstd(sums.bank, D, S, sums.m)
        s_o = sem("s_o")
        outv = out.rearrange("p (k s) -> p k s", k=KD)
        for i in range(KD):
            if i in (2, 5):
                pool.wait(mr)
                m0 = pool.mark(lambda e, i=i: e.tensor_tensor(X[:, i, :], X[:, i, :], R, ALU.mult))
                act.wait(m0)
                m1 = act.mark(lambda e, i=i: e.activation(X[:, i, :], X[:, i, :], ACT.Copy, scale=vec("final_norm_2", i)))
            else:
                dve.wait(mr)
                m1 = dve.mark(lambda e, i=i: e.scalar_tensor_tensor(
                    out=X[:, i, :], in0=X[:, i, :], scalar=vec("final_norm_2", i), in1=R, op0=ALU.mult, op1=ALU.mult))
            sp.wait(m1)
            if i % 2:
                mo = dma(sp, s_o, outv[:, i - 1:i + 1, :], X[:, i - 1:i + 1, :], i // 2 + 1)
        sp.wait(mo)

    with ExitStack() as outer:
        block = outer.enter_context(nc.Block())

        @block.tensor
        def _(e):
            walk(e, "s_pe")

        @block.scalar
        def _(e):
            walk(e, "s_act")

        @block.vector
        def _(e):
            walk(e, "s_dve")

        @block.gpsimd
        def _(e):
            walk(e, "s_pool")

        @block.sync
        def _(e):
            walk(e, "s_sp")


def shape_constants():
    p = np.arange(P)[:, None]
    d = P + p - np.arange(S)[None, :]
    count = ((d >= 0) & (d <= 128)).astype(np.float64) + ((d >= 0) & (d % 4 == 0)) + ((d >= 0) & (d % 16 == 0))
    lc = np.where(count > 0, np.log(np.maximum(count, 1)), NEG)
    tabs = np.empty((NH + 1, P, S), np.float32)
    for h in range(NH):
        slope = 2.0 ** (-8.0 * (h + 1) / NH)
        tabs[h] = np.where(count > 0, lc - slope * d, NEG)
    tabs[NH] = np.where(d >= 0, 0.0, NEG)
    j, i = np.arange(P)[:, None], np.arange(P)[None, :]
    ms = np.zeros((P, 7, P), np.float32)
    for n, s in enumerate(LEVELS):
        if s == 0:
            ms[:, n] = j == i
        else:
            ms[:, n] = (j // (2 * s) == i // (2 * s)) & (j % (2 * s) < s) & (i % (2 * s) >= s)
    half = np.arange(16, dtype=np.float32) / np.float32(16)
    inv = (np.float32(1.0) / (np.float32(10000.0) ** half)).astype(np.float32)
    q = np.arange(P)
    return tabs, ms.reshape(P, 7 * P), inv[q % 16], np.where(q % 32 < 16, -1.0, 1.0).astype(np.float32)


def kernel(**inputs):
    import concourse.bacc as bacc
    from concourse.bass_utils import run_bass_kernel_spmd

    a = {k: np.ascontiguousarray(v) for k, v in inputs.items()}
    placed, n_chunks = place_jobs()
    ws = np.zeros((n_chunks, P, CW), np.float32)
    for _, name, cols, kt, at in placed:
        w = a[name][0]
        n = len(cols)
        for k in range(kt):
            b = at + k * (n // P)
            o = b % CB * P
            ws[b // CB, :, o:o + n] = w[k * P:(k + 1) * P][:, cols]
    tabs, ms, inv, sgn = shape_constants()
    V, NV = vec_at()
    vecs = np.zeros((P, NV), np.float32)

    def put(name, rows):
        vecs[:, V[name]:V[name] + rows.shape[0]] = rows.T

    for name in ("norm1_g", "gate_b", "conv_b", "conv_norm_g", "norm2_g", "ffn_conv_b", "ln_mix_2", "mla_norm_cq_2",
                 "mla_norm_ckv_2", "gla_b_gate_2", "gla_norm_2", "ln_ffn_2", "final_norm_2", "conv_w", "ffn_conv_w"):
        put(name, a[name].reshape(-1, P))
    put("qg", np.concatenate([a["q_norm_g"][0]] * 2)[None])
    put("kg", np.concatenate([a["k_norm_g"][0]] * 2)[None])
    put("inv", inv[None])
    put("sgn", sgn[None])
    put("eps", np.full((1, P), EPS, np.float32))
    put("one", np.ones((1, P), np.float32))
    put("sel", np.tile(np.eye(32, dtype=np.float32), (4, 4)))
    xs = np.ascontiguousarray(a["x"][0].T.reshape(KD, P, S).transpose(1, 0, 2).reshape(P, KD * S))
    feed = {
        "ws": ws, "xs": xs, "vecs": vecs,
        "pos": np.ascontiguousarray(np.broadcast_to(a["positions_2"].reshape(1, S), (P, S))),
        "wgate": a["gla_w_gate2_2"][0], "tabs": tabs, "lmask": ms,
    }
    nc = bacc.Bacc("TRN2", target_bir_lowering=False, num_devices=1)
    args = [nc.dram_tensor(n, v.shape, mybir.dt.from_np(v.dtype), kind="ExternalInput").ap() for n, v in feed.items()]
    out = nc.dram_tensor("out", (P, KD * S), F32, kind="ExternalOutput").ap()
    two_blocks(nc, args[0], args[1], args[2], args[3], args[4], args[5], args[6], out)
    r = run_bass_kernel_spmd(nc, [feed], core_ids=[0])
    y = r.results[0]["out"]
    return np.ascontiguousarray(y.reshape(P, KD, S).transpose(2, 1, 0).reshape(1, S, D))
```
